# Optimizing a Trainium2 kernel written in Bass

```python
import math
import jax, jax.numpy as jnp
from jax import lax
import numpy as np

D_MODEL = 1024
BATCH = 1
SEQ = 256
DEPTH = 2

N_MIXERS = 2
N_META = 16
RWKV_HEAD = 64
RWKV_HEADS = D_MODEL // RWKV_HEAD
DECAY_LORA = max(32, int(round(1.8 * D_MODEL ** 0.5 / 32)) * 32)
AAA_LORA = max(32, int(round(1.8 * D_MODEL ** 0.5 / 32)) * 32)
GATE_LORA = max(32, int(round(0.6 * D_MODEL ** 0.8 / 32)) * 32)
GN_EPS = 64e-5
ATT_HEADS = 16
ATT_KV_HEADS = 4
ATT_HEAD_DIM = D_MODEL // ATT_HEADS
ATT_GROUP = ATT_HEADS // ATT_KV_HEADS
WINDOW = 128
ATT_BLOCK = 128
QKV_WIDTH = (ATT_HEADS + 2 * ATT_KV_HEADS) * ATT_HEAD_DIM
N_BUCKETS = 32
MAX_DISTANCE = 128
N_EXPERTS = 64
TOP_K = 8
N_GROUPS = 8
TOPK_GROUPS = 4
EXPERT_FF = 256
SHARED_FF = 256
ROUTED_SCALE = 2.5
MOE_BLOCK = 256
DEEPNORM_ALPHA = (2 * DEPTH) ** 0.25
DEEPNORM_BETA = (8 * DEPTH) ** -0.25
LN_EPS = 1e-5
N_RWKV_LAYERS = (DEPTH + 1) // 2
N_ATT_LAYERS = DEPTH // 2

kernel_name = 'hybrid_rwkv7_swa_sink_moe_deepnorm'

F32 = jnp.float32

def layer_norm(x, g, b):
    xf = x.astype(F32)
    mu = jnp.mean(xf, -1, keepdims=True)
    var = jnp.mean(jnp.square(xf - mu), -1, keepdims=True)
    return ((xf - mu) * lax.rsqrt(var + LN_EPS) * g.astype(F32) + b.astype(F32)).astype(x.dtype)

def _wkv7_step(S, inp):
    r_t, d_t, k_t, v_t, kk_t, a_t = inp
    sa = jnp.einsum('bhij,bhj->bhi', S, -kk_t)
    S = (S * d_t[:, :, None, :] + sa[..., None] * (kk_t * a_t)[:, :, None, :]
         + v_t[..., None] * k_t[:, :, None, :])
    y = jnp.einsum('bhij,bhj->bhi', S, r_t)
    return S, y

def rwkv7_time_mix(x, mu, w0, w1, w2, a0, a1, a2, g1, g2, k_k, k_a, r_k,
                   w_r, w_k, w_v, w_o, lnx_g, lnx_b):
    B, L, D = x.shape
    H, N = RWKV_HEADS, RWKV_HEAD
    xx = jnp.pad(x, ((0, 0), (1, 0), (0, 0)))[:, :L] - x
    r = (x + xx * mu[0]) @ w_r
    logw = -jax.nn.softplus(-(w0 + jnp.tanh((x + xx * mu[1]) @ w1) @ w2)) - 0.5
    k = (x + xx * mu[2]) @ w_k
    v = (x + xx * mu[3]) @ w_v
    a = jax.nn.sigmoid(a0 + ((x + xx * mu[4]) @ a1) @ a2)
    g = jax.nn.sigmoid((x + xx * mu[5]) @ g1) @ g2
    kk = (k * k_k).reshape(B, L, H, N).astype(F32)
    kk = kk / jnp.maximum(jnp.linalg.norm(kk, axis=-1, keepdims=True), 1e-12)
    k = k * (1 + (a - 1) * k_a)
    decay = jnp.exp(-jnp.exp(logw.astype(F32)))
    to_t = lambda t: jnp.swapaxes(t.reshape(B, L, H, N).astype(F32), 0, 1)
    xs = (to_t(r), to_t(decay), to_t(k), to_t(v), jnp.swapaxes(kk, 0, 1), to_t(a))
    _, y = lax.scan(_wkv7_step, jnp.zeros((B, H, N, N), F32), xs)
    y = jnp.swapaxes(y, 0, 1)
    m = jnp.mean(y, -1, keepdims=True)
    var = jnp.mean(jnp.square(y - m), -1, keepdims=True)
    y = ((y - m) * lax.rsqrt(var + GN_EPS)).reshape(B, L, D) * lnx_g.astype(F32) + lnx_b.astype(F32)
    rh, kh, vh = [t.reshape(B, L, H, N).astype(F32) for t in (r, k, v)]
    bonus = (jnp.sum(rh * kh * r_k.astype(F32), -1, keepdims=True) * vh).reshape(B, L, D)
    out = ((y + bonus) * g.astype(F32)).astype(x.dtype)
    return out @ w_o

def t5_bucket(dist):
    exact = N_BUCKETS // 2
    d = jnp.maximum(dist, 0)
    ratio = jnp.log(jnp.maximum(d, 1).astype(F32) / exact) / math.log(MAX_DISTANCE / exact)
    large = jnp.minimum(exact + (ratio * (N_BUCKETS - exact)).astype(jnp.int32), N_BUCKETS - 1)
    return jnp.where(d < exact, d, large)

def rel_bias_for(dist, rel_bias):
    b = rel_bias[t5_bucket(dist)]
    return jnp.moveaxis(b, -1, 0).reshape(ATT_KV_HEADS, ATT_GROUP, *dist.shape).astype(F32)

def sink_softmax_attend(logits, vals, sinks):
    s = sinks.astype(F32)[None, :, :, None, None]
    m = jnp.maximum(jnp.max(logits, -1, keepdims=True), s)
    p = jnp.exp(logits - m)
    probs = p / (jnp.sum(p, -1, keepdims=True) + jnp.exp(s - m))
    return jnp.einsum('bkgqs,bskd->bqkgd', probs.astype(vals.dtype), vals)

def swa_sink_attention(x, w_qkv, b_qkv, sinks, w_o, b_o, rel_bias):
    B, L, _ = x.shape
    S = L - N_META
    nb = S // ATT_BLOCK
    H, KV, G, hd = ATT_HEADS, ATT_KV_HEADS, ATT_GROUP, ATT_HEAD_DIM
    qkv = x @ w_qkv + b_qkv
    q = (qkv[..., :H * hd] * hd ** -0.5).reshape(B, L, KV, G, hd)
    k = qkv[..., H * hd:(H + KV) * hd].reshape(B, L, KV, hd)
    v = qkv[..., (H + KV) * hd:].reshape(B, L, KV, hd)
    sinks = sinks.reshape(KV, G)
    qm, km, vm = q[:, :N_META], k[:, :N_META], v[:, :N_META]
    pm = jnp.arange(N_META)
    d_mm = pm[:, None] - pm[None, :]
    lg = jnp.einsum('bqkgd,bskd->bkgqs', qm, km).astype(F32) + rel_bias_for(d_mm, rel_bias)
    lg = jnp.where(d_mm >= 0, lg, -jnp.inf)
    out_meta = sink_softmax_attend(lg, vm, sinks)
    blocks = lambda t: jnp.moveaxis(t[:, N_META:].reshape(B, nb, ATT_BLOCK, *t.shape[2:]), 1, 0)
    qb, kb, vb = blocks(q), blocks(k), blocks(v)
    band = lambda t: jnp.concatenate([jnp.concatenate([jnp.zeros_like(t[:1]), t[:-1]], 0), t], axis=2)
    kband, vband = band(kb), band(vb)
    qi = jnp.arange(ATT_BLOCK)[:, None]
    sj = jnp.arange(2 * ATT_BLOCK)[None, :]
    d_band = qi + ATT_BLOCK - sj
    in_window = (d_band >= 0) & (d_band < WINDOW)
    bias_band = rel_bias_for(d_band, rel_bias)
    meta_cols = jnp.arange(N_META)[None, :]

    def block_attend(args):
        j, q_j, k_j, v_j = args
        d_meta = N_META + j * ATT_BLOCK + qi - meta_cols
        lg_meta = jnp.einsum('bqkgd,bmkd->bkgqm', q_j, km).astype(F32) + rel_bias_for(d_meta, rel_bias)
        visible = in_window & ((j > 0) | (sj >= ATT_BLOCK))
        lg_band = jnp.einsum('bqkgd,bskd->bkgqs', q_j, k_j).astype(F32) + bias_band
        lg_band = jnp.where(visible, lg_band, -jnp.inf)
        return sink_softmax_attend(jnp.concatenate([lg_meta, lg_band], -1),
                                   jnp.concatenate([vm, v_j], 1), sinks)

    out_real = lax.map(block_attend, (jnp.arange(nb), qb, kband, vband))
    out_real = jnp.moveaxis(out_real, 0, 1).reshape(B, S, H * hd)
    out = jnp.concatenate([out_meta.reshape(B, N_META, H * hd), out_real], 1)
    return out @ w_o + b_o

def swiglu(x, wg, wu, wd):
    return (jax.nn.silu(x @ wg) * (x @ wu)) @ wd

def moe_ffn(x2d, router, bias, w_gate, w_up, w_down, sh_gate, sh_up, sh_down):
    T, D = x2d.shape
    scores = jax.nn.sigmoid(x2d.astype(F32) @ router.astype(F32))
    choice = scores + bias.astype(F32)
    grp = choice.reshape(T, N_GROUPS, N_EXPERTS // N_GROUPS)
    grp_score = jnp.sum(lax.top_k(grp, 2)[0], -1)
    _, top_g = lax.top_k(grp_score, TOPK_GROUPS)
    keep_g = jnp.any(top_g[:, :, None] == jnp.arange(N_GROUPS)[None, None, :], axis=1)
    keep = jnp.repeat(keep_g, N_EXPERTS // N_GROUPS, axis=1)
    _, idx = lax.top_k(jnp.where(keep, choice, -jnp.inf), TOP_K)
    gate = jnp.take_along_axis(scores, idx, axis=1)
    gate = gate / jnp.sum(gate, -1, keepdims=True) * ROUTED_SCALE
    A = T * TOP_K
    e_flat = idx.reshape(A)
    tok_flat = jnp.repeat(jnp.arange(T, dtype=jnp.int32), TOP_K)
    order = jnp.argsort(e_flat)
    e_sorted = e_flat[order]
    counts = jnp.zeros((N_EXPERTS,), jnp.int32).at[e_flat].add(1)
    padded = (counts + MOE_BLOCK - 1) // MOE_BLOCK * MOE_BLOCK
    start = jnp.cumsum(counts) - counts
    pend = jnp.cumsum(padded)
    pstart = pend - padded
    dest = pstart[e_sorted] + jnp.arange(A, dtype=jnp.int32) - start[e_sorted]
    nblk = -(-A // MOE_BLOCK) + N_EXPERTS
    P = nblk * MOE_BLOCK
    slot_tok = jnp.zeros((P,), jnp.int32).at[dest].set(tok_flat[order])
    slot_gate = jnp.zeros((P,), F32).at[dest].set(gate.reshape(A)[order])
    block_e = jnp.minimum(jnp.searchsorted(pend, jnp.arange(nblk) * MOE_BLOCK, side='right'),
                          N_EXPERTS - 1)

    def expert_block(args):
        tok, e, gt = args
        y = swiglu(x2d[tok], w_gate[e], w_up[e], w_down[e])
        return y * gt[:, None].astype(y.dtype)

    y = lax.map(expert_block, (slot_tok.reshape(nblk, MOE_BLOCK), block_e,
                               slot_gate.reshape(nblk, MOE_BLOCK)))
    routed = jax.ops.segment_sum(y.reshape(P, D), slot_tok, num_segments=T)
    return swiglu(x2d, sh_gate, sh_up, sh_down) + routed

def setup_inputs(seed: int = 0) -> dict:
    key = jax.random.key(seed)
    ks = iter(jax.random.split(key, 48))
    D, NA, NB = D_MODEL, N_RWKV_LAYERS, N_ATT_LAYERS
    H, N = RWKV_HEADS, RWKV_HEAD
    att_w = ATT_HEADS * ATT_HEAD_DIM

    def nrm(shape, scale):
        return jax.random.normal(next(ks), shape, F32) * scale

    def unif(shape, lo, hi):
        return jax.random.uniform(next(ks), shape, F32, lo, hi)

    return {
        'x': nrm((BATCH, SEQ, D), 1.0),
        'meta': nrm((N_META, D), 1.0),
        'rel_bias': nrm((N_BUCKETS, ATT_HEADS), 0.5),
        'rwkv_mu': unif((NA, 6, D), 0.0, 1.0),
        'rwkv_w0': unif((NA, D), -6.5, -1.5),
        'rwkv_w1': nrm((NA, D, DECAY_LORA), D ** -0.5),
        'rwkv_w2': nrm((NA, DECAY_LORA, D), 0.5 * DECAY_LORA ** -0.5),
        'rwkv_a0': nrm((NA, D), 0.1),
        'rwkv_a1': nrm((NA, D, AAA_LORA), D ** -0.5),
        'rwkv_a2': nrm((NA, AAA_LORA, D), AAA_LORA ** -0.5),
        'rwkv_g1': nrm((NA, D, GATE_LORA), D ** -0.5),
        'rwkv_g2': nrm((NA, GATE_LORA, D), GATE_LORA ** -0.5),
        'rwkv_k_k': 0.85 + nrm((NA, D), 0.05),
        'rwkv_k_a': 1.0 + nrm((NA, D), 0.05),
        'rwkv_r_k': nrm((NA, H, N), 0.1),
        'rwkv_w_r': nrm((NA, D, D), D ** -0.5),
        'rwkv_w_k': nrm((NA, D, D), D ** -0.5),
        'rwkv_w_v': nrm((NA, D, D), D ** -0.5),
        'rwkv_w_o': nrm((NA, D, D), DEEPNORM_BETA * D ** -0.5),
        'rwkv_lnx_g': 1.0 + nrm((NA, D), 0.02),
        'rwkv_lnx_b': nrm((NA, D), 0.02),
        'attn_w_qkv': nrm((NB, D, QKV_WIDTH), D ** -0.5),
        'attn_b_qkv': nrm((NB, QKV_WIDTH), 0.02),
        'attn_sinks': nrm((NB, ATT_HEADS), 0.5),
        'attn_w_o': nrm((NB, att_w, D), DEEPNORM_BETA * att_w ** -0.5),
        'attn_b_o': nrm((NB, D), 0.02),
        'ln_mix_g': 1.0 + nrm((DEPTH, D), 0.02),
        'ln_mix_b': nrm((DEPTH, D), 0.02),
        'ln_ffn_g': 1.0 + nrm((DEPTH, D), 0.02),
        'ln_ffn_b': nrm((DEPTH, D), 0.02),
        'moe_router': nrm((DEPTH, D, N_EXPERTS), D ** -0.5),
        'moe_bias': nrm((DEPTH, N_EXPERTS), 0.01),
        'moe_w_gate': nrm((DEPTH, N_EXPERTS, D, EXPERT_FF), D ** -0.5),
        'moe_w_up': nrm((DEPTH, N_EXPERTS, D, EXPERT_FF), D ** -0.5),
        'moe_w_down': nrm((DEPTH, N_EXPERTS, EXPERT_FF, D), DEEPNORM_BETA * EXPERT_FF ** -0.5),
        'shared_w_gate': nrm((DEPTH, D, SHARED_FF), D ** -0.5),
        'shared_w_up': nrm((DEPTH, D, SHARED_FF), D ** -0.5),
        'shared_w_down': nrm((DEPTH, SHARED_FF, D), DEEPNORM_BETA * SHARED_FF ** -0.5),
    }

def reference(x, meta, rel_bias,
              rwkv_mu, rwkv_w0, rwkv_w1, rwkv_w2, rwkv_a0, rwkv_a1, rwkv_a2, rwkv_g1, rwkv_g2,
              rwkv_k_k, rwkv_k_a, rwkv_r_k, rwkv_w_r, rwkv_w_k, rwkv_w_v, rwkv_w_o,
              rwkv_lnx_g, rwkv_lnx_b,
              attn_w_qkv, attn_b_qkv, attn_sinks, attn_w_o, attn_b_o,
              ln_mix_g, ln_mix_b, ln_ffn_g, ln_ffn_b,
              moe_router, moe_bias, moe_w_gate, moe_w_up, moe_w_down,
              shared_w_gate, shared_w_up, shared_w_down):
    B = x.shape[0]
    h = jnp.concatenate([jnp.broadcast_to(meta[None].astype(x.dtype), (B, N_META, D_MODEL)), x], axis=1)
    L = h.shape[1]
    for i in range(DEPTH):
        j = i // N_MIXERS
        if i % N_MIXERS == 0:
            mix = rwkv7_time_mix(h, rwkv_mu[j], rwkv_w0[j], rwkv_w1[j], rwkv_w2[j], rwkv_a0[j],
                                 rwkv_a1[j], rwkv_a2[j], rwkv_g1[j], rwkv_g2[j], rwkv_k_k[j],
                                 rwkv_k_a[j], rwkv_r_k[j], rwkv_w_r[j], rwkv_w_k[j], rwkv_w_v[j],
                                 rwkv_w_o[j], rwkv_lnx_g[j], rwkv_lnx_b[j])
        else:
            mix = swa_sink_attention(h, attn_w_qkv[j], attn_b_qkv[j], attn_sinks[j],
                                     attn_w_o[j], attn_b_o[j], rel_bias)
        h = layer_norm(DEEPNORM_ALPHA * h + mix, ln_mix_g[i], ln_mix_b[i])
        f = moe_ffn(h.reshape(B * L, D_MODEL), moe_router[i], moe_bias[i], moe_w_gate[i],
                    moe_w_up[i], moe_w_down[i], shared_w_gate[i], shared_w_up[i],
                    shared_w_down[i]).reshape(B, L, D_MODEL)
        h = layer_norm(DEEPNORM_ALPHA * h + f, ln_ffn_g[i], ln_ffn_b[i])
    return h[:, N_META:]


_drawn_inputs = setup_inputs


def setup_inputs(seed=0):
    import zlib

    import numpy as np

    out = dict(_drawn_inputs(seed))
    spreads = {}
    factors = {'rwkv_w2': 2.895,
     'rwkv_lnx_g': 2.747,
     'attn_sinks': 8.0,
     'attn_b_qkv': 2.813,
     'rwkv_lnx_b': 3.449}
    for name, (base, spread) in spreads.items():
        noise = np.random.default_rng([zlib.crc32(name.encode()), seed]).standard_normal(out[name].shape)
        drawn = base * np.exp(spread * noise) if base else spread * noise
        out[name] = __import__('jax').numpy.asarray(drawn.astype(out[name].dtype))
    for name, factor in factors.items():
        out[name] = (out[name] * factor).astype(out[name].dtype)
    return out
```

```python
from contextlib import ExitStack

import numpy as np

import concourse.bass as bass
from concourse import mybir

ALU = mybir.AluOpType
ACT = mybir.ActivationFunctionType
AX = mybir.AxisListType
F32 = mybir.dt.float32
I32 = mybir.dt.int32

D = 1024
SEQ = 256
META = 16
T = SEQ + META
P = 128
KC = D // P
TILES = [(0, 128), (128, 128), (256, 16)]
NT = len(TILES)
HEADS = 16
HD = 64
PAIRS = HEADS // 2
CHUNK = 32
HALF = 16
NCH = -(-T // CHUNK)
LORA = 64
GLORA = 160
GN_EPS = 64e-5
LN_EPS = 1e-5
EXP_HALF = float(np.exp(-0.5))
ALPHA = float((2 * 2) ** 0.25)
KV = 4
GROUP = HEADS // KV
WINDOW = 128
BUCKETS = 32
QKV = (HEADS + 2 * KV) * HD
E = 64
TOPK = 8
GROUPS = 8
GE = E // GROUPS
TOP_GROUPS = 4
FF = 256
SCALE = 2.5
SLOTS = 128
RING = 6
SLOT = 2048
OUT_OF_RANGE = 65536.0
HIDDEN = -1.0e30
BIASLEN = 2 * T


class Steps:

    def __init__(self, sem, order):
        self.sem, self.first, self.units, n = sem, {}, dict(order), 0
        for name, units in order:
            self.first[name] = n
            n += units
        self.total, self.done = n, 0

    def index(self, name, u=0):
        assert 0 <= u < self.units[name], (name, u)
        return self.first[name] + u

    def at(self, name, u=None):
        return self.sem, self.index(name, self.units[name] - 1 if u is None else u) + 1

    def step(self, name, u=0):
        assert self.index(name, u) == self.done, (name, u, self.index(name, u), self.done)
        self.done += 1
        return self.sem, 1

    def end(self):
        return self.sem, self.total


def t5_one_hot():
    exact = BUCKETS // 2
    d = T - 1 - np.arange(BIASLEN)
    near = np.maximum(d, 1).astype(np.float32)
    ratio = np.log(near / np.float32(exact)) / np.float32(np.log(128 / exact))
    large = np.minimum(exact + (ratio * (BUCKETS - exact)).astype(np.int32), BUCKETS - 1)
    bucket = np.where(d < exact, np.maximum(d, 0), large)
    out = np.zeros((BUCKETS + 1, 2, BIASLEN), np.float32)
    for plane, hidden in enumerate(((d < 0) | (d >= WINDOW), d < 0)):
        out[np.where(hidden, BUCKETS, bucket), plane, np.arange(BIASLEN)] = 1.0
    return out


def hybrid_trunk(nc, I, out):
    with ExitStack() as ctx:
        def sb(name, shape, dt=F32):
            return ctx.enter_context(nc.sbuf_tensor(name, shape, dt))

        def sem(name):
            return ctx.enter_context(nc.semaphore(name))

        ps = ctx.enter_context(nc.psum_tensor("ps", [P, 8, 512], F32))

        ring = sb("ring", [P, RING, SLOT])
        h = sb("h", [P, NT, D])
        lnrow = sb("lnrow", [P, 2, D])
        router = sb("router", [P, 2, KC, E])
        rbias = sb("rbias", [P, 2, E])
        ident = sb("ident", [P, P])
        anti = sb("anti", [P, P])
        allones = sb("allones", [P, P])
        headones = sb("headones", [P, P])
        up16 = sb("up16", [P, P])
        up32 = sb("up32", [P, P])
        up32d = sb("up32d", [P, P])
        low16 = sb("low16", [P, P])
        lowoff = sb("lowoff", [P, P])
        before = sb("before", [P, P])
        notfirst = sb("notfirst", [P, T])
        small = sb("small", [P, 256])
        eps = sb("eps", [P, 2])
        most_tokens = sb("most_tokens", [P, 2], I32)
        arena = sb("arena", [P, 32300])

        def view(at, *shape, rows=P, dt=None):
            n = int(np.prod(shape))
            assert at + n <= 32300, (at, n)
            v = arena[0:rows, at:at + n]
            if dt is not None:
                v = v.bitcast(dt)
            if len(shape) == 2:
                v = v.rearrange("p (a b) -> p a b", a=shape[0])
            if len(shape) == 3:
                v = v.rearrange("p (a b c) -> p a b c", a=shape[0], b=shape[1])
            return v

        hx = [nc.dram_tensor(f"hx{l}", (T, D), F32, kind="Internal").ap() for l in range(2)]
        routed = [nc.dram_tensor(f"routed{l}", (T * TOPK, D), F32, kind="Internal").ap() for l in range(2)]
        biasd = nc.dram_tensor("biasd", (HEADS, 2, BIASLEN), F32, kind="Internal").ap()

        consts = Steps(sem("consts_ready"), [("ones", 3), ("made", 1)])
        x_loaded = sem("x_loaded")
        h_loaded = sem("h_loaded")
        params_loaded = sem("params_loaded")
        attn_loaded = sem("attn_loaded")
        ln_loaded = sem("ln_loaded")
        bias_stored = sem("bias_stored")
        bias_loaded = sem("bias_loaded")
        hx_stored = [sem(f"hx_stored{l}") for l in range(2)]
        routed_loaded = [sem(f"routed_loaded{t}") for t in range(NT)]
        out_stored = sem("out_stored")
        hidden_row = sem("hidden_row")
        rn_step = sem("rn_step")
        route_consts = sem("route_consts")
        slot_loaded = [sem(f"slot_loaded{s}") for s in range(RING)]

        def per_tile(steps):
            return [(f"{n}{t}", u) for t in range(NT) for n, u in steps(t)]

        UNITS = 4

        def chunk_ids(t):
            return range(t * 4, min(t * 4 + 4, NCH))

        def rw_pe_tile(t):
            for g in range(UNITS):
                for n in ("ab", "ba", "ak", "bb", "bk", "x2", "x2t", "tt2", "x4", "x4t", "tt3", "x8", "tt4",
                          "td", "f", "tt5", "g1", "w12", "q1", "q2"):
                    yield f"{n}_{g}_", 1

        def rw_order(t, who):
            o = []
            if who == "pe":
                o += [("tr", 8)]
                o += list(rw_pe_tile(t))
            if who == "dve":
                o += [("bt", 1), ("kt", 1)]
                for g in range(UNITS):
                    o += [(f"{n}_{g}_", 1) for n in ("ab", "tt1", "ba", "off", "ak", "bb", "bk", "tt2", "tt3",
                                                     "tt4", "tt5", "q1")]
            if who == "act":
                o += [("tr", 8)]
                for g in range(UNITS):
                    o += [(f"{n}_{g}_", 1) for n in ("x2", "x2t", "x4", "x4t", "x8", "td", "f", "g1", "w12",
                                                     "q2")]
            for c in chunk_ids(t):
                last = c == NCH - 1
                if who == "pe":
                    o += ([] if last else [(f"m_{c}_", 2)]) + [(f"y_{c}_", 1)] + ([] if last else [(f"s_{c}_", 2)])
                if who == "act" and not last:
                    o += [(f"m_{c}_", 2)]
                if who == "dve":
                    o += ([] if last else [(f"sp_{c}_", 1)]) + [(f"y_{c}_", 1)] + ([] if last else [(f"s_{c}_", 2)])
            return o

        C8 = KC
        rp = Steps(sem("rwkv_pe"), [("par", 1), ("xT", C8), ("bias", 4), ("r", C8), ("k", C8), ("v", C8),
                                    ("wh", 1), ("w", C8), ("ah", 1), ("a", C8), ("gh", 2), ("g", C8),
                                    ("n2", C8), ("bon", C8)]
                   + per_tile(lambda t: rw_order(t, "pe"))
                   + [("mean", C8), ("var", C8), ("o", 12)])
        ra = Steps(sem("rwkv_act"), [("r", C8), ("k", C8), ("v", C8), ("wh", 1), ("w", C8), ("ah", 1),
                                     ("a", C8), ("gh", 2), ("g", C8), ("sq", C8), ("n2", C8), ("pm", C8), ("pi", C8),
                                     ("pp", C8)]
                   + per_tile(lambda t: rw_order(t, "act"))
                   + [("ysq", C8), ("std", C8), ("ln", 1)])
        rv = Steps(sem("rwkv_dve"), [("par", 1), ("omk", 1), ("xT", C8), ("bias", 4), ("xx", 2),
                                     ("mix0", C8), ("mix2", C8), ("mix3", C8), ("mix1", C8), ("mix4", C8),
                                     ("mix5", C8), ("kk0", C8), ("cum", C8), ("cumx", C8), ("rn", C8), ("kk", C8),
                                     ("k2t", C8), ("k2", C8), ("b", C8), ("rk", C8), ("z", C8), ("bonus", C8), ("pc", 2),
                                     ("bh", C8), ("kh", C8), ("rh", C8), ("s0", 1)]
                   + per_tile(lambda t: rw_order(t, "dve"))
                   + [("ym", C8), ("yr", C8), ("yn", C8), ("yg", C8), ("yb", C8), ("yo", C8), ("res", 12),
                      ("ln", 9)])

        moe_pe = [Steps(sem(f"route_pe{l}"), [("hT", KC), ("lg", NT), ("sg", 4), ("pos", 4), ("sd", 6)])
                  for l in range(2)]
        moe_act = [Steps(sem(f"route_act{l}"), [("sc", NT), ("sg", 2)]) for l in range(2)]
        moe_dve = [Steps(sem(f"route_dve{l}"),
                         [("zero", 5), ("hT", KC), ("choice", 1), ("top2", 24), ("gs", 1), ("rank", 15), ("keep", 1),
                          ("hide", 1), ("mask", 2), ("top8", 6), ("sel", 2), ("sm", 2), ("g0", 1), ("gsum", 1),
                          ("grec", 2), ("g1", 1),
                          ("g2", 1), ("kr", 3), ("kr2", 1), ("dest", 3), ("tok", 3), ("pos", 3), ("pos2", 1),
                          ("max", 1), ("maxi", 1), ("sd", 6)]) for l in range(2)]
        end_act = [Steps(sem(f"combine_act{l}"), [("ln", 1)]) for l in range(2)]
        end_dve = [Steps(sem(f"combine_dve{l}"), [("sum", 8 * NT), ("ln", 9)]) for l in range(2)]

        NK = [128, 256, 272]
        ab_pe = [("hT", KC), ("q", 8), ("k", 4), ("v", 2), ("vt", 3)]
        ab_act = [("q", 8), ("k", 4), ("v", 2)]
        ab_dve = [("sink", 1), ("hT", KC), ("vt", 3)]
        for t in range(NT):
            for g in range(KV):
                ab_pe += [(f"sc{t}_{g}", 4), (f"pt{t}_{g}", t + 1), (f"pv{t}_{g}", 1)]
                ab_act += [(f"ex{t}_{g}", 5)]
                ab_dve += [(f"mx{t}_{g}", 4), (f"den{t}_{g}", 2), (f"pt{t}_{g}", t + 1), (f"pv{t}_{g}", 4)]
        ab_pe += [("oT", 8), ("o", 12)]
        ab_act += [("oT", 8), ("ln", 1)]
        ab_dve += [("res", 12), ("bo", 3), ("ln", 9)]
        ap, aa, av = (Steps(sem("attn_pe"), ab_pe), Steps(sem("attn_act"), ab_act), Steps(sem("attn_dve"), ab_dve))

        slot_count = [0] * RING
        slot_free = [None] * RING
        landed = {}
        fills = {}

        def w_split(w, n0, n):
            return w[:, n0:n0 + n].rearrange("(p k) n -> p k n", k=KC)

        def w_nat(w, n0, n):
            return w[:, n0:n0 + n].rearrange("(c p) n -> p c n", p=P)

        def slot3(s, k=KC):
            return ring[:, s, :].rearrange("p (k n) -> p k n", k=k)

        def plan(group, name, slot, pieces, released_by):
            fills.setdefault(group, []).append((slot, pieces, slot_free[slot]))
            slot_count[slot] += 16 * len(pieces)
            landed[name] = (slot_loaded[slot], slot_count[slot], slot)
            slot_free[slot] = released_by

        n = 0
        for what, w in (("r", I["rwkv_w_r"]), ("k", I["rwkv_w_k"]), ("v", I["rwkv_w_v"])):
            for q in range(4):
                plan("rwkv", f"{what}{q}", n % RING, [(slot3(n % RING), w_split(w[0], 256 * q, 256))],
                     rp.at(what, 2 * q + 1))
                n += 1
        s = n % RING
        plan("rwkv", "w", s, [(ring[:, s, 0:512], I["rwkv_w1"][0].rearrange("(p k) n -> p (k n)", k=KC)),
                              (ring[0:LORA, s, 512:1536], I["rwkv_w2"][0])], rp.at("w"))
        s = (n + 1) % RING
        plan("rwkv", "a", s, [(ring[:, s, 0:512], I["rwkv_a1"][0].rearrange("(p k) n -> p (k n)", k=KC)),
                              (ring[0:LORA, s, 512:1536], I["rwkv_a2"][0])], rp.at("a"))
        s = (n + 2) % RING
        plan("rwkv", "g1", s, [(ring[:, s, 0:KC * GLORA], I["rwkv_g1"][0].rearrange("(p k) n -> p (k n)", k=KC))],
             rp.at("gh"))
        s = (n + 3) % RING
        plan("rwkv", "g2", s, [(ring[:, s, 0:1024], I["rwkv_g2"][0, 0:P]),
                               (ring[0:GLORA - P, s, 1024:2048], I["rwkv_g2"][0, P:GLORA])], rp.at("g"))
        n += 4
        for q in range(4):
            plan("rwkv", f"o{q}", n % RING, [(slot3(n % RING), w_nat(I["rwkv_w_o"][0], 256 * q, 256))],
                 rp.at("o", 3 * q + 2))
            n += 1

        def plan_shared(l):
            for j, w in enumerate((I["shared_w_gate"], I["shared_w_up"])):
                plan(f"moe{l}", f"sh{j}_{l}", 3 + j, [(ring[:, 3 + j, :], w[l].rearrange("(p k) n -> p (k n)", k=KC))],
                     moe_pe[l].at("sg"))
            plan(f"moe{l}", f"sh2_{l}", 5,
                 [(ring[:, 5, :], I["shared_w_down"][l].rearrange("(p j) n -> p (j n)", j=2))], moe_pe[l].at("sd"))

        class Loop:

            def __init__(self, tag, own_slots=False):
                mk = lambda n: sem(f"{n}_{tag}")
                self.onehot, self.values, self.index = mk("onehot_made"), mk("values_picked"), mk("index_ready")
                self.gathered = [mk("gathered0"), mk("gathered1")]
                self.xt, self.xt_a, self.xt_v = mk("x_turned"), mk("x_copied_act"), mk("x_copied_dve")
                self.gu, self.silu, self.hid = mk("gate_up"), mk("silu_done"), mk("hidden_ready")
                self.ht, self.ht_a = mk("hidden_turned"), mk("hidden_copied")
                self.down, self.y_a, self.y_v = mk("down_done"), mk("y_scaled_act"), mk("y_scaled_dve")
                self.scattered = [mk("scattered0"), mk("scattered1")]
                self.slot = [mk(f"weights{s}") for s in range(RING)] if own_slots else slot_loaded
                self.slot_base = [0] * RING
                self.base = 0
                self.entry_free = [None] * RING

        main = Loop("main")
        spill = [Loop(f"spill{l}", own_slots=True) for l in range(2)]
        main_slots = []

        def plan_experts(l):
            main_slots.append((list(slot_count), list(slot_free)))
            done = (l + 1) * E
            for s in range(RING):
                slot_count[s] += 16 * (E // 2)
                slot_free[s] = (main.down, 2 * done) if s % 3 == 2 else (main.gu, done)

        plan_shared(0)
        plan_experts(0)
        n = 0
        for q in range(6):
            plan("attn", f"qkv{q}", n % RING, [(slot3(n % RING), w_split(I["attn_w_qkv"][0], 256 * q, 256))],
                 ap.at("q", 2 * q + 1) if q < 4 else ap.at("k") if q == 4 else ap.at("v"))
            n += 1
        for q in range(4):
            plan("attn", f"ao{q}", n % RING, [(slot3(n % RING), w_nat(I["attn_w_o"][0], 256 * q, 256))],
                 ap.at("o", 3 * q + 2))
            n += 1
        plan_shared(1)
        plan_experts(1)

        A = [view(2176 * i, KC, T) for i in range(10)]
        hT, cum = A[0], A[0]
        xx, kkn, zT = A[1], A[1], A[1]
        xm = [A[2], A[3]]
        rT, kT, vT, wT, aT, gT = A[4], A[5], A[6], A[7], A[8], A[9]
        PEX, PIN, PMX = A[2], A[7], A[3]
        bT, bonus, yT = A[8], A[3], A[1]
        btile = view(0, KC, P)
        ktile = view(1024, KC, P)
        tokB, tokK = view(2 * 2176, KC, P), view(2 * 2176 + 1024, KC, P)
        tokV, tokZ = view(7 * 2176, KC, P), view(7 * 2176 + 1024, KC, P)
        W12 = view(21760, HEADS, 2 * HD)
        UX = 21760 + 2048
        X, XT, X2, X2T, OFF, TT, AK, BB, BK = (view(UX + 512 * i, 4, P) for i in range(9))
        GZ = view(UX + 9 * 512, 4, HD)
        S = view(UX + 9 * 512 + 256, KC, P)
        SP = view(UX + 9 * 512 + 1280, KC, P)
        M = view(UX + 9 * 512 + 2304, KC, P)
        assert UX + 9 * 512 + 2304 + 1024 <= 32300
        x0 = view(UX, NT, D)
        facc = view(2 * 2176, NT, D)
        prow = view(UX + 3072, P, rows=56)
        onehot = view(UX + 3200, 2, BIASLEN, rows=BUCKETS + 1)
        relt = view(UX + 3200 + 2 * BIASLEN, HEADS, rows=BUCKETS + 1)
        brow = view(UX + 3200 + 2 * BIASLEN + 16, 2, BIASLEN, rows=HEADS)
        thid = view(UX, T, rows=LORA)
        ahid = view(UX + 272, T, rows=LORA)
        ghid = view(UX + 544, 2, T)
        tmp = [view(UX + 1088 + 272 * i, T) for i in range(2)]
        par = small[:, 0:56]
        omk = small[:, 56:64]
        mu = small[:, 64:112].rearrange("p (m k) -> p m k", m=6)
        pc = small[:, 112:112 + KC * NCH].rearrange("p (c n) -> p c n", c=KC)
        stat = small[:, 184:184 + 36].rearrange("p (t s) -> p t s", t=NT)
        mv = small[:, 220:226].rearrange("p (t s) -> p t s", t=NT)
        std = small[:, 226:229]
        rstd = small[:, 229:232]
        (PW0, PA0, PKK, PKA, PRK, PLG, PLB) = range(7)

        relt_hidden = relt[BUCKETS:BUCKETS + 1, :]
        MIXBUF = {0: 0, 2: 1, 3: 0, 1: 1, 4: 0, 5: 1}

        def tmpN(c):
            return A[2][:, c, :]

        def unit(arr, g, rows):
            return arr[rows].rearrange("p (a i r) m -> p a r i m", a=2, r=2)[:, g // 2, g % 2]

        def tpos(row, cols):
            return (row, cols.start)

        def param(i, c):
            return par[:, 8 * i + c:8 * i + c + 1]

        block = ctx.enter_context(nc.Block())

        def psum_of(steps, name, u=0):
            return ps[:, steps.index(name, u) % 8, :]

        def bank_free(eng, steps, evac, name, u=0):
            i = steps.index(name, u) - 8
            if i < 0:
                return
            for nm, first in steps.first.items():
                if first <= i < first + steps.units[nm]:
                    eng.wait_ge(*evac(nm, i - first))

        def r_evac(nm, u):
            base = nm.split("_")[0].rstrip("0123456789") if nm.startswith("tr") else nm.split("_")[0]
            if base == "ba":
                return rv.at(nm.replace("ba", "off"), u)
            if nm in rv.first and (nm not in ra.first):
                return rv.at(nm, u)
            if nm in ("r", "k", "v", "wh", "w", "ah", "a", "gh", "g", "n2") or base == "tr":
                return ra.at(nm, u)
            if nm == "bon":
                return rv.at("bonus", u)
            if nm == "mean":
                return rv.at("ym", u)
            if nm == "var":
                return ra.at("std", u)
            if nm == "o":
                return rv.at("res", u)
            return ra.at(nm, u)

        def m_evac(l):
            def f(nm, u):
                if nm == "lg":
                    return moe_act[l].at("sc", u)
                if nm == "sg":
                    return moe_dve[l].at("sm", u % 2)
                return moe_dve[l].at(nm, min(u, moe_dve[l].units[nm] - 1)) if nm != "pos" else \
                    (moe_dve[l].at("pos", u) if u < 3 else moe_dve[l].at("max"))
            return f

        def a_evac(nm, u):
            if nm in ("q", "k", "v", "oT"):
                return aa.at(nm, u)
            if nm.startswith("sc"):
                return aa.at("ex" + nm[2:], u)
            if nm == "o":
                return av.at("res", u)
            if nm.startswith("pv"):
                return av.at(nm)
            return av.at(nm, u)

        def phase_start(eng, *ends):
            for e in ends:
                eng.wait_ge(*e)

        def heads_of(g):
            return [4 * g + i for i in range(4)]

        def unit_heads(g):
            return [8 * (g // 2) + 2 * i + g % 2 for i in range(4)]

        def hrows(head):
            return slice(HD * (head % 2), HD * (head % 2) + HD)

        turned_count, indexed_count, scaled_count = (nc.gpsimd.alloc_register(n)
                                                     for n in ("turned_count", "indexed_count", "scaled_count"))

        def num(e, times=1, add=0):
            i, k = e
            v = times * k + add
            return v if isinstance(i, int) else i * (4 * times) + v

        def halfnum(e, times, add):
            i, k = e
            v = times * (k // 2) + add
            return v if isinstance(i, int) else i * (2 * times) + v

        def wait(eng, s, value):
            if not isinstance(value, int) or value > 0:
                eng.wait_ge(s, value)

        def plus(e, k):
            return (e[0], e[1] + k)

        mhT = view(0, KC, T)
        macc = view(2176, NT, D)
        xg = [view(5248 + 1024 * b, D) for b in range(2)]
        xgT = [view(7296 + 1024 * b, KC, P) for b in range(2)]
        hg = view(9344, FF)
        hm = view(9600, FF)
        hmT = view(9856, 2, P)
        ysc = [view(10112 + 1024 * b, D) for b in range(2)]
        sel1h = [view(12160 + 384 * b, NT, P) for b in range(2)]
        iota_s = view(12928, P)
        values = view(13056, NT, E * 3)
        gidx = [view(13632 + b, 1, dt=I32) for b in range(4)]
        sidx = [view(13636 + b, 1, dt=I32) for b in range(4)]
        gate_s = [view(13640 + b, 1) for b in range(4)]
        posm = view(13648, NT, E)
        score = view(13840, NT, E)
        choice = view(14032, NT, E)
        top2 = view(14224, NT, GROUPS * 8)
        gsc = view(14416, NT, GROUPS)
        cmp1 = view(14440, GROUPS, GROUPS)
        cmp2 = view(14504, GROUPS, GROUPS)
        grank = view(14568, NT, GROUPS)
        keep = view(14592, NT, GROUPS)
        masked = view(14616, NT, E)
        top8 = view(14808, NT, 8)
        taken = view(14832, NT, E)
        sel = view(15024, NT, E)
        gsum = view(15216, NT)
        grec = view(15220, NT)
        krank = view(15224, NT, E)
        tokid = view(15416, NT)
        tie = view(15420, GROUPS, GROUPS)
        rowok = view(15484, NT)
        most = view(15488, 1)
        mosti_of = [most_tokens[:, l:l + 1] for l in range(2)]
        shid = view(15492, 2, T)
        shm = view(16036, 2, T)
        gate = view(16580, NT, E)
        rt = [view(17000 + 8192 * 0, TOPK, D), view(5248, TOPK, D)]

        tie2i = view(16772, P + NT, dt=I32)
        dest8 = view(16904, NT)
        rowbad = view(16908, NT)

        ahT = view(0, KC, T)
        qT = view(2176, KC, T)
        kdT = view(4352, KV, T)
        vcT = view(5440, 2, T)
        vtok = view(5984, NT, KV * HD)
        hank = [view(6752, HEADS, NK[0]), view(8800, HEADS, NK[1]), view(12896, HEADS, NK[2])]
        prob = view(17248, 4, T)
        probT = view(18336, NT, 4, P)
        otok = view(19872, NT, D)
        oT = view(22944, KC, T)
        aacc = view(25120, NT, D)
        borow = view(28192, D)
        bqkv = view(29216, 14)
        sinks = view(29232, HEADS)
        bq8 = view(29248, 8)
        negm, dens, dens2, esink, esin = (view(29256 + 4 * i, 4) for i in range(5))

        bV, bX, bG, bH, bY = 0, (1, 2), 3, 4, (5, 6)

        def e_slots(e):
            s0 = 3 * (e[1] % 2)
            return s0, s0 + 1, s0 + 2

        def sp_expert(sp, L, l, e, first):
            g, u, d = e_slots(e)
            ei = num(e)
            for s, w in ((g, I["moe_w_gate"]), (u, I["moe_w_up"]), (d, I["moe_w_down"])):
                if first:
                    if L.entry_free[s]:
                        sp.wait_ge(*L.entry_free[s])
                elif s == g:
                    sp.wait_ge(L.gu, num(plus(e, -2), 1, L.base + 1))
                elif s == d:
                    sp.wait_ge(L.down, num(plus(e, -2), 2, 2 * L.base + 2))
                src = w[l][bass.ds(ei, 1), :, :] if not isinstance(ei, int) else w[l][ei:ei + 1, :, :]
                j = KC if s != d else 2
                sp.dma_start(ring[:, s, :], src.rearrange("a (p k) n -> p (a k n)", k=j)).then_inc(L.slot[s], 16)

        def pe_expert(pe, L, e, nxt2, nxt1, this, prev):
            g, u, d = e_slots(e)
            if nxt2:
                pe_pick(pe, L, plus(e, 2))
            if nxt1:
                pe_turn(pe, L, plus(e, 1))
            if this:
                b = e[1] % 2
                pe.wait_ge(L.xt_a, num(e, 1, L.base + 1))
                pe.wait_ge(L.xt_v, num(e, 1, L.base + 1))
                pe.wait_ge(L.slot[g], halfnum(e, 16, L.slot_base[g] + 16))
                pe.wait_ge(L.slot[u], halfnum(e, 16, L.slot_base[u] + 16))
                wait(pe, L.hid, num(e, 1, L.base))
                for k in range(KC):
                    mm = nc.tensor.matmul(ps[:, bG, :].rearrange("p (a n) -> p a n", a=2), xgT[b][:, k, :],
                                          ring[:, g:g + 2, FF * k:FF * k + FF],
                                          start=(k == 0), stop=(k == KC - 1))
                mm.then_inc(L.gu, 1)
            if prev:
                q = plus(e, -1)
                _, _, pd = e_slots((e[0], e[1] + 1))
                pe.wait_ge(L.ht_a, num(q, 1, L.base + 1))
                pe.wait_ge(L.slot[pd], halfnum(q, 16, L.slot_base[pd] + 16))
                wait(pe, L.y_a, num(q, 1, L.base))
                wait(pe, L.y_v, num(q, 1, L.base))
                for n in range(2):
                    for j in range(2):
                        mm = nc.tensor.matmul(ps[:, bY[n], :], hmT[:, j, :],
                                              ring[:, pd, D * j + 512 * n:D * j + 512 * n + 512],
                                              start=(j == 0), stop=(j == 1))
                    mm.then_inc(L.down, 1)
            if this:
                pe.wait_ge(L.hid, num(e, 1, L.base + 1))
                hv = hm.rearrange("p (m j) -> p j m", j=2)
                for j in range(2):
                    mm = nc.tensor.transpose(ps[:, bH, P * j:P * j + P], hv[:, j, :], ident[:, :])
                mm.then_inc(L.ht, 1)

        def pe_pick(pe, L, e):
            b = e[1] % 2
            pe.wait_ge(L.onehot, num(e, 1, L.base + 1))
            wait(pe, L.index, num(e, 1, L.base))
            ei = num(e, 3)
            for t in range(NT):
                mm = nc.tensor.matmul(ps[:, bV, 0:3], sel1h[b][:, t, :],
                                      values[:, t, bass.ds(ei, 3)] if not isinstance(ei, int)
                                      else values[:, t, ei:ei + 3], start=(t == 0), stop=(t == NT - 1))
            mm.then_inc(L.values, 1)

        def pe_turn(pe, L, e):
            b = e[1] % 2
            pe.wait_ge(L.gathered[b], halfnum(e, 16, 8 * L.base + 16))
            wait(pe, L.xt_a, num(e, 1, L.base))
            wait(pe, L.xt_v, num(e, 1, L.base))
            xv = xg[b].rearrange("p (m k) -> p k m", k=KC)
            for k in range(KC):
                mm = nc.tensor.transpose(ps[:, bX[k // 4], P * (k % 4):P * (k % 4) + P], xv[:, k, :], ident[:, :])
                if k % 4 == 3:
                    mm.then_inc(L.xt, 1)

        def act_copy_x(act, L, e):
            b = e[1] % 2
            act.wait_ge(L.xt, num(e, 2, 2 * L.base + 1))
            wait(act, L.gu, num(e, 1, L.base - 1))
            nc.scalar.copy(xgT[b][:, 0:4, :], ps[:, bX[0], :].rearrange("p (k m) -> p k m", k=4)).then_inc(L.xt_a, 1)

        def act_expert(act, L, e, nxt1, this, prev):
            if nxt1:
                act_copy_x(act, L, plus(e, 1))
            if this:
                act.wait_ge(L.gu, num(e, 1, L.base + 1))
                wait(act, L.hid, num(e, 1, L.base))
                nc.scalar.activation(hg, ps[:, bG, 0:FF], ACT.Silu).then_inc(L.silu, 1)
            if prev:
                q = plus(e, -1)
                act.wait_ge(L.down, num(q, 2, 2 * L.base + 1))
                act.wait_ge(L.index, num(q, 1, L.base + 1))
                wait(act, L.scattered[q[1] % 2], halfnum(q, 16, 8 * L.base))
                nc.scalar.activation(ysc[q[1] % 2][:, 0:512], ps[:, bY[0], :], ACT.Copy,
                                     scale=gate_s[q[1] % 4]).then_inc(L.y_a, 1)
            if this:
                act.wait_ge(L.ht, num(e, 1, L.base + 1))
                wait(act, L.down, num(e, 2, 2 * L.base))
                nc.scalar.copy(hmT, ps[:, bH, 0:2 * P].rearrange("p (j m) -> p j m", j=2)).then_inc(L.ht_a, 1)

        def dve_onehot(dve, L, e, first_slot):
            b = e[1] % 2
            wait(dve, L.values, num(e, 1, L.base - 1))
            ei = num(e)
            pos = posm[:, :, bass.ds(ei, 1)] if not isinstance(ei, int) else posm[:, :, ei:ei + 1]
            nc.vector.scalar_tensor_tensor(out=sel1h[b], in0=iota_s.unsqueeze(1).to_broadcast([P, NT, P]),
                                           scalar=float(first_slot), in1=pos.to_broadcast([P, NT, P]),
                                           op0=ALU.add, op1=ALU.is_equal).then_inc(L.onehot, 1)

        def dve_index(dve, L, e):
            k = e[1] % 4
            dve.wait_ge(L.values, num(e, 1, L.base + 1))
            q = plus(e, -4)
            wait(dve, L.scattered[e[1] % 2], halfnum(e, 16, 8 * L.base - 16))
            nc.vector.tensor_scalar(gidx[k], ps[:, bV, 0:1], OUT_OF_RANGE, None, ALU.add)
            nc.vector.tensor_scalar(sidx[k], ps[:, bV, 1:2], OUT_OF_RANGE, None, ALU.add)
            nc.vector.tensor_copy(gate_s[k], ps[:, bV, 2:3]).then_inc(L.index, 1)

        def dve_copy_x(dve, L, e):
            b = e[1] % 2
            dve.wait_ge(L.xt, num(e, 2, 2 * L.base + 2))
            wait(dve, L.gu, num(e, 1, L.base - 1))
            nc.vector.tensor_copy(xgT[b][:, 4:8, :], ps[:, bX[1], :].rearrange("p (k m) -> p k m", k=4))\
                .then_inc(L.xt_v, 1)

        def dve_expert(dve, L, e, first_slot, nxt2, nxt1, this, prev):
            if nxt2:
                dve_onehot(dve, L, plus(e, 2), first_slot)
                dve_index(dve, L, plus(e, 2))
            if nxt1:
                dve_copy_x(dve, L, plus(e, 1))
            if this:
                dve.wait_ge(L.silu, num(e, 1, L.base + 1))
                wait(dve, L.ht, num(e, 1, L.base))
                nc.vector.tensor_tensor(hm, ps[:, bG, FF:2 * FF], hg, ALU.mult).then_inc(L.hid, 1)
            if prev:
                q = plus(e, -1)
                dve.wait_ge(L.down, num(q, 2, 2 * L.base + 2))
                dve.wait_ge(L.index, num(q, 1, L.base + 1))
                wait(dve, L.scattered[q[1] % 2], halfnum(q, 16, 8 * L.base))
                nc.vector.tensor_scalar(ysc[q[1] % 2][:, 512:1024], ps[:, bY[1], :], gate_s[q[1] % 4], None,
                                        ALU.mult).then_inc(L.y_v, 1)

        def pool_gather(pool, L, l, e):
            b = e[1] % 2
            turned, indexed = num(e, 2, 2 * L.base - 2), num(e, 1, L.base + 1)
            if not isinstance(turned, int):
                pool.reg_add(turned_count, turned_count, 2)
                pool.reg_add(indexed_count, indexed_count, 1)
                turned, indexed = turned_count, indexed_count
            pool.wait_ge(*moe_dve[l].at("zero"))
            wait(pool, L.xt, turned)
            pool.wait_ge(L.index, indexed)
            nc.gpsimd.indirect_dma_start(out=xg[b], out_offset=None, in_=hx[l],
                                         in_offset=bass.IndirectOffsetOnAxis(ap=gidx[e[1] % 4], axis=0),
                                         bounds_check=T - 1, oob_is_err=False).then_inc(L.gathered[b], 16)

        def pool_scatter(pool, L, l, e):
            b = e[1] % 2
            scaled = num(e, 1, L.base + 1)
            if not isinstance(scaled, int):
                pool.reg_add(scaled_count, scaled_count, 1)
                scaled = scaled_count
            pool.wait_ge(*moe_dve[l].at("zero"))
            pool.wait_ge(L.y_a, scaled)
            pool.wait_ge(L.y_v, scaled)
            nc.gpsimd.indirect_dma_start(out=routed[l],
                                         out_offset=bass.IndirectOffsetOnAxis(ap=sidx[e[1] % 4], axis=0),
                                         in_=ysc[b], in_offset=None, bounds_check=T * TOPK - 1,
                                         oob_is_err=False).then_inc(L.scattered[b], 16)

        def over_experts(eng, body):
            for k in range(4):
                body((0, k))
            with eng.Fori(0, (E - 8) // 4) as i:
                for j in range(4):
                    body((i, 4 + j))
            for k in range(E - 4, E):
                body((0, k))

        def ahead(e):
            loop = not isinstance(e[0], int)
            return loop or e[1] + 2 < E, loop or e[1] + 1 < E, loop or e[1] >= 1

        def sp_experts(sp, L, l):
            over_experts(sp, lambda e: sp_expert(sp, L, l, e, isinstance(e[0], int) and e[1] < 2))

        def pe_experts(pe, L):
            pe_pick(pe, L, (0, 0))
            pe_pick(pe, L, (0, 1))
            pe_turn(pe, L, (0, 0))
            over_experts(pe, lambda e: pe_expert(pe, L, e, ahead(e)[0], ahead(e)[1], True, ahead(e)[2]))
            pe_expert(pe, L, (0, E), False, False, False, True)

        def act_experts(act, L):
            act_copy_x(act, L, (0, 0))
            over_experts(act, lambda e: act_expert(act, L, e, ahead(e)[1], True, ahead(e)[2]))
            act_expert(act, L, (0, E), False, False, True)

        def dve_experts(dve, L, first_slot):
            for e in ((0, 0), (0, 1)):
                dve_onehot(dve, L, e, first_slot)
                dve_index(dve, L, e)
            dve_copy_x(dve, L, (0, 0))
            over_experts(dve, lambda e: dve_expert(dve, L, e, first_slot, ahead(e)[0], ahead(e)[1], True, ahead(e)[2]))
            dve_expert(dve, L, (0, E), first_slot, False, False, False, True)

        def pool_experts(pool, L, l):
            pool.reg_mov(turned_count, num((0, 5), 2, 2 * L.base - 2))
            pool.reg_mov(indexed_count, num((0, 5), 1, L.base + 1))
            pool.reg_mov(scaled_count, num((0, 2), 1, L.base + 1))
            pool_gather(pool, L, l, (0, 0))
            pool_gather(pool, L, l, (0, 1))

            def body(e):
                if ahead(e)[0]:
                    pool_gather(pool, L, l, plus(e, 2))
                if ahead(e)[2]:
                    pool_scatter(pool, L, l, plus(e, -1))
            over_experts(pool, body)
            pool_scatter(pool, L, l, (0, E - 1))

        SPILLS = [SLOTS * p for p in range(1, -(-T // SLOTS))]

        def all_scattered(eng, L, experts):
            for b in range(2):
                eng.wait_ge(L.scattered[b], 8 * experts)

        def run_spill(eng, l, run):
            L = spill[l]
            eng.wait_ge(*moe_dve[l].at("maxi"))
            count = eng.value_load(mosti_of[l][0:1, 0:1], min_val=0, max_val=T)
            with eng.If(count > SLOTS):
                for p, first_slot in enumerate(SPILLS):
                    L.base = p * E
                    L.slot_base = [16 * (E // 2) * p] * RING
                    L.entry_free = [(main.down, 2 * E * (l + 1))] * RING if p == 0 else \
                        [(L.down, 2 * E * p)] * RING
                    run(L, first_slot)
                all_scattered(eng, L, len(SPILLS) * E)

        def set_main(l):
            main.base = l * E
            main.slot_base, main.entry_free = main_slots[l]

        @block.sync
        def _(sp):
            def static(group):
                for slot, pieces, free in fills[group]:
                    if free:
                        sp.wait_ge(*free)
                    for dst, src in pieces:
                        sp.dma_start(dst, src).then_inc(slot_loaded[slot], 16)

            sp.dma_start(x0[0:META, 0, :], I["meta"]).then_inc(x_loaded, 16)
            sp.dma_start(x0[META:P, 0, :], I["x"][0, 0:P - META, :]).then_inc(x_loaded, 16)
            sp.dma_start(x0[:, 1, :], I["x"][0, P - META:2 * P - META, :]).then_inc(x_loaded, 16)
            sp.dma_start(x0[0:16, 2, :], I["x"][0, 2 * P - META:SEQ, :]).then_inc(x_loaded, 16)
            static("rwkv")
            for l in range(2):
                static(f"moe{l}")
                set_main(l)
                sp_experts(sp, main, l)
                run_spill(sp, l, lambda L, first: sp_experts(sp, L, l))
                if l == 0:
                    static("attn")

        @block.gpsimd
        def _(pool):
            nc.gpsimd.memset(ident[:, :], 0.0).then_inc(*consts.step("ones", 0))
            for m in (up16, up32, up32d, low16, lowoff, before, allones, headones):
                last = nc.gpsimd.memset(m[:, :], 1.0)
            last.then_inc(*consts.step("ones", 1))
            nc.gpsimd.memset(anti[:, :], 0.0)
            nc.gpsimd.memset(notfirst[:, :], 1.0)
            nc.gpsimd.memset(eps[:, 0:1], LN_EPS)
            nc.gpsimd.memset(eps[:, 1:2], GN_EPS).then_inc(*consts.step("ones", 2))
            pool.wait_ge(*consts.at("ones"))
            made = sem("mask_step")
            count = [0]

            def select(m, blk, op, base, cm, pattern, fill=0.0):
                v = m if blk is None else m.rearrange("p (b n) -> p b n", n=blk)
                nc.gpsimd.affine_select(out=v, in_=v, compare_op=op, fill=fill, base=base, pattern=pattern,
                                        channel_multiplier=cm).then_inc(made, 1)
                count[0] += 1
                pool.wait_ge(made, count[0])

            def same_block(m, blk):
                nb = P // blk
                select(m[:, :], blk, ALU.is_ge, 0, 1, [[-blk, nb], [0, blk]])
                select(m[:, :], blk, ALU.is_ge, blk - 1, -1, [[blk, nb], [0, blk]])

            select(ident[:, :], None, ALU.not_equal, 0, 1, [[-1, P]], 1.0)
            select(anti[:, :], None, ALU.not_equal, -(P - 1), 1, [[1, P]], 1.0)
            same_block(headones, HD)
            for m, op, blk in ((up16, ALU.is_gt, HALF), (up32, ALU.is_gt, CHUNK), (up32d, ALU.is_ge, CHUNK)):
                select(m[:, :], None, op, 0, -1, [[1, P]])
                same_block(m, blk)
            select(before[:, :], None, ALU.is_gt, 0, -1, [[1, P]])
            select(low16[:, :], None, ALU.is_gt, 0, 1, [[-1, P]])
            same_block(low16, HALF)
            same_block(lowoff, CHUNK)
            select(lowoff[:, :], HALF, ALU.is_ge, -HALF, 1, [[-HALF, P // HALF], [0, HALF]])
            select(notfirst[:, 0:256], CHUNK, ALU.is_gt, 0, 0, [[0, 256 // CHUNK], [1, CHUNK]])
            select(notfirst[:, 256:T], None, ALU.is_gt, 0, 0, [[1, T - 256]])
            pool.nop().then_inc(*consts.step("made"))

            def row(src):
                return src.rearrange("(a n) -> a n", a=1).to_broadcast([P, src.shape[0]])

            vecs = (I["rwkv_w0"][0], I["rwkv_a0"][0], I["rwkv_k_k"][0], I["rwkv_k_a"][0],
                    I["rwkv_r_k"][0].rearrange("h n -> (h n)"), I["rwkv_lnx_g"][0], I["rwkv_lnx_b"][0])
            for i, v in enumerate(vecs):
                pool.dma_start(prow[8 * i:8 * i + 8, :], v.rearrange("(c p) -> c p", p=P)).then_inc(params_loaded, 16)
            pool.dma_start(mu, I["rwkv_mu"][0].rearrange("m (p k) -> p m k", k=KC)).then_inc(params_loaded, 16)
            pool.dma_start(onehot, I["t5"]).then_inc(params_loaded, 16)
            pool.dma_start(relt[0:BUCKETS, :], I["rel_bias"]).then_inc(params_loaded, 16)
            for l in range(2):
                pool.dma_start(router[:, l], I["moe_router"][l].rearrange("(p k) n -> p k n", k=KC))\
                    .then_inc(params_loaded, 16)
                pool.dma_start(rbias[:, l, :], row(I["moe_bias"][l])).then_inc(params_loaded, 16)

            def load_ln(g, b):
                pool.dma_start(lnrow[:, 0, :], row(g)).then_inc(ln_loaded, 16)
                pool.dma_start(lnrow[:, 1, :], row(b)).then_inc(ln_loaded, 16)

            load_ln(I["ln_mix_g"][0], I["ln_mix_b"][0])
            pool.wait_ge(*rv.at("bias"))
            pool.dma_start(biasd, brow).then_inc(bias_stored, 16)
            pool.dma_start(h[0:META, 0, :], I["meta"]).then_inc(h_loaded, 16)
            pool.dma_start(h[META:P, 0, :], I["x"][0, 0:P - META, :]).then_inc(h_loaded, 16)
            pool.dma_start(h[:, 1, :], I["x"][0, P - META:2 * P - META, :]).then_inc(h_loaded, 16)
            pool.dma_start(h[0:16, 2, :], I["x"][0, 2 * P - META:SEQ, :]).then_inc(h_loaded, 16)

            for l in range(2):
                before_dve = rv if l == 0 else av
                pool.wait_ge(*before_dve.end())
                load_ln(I["ln_ffn_g"][l], I["ln_ffn_b"][l])
                for t, (r0, n) in enumerate(TILES):
                    pool.dma_start(hx[l][r0:r0 + n, :], h[0:n, t, :]).then_inc(hx_stored[l], 16)
                nc.gpsimd.iota(tie2i[:, 0:P], [[1, P]], base=0, channel_multiplier=0).then_inc(made, 1)
                nc.gpsimd.iota(tie2i[:, P:P + NT], [[P, NT]], base=0, channel_multiplier=1).then_inc(made, 1)
                count[0] += 2
                pool.wait_ge(made, count[0])
                nc.gpsimd.tensor_copy(iota_s, tie2i[:, 0:P]).then_inc(made, 1)
                nc.gpsimd.tensor_copy(tokid, tie2i[:, P:P + NT]).then_inc(made, 1)
                nc.gpsimd.memset(rowok, 1.0).then_inc(made, 1)
                nc.gpsimd.memset(tie, 1.0).then_inc(made, 1)
                count[0] += 4
                pool.wait_ge(made, count[0])
                select(rowok[:, 2:3], None, ALU.is_gt, 16, -1, [[0, 1]])
                nc.gpsimd.affine_select(out=tie, in_=tie, compare_op=ALU.is_gt, fill=0.0, base=0,
                                        pattern=[[1, GROUPS], [-1, GROUPS]], channel_multiplier=0)\
                    .then_inc(route_consts, 1)
                pool.wait_ge(hx_stored[l], 16 * NT)
                pool.wait_ge(*moe_dve[l].at("zero"))
                set_main(l)
                pool_experts(pool, main, l)
                run_spill(pool, l, lambda L, first: pool_experts(pool, L, l))
                all_scattered(pool, main, (l + 1) * E)
                pool.wait_ge(main.down, 2 * E * (l + 1))
                pool.wait_ge(main.y_v, E * (l + 1))
                rv3 = routed[l].rearrange("(t k) d -> t k d", k=TOPK)
                for t, (r0, n) in enumerate(TILES):
                    if t == 2:
                        pool.wait_ge(*end_dve[l].at("sum", 7))
                    pool.dma_start(rt[t % 2][0:n], rv3[r0:r0 + n]).then_inc(routed_loaded[t], 16)
                if l == 0:
                    pool.wait_ge(*end_dve[0].end())
                    load_ln(I["ln_mix_g"][1], I["ln_mix_b"][1])
                    pool.dma_start(bqkv[:, 0:8], I["attn_b_qkv"][0, 0:HEADS * HD].rearrange("(c p) -> p c", p=P),
                                   allow_slow_non_contiguous=True).then_inc(attn_loaded, 16)
                    bk = I["attn_b_qkv"][0, HEADS * HD:(HEADS + KV) * HD].rearrange("(g p) -> p g", p=HD)
                    for r in range(2):
                        pool.dma_start(bqkv[HD * r:HD * r + HD, 8:12], bk,
                                       allow_slow_non_contiguous=True).then_inc(attn_loaded, 16)
                    pool.dma_start(bqkv[:, 12:14], I["attn_b_qkv"][0, (HEADS + KV) * HD:QKV]
                                   .rearrange("(c p) -> p c", p=P), allow_slow_non_contiguous=True)\
                        .then_inc(attn_loaded, 16)
                    pool.dma_start(sinks, row(I["attn_sinks"][0])).then_inc(attn_loaded, 16)
                    pool.dma_start(borow, row(I["attn_b_o"][0])).then_inc(attn_loaded, 16)
            pool.wait_ge(*end_dve[1].end())
            o = out[0]
            pool.dma_start(o[0:P - META, :], h[META:P, 0, :]).then_inc(out_stored, 16)
            pool.dma_start(o[P - META:2 * P - META, :], h[:, 1, :]).then_inc(out_stored, 16)
            pool.dma_start(o[2 * P - META:SEQ, :], h[0:16, 2, :]).then_inc(out_stored, 16)
            pool.wait_ge(out_stored, 48)

        @block.tensor
        def _(pe):
            mm_ = nc.tensor.matmul

            def need(name):
                s, v, slot = landed[name]
                pe.wait_ge(s, v)
                return slot

            def start(steps, evac, name, u=0):
                bank_free(pe, steps, evac, name, u)
                return psum_of(steps, name, u)

            def R(name, u=0):
                return start(rp, r_evac, name, u)

            pe.wait_ge(*consts.at("made"))
            pe.wait_ge(params_loaded, 16 * 14)
            b = R("par")
            nc.tensor.transpose(b[:, 0:56], prow[0:56, :], ident[0:56, 0:56]).then_inc(*rp.step("par"))
            pe.wait_ge(x_loaded, 64)
            for k in range(KC):
                b = R("xT", k)
                for t, (r0, n) in enumerate(TILES):
                    xv = x0[0:n, t, :].rearrange("p (m k) -> p k m", k=KC)
                    m = nc.tensor.transpose(b[:, r0:r0 + n], xv[:, k, :], ident[0:n, 0:n])
                m.then_inc(*rp.step("xT", k))
            pe.wait_ge(hidden_row, 1)
            for j in range(4):
                b = R("bias", j)
                mm_(b[0:HEADS, 0:T], relt[:, :], onehot[:, j // 2, T * (j % 2):T * (j % 2) + T], start=True,
                    stop=True).then_inc(*rp.step("bias", j))

            def proj(name, mix):
                pe.wait_ge(*rv.at(f"mix{mix}"))
                for c in range(C8):
                    s = need(f"{name}{c // 2}")
                    b = R(name, c)
                    for k in range(KC):
                        m = mm_(b[:, 0:T], slot3(s)[:, k, P * (c % 2):P * (c % 2) + P], xm[MIXBUF[mix]][:, k, :],
                                start=(k == 0), stop=(k == KC - 1))
                    m.then_inc(*rp.step(name, c))

            proj("r", 0)
            proj("k", 2)
            proj("v", 3)
            for nm, mix, wn, dst in (("w", 1, LORA, thid), ("a", 4, LORA, ahid)):
                pe.wait_ge(*rv.at(f"mix{mix}"))
                s = need(nm)
                b = R(nm + "h")
                for k in range(KC):
                    m = mm_(b[0:LORA, 0:T], ring[:, s, LORA * k:LORA * k + LORA], xm[MIXBUF[mix]][:, k, :],
                            start=(k == 0), stop=(k == KC - 1))
                m.then_inc(*rp.step(nm + "h"))
                pe.wait_ge(*ra.at(nm + "h"))
                for c in range(C8):
                    b = R(nm, c)
                    mm_(b[:, 0:T], ring[0:LORA, s, 512 + P * c:512 + P * c + P], dst, start=True,
                        stop=True).then_inc(*rp.step(nm, c))
            pe.wait_ge(*rv.at("mix5"))
            s = need("g1")
            for j, (m0, mn) in enumerate(((0, P), (P, GLORA - P))):
                b = R("gh", j)
                for k in range(KC):
                    m = mm_(b[0:mn, 0:T], ring[:, s, GLORA * k + m0:GLORA * k + m0 + mn], xm[MIXBUF[5]][:, k, :],
                            start=(k == 0), stop=(k == KC - 1))
                m.then_inc(*rp.step("gh", j))
            pe.wait_ge(*ra.at("gh"))
            s = need("g2")
            for c in range(C8):
                b = R("g", c)
                mm_(b[:, 0:T], ring[:, s, P * c:P * c + P], ghid[:, 0, :], start=True, stop=False)
                mm_(b[:, 0:T], ring[0:GLORA - P, s, D + P * c:D + P * c + P], ghid[0:GLORA - P, 1, :],
                    start=False, stop=True).then_inc(*rp.step("g", c))
            for c in range(C8):
                pe.wait_ge(*ra.at("sq", c))
                b = R("n2", c)
                mm_(b[:, 0:T], headones[:, :], tmpN(c), start=True, stop=True).then_inc(*rp.step("n2", c))
            for c in range(C8):
                pe.wait_ge(*rv.at("rk", c))
                b = R("bon", c)
                mm_(b[:, 0:T], headones[:, :], A[0][:, c, :], start=True, stop=True).then_inc(*rp.step("bon", c))

            for t, (r0, n) in enumerate(TILES):
                cols = slice(r0, r0 + n)
                for j, (src, w) in enumerate(((btile, "bt"), (ktile, "kt"), (vT, None), (zT, None))):
                    if w:
                        pe.wait_ge(*rv.at(f"{w}{t}"))
                    for half in range(2):
                        u = 2 * j + half
                        b = R(f"tr{t}", u)
                        for i in range(4):
                            c = 4 * half + i
                            a_in = src[:, c, 0:n] if w else src[:, c, cols]
                            m = nc.tensor.transpose(b[0:n, P * i:P * i + P], a_in, ident[:, :])
                        m.then_inc(*rp.step(f"tr{t}", u))
                for g in range(UNITS):
                    N = lambda x: f"{x}_{g}_{t}"

                    def four(name, f, after=()):
                        for w in after:
                            pe.wait_ge(*w)
                        b = R(N(name))
                        for i, hd in enumerate(unit_heads(g)):
                            m = f(i, hd, b[0:n, P * i:P * i + n])
                        m.then_inc(*rp.step(N(name)))

                    def ch(arr, hd):
                        return arr[hrows(hd), hd // 2, cols]

                    four("ab", lambda i, hd, o: mm_(o, ch(bT, hd), ch(zT, hd), start=True, stop=True),
                         [rv.at("s0")])
                    four("ba", lambda i, hd, o: mm_(o, ch(zT, hd), ch(bT, hd), start=True, stop=True))
                    four("ak", lambda i, hd, o: mm_(o, ch(kT, hd), ch(zT, hd), start=True, stop=True))
                    four("bb", lambda i, hd, o: mm_(o, ch(bT, hd), ch(rT, hd), start=True, stop=True))
                    four("bk", lambda i, hd, o: mm_(o, ch(kT, hd), ch(rT, hd), start=True, stop=True))

                    def sq(lhs, rhs):
                        return lambda i, hd, o: mm_(o, lhs[0:n, i, 0:n], rhs[0:n, i, 0:n], start=True, stop=True)

                    four("x2", sq(XT, X), [rv.at(N("ba"))])
                    four("x2t", sq(X, XT))
                    four("tt2", sq(X2, TT), [ra.at(N("x2")), rv.at(N("tt1"))])
                    four("x4", sq(X2T, X2), [ra.at(N("x2t"))])
                    four("x4t", sq(X2, X2T))
                    four("tt3", sq(X, TT), [ra.at(N("x4")), rv.at(N("tt2"))])
                    four("x8", sq(XT, X), [ra.at(N("x4t"))])
                    four("tt4", sq(X2, TT), [ra.at(N("x8")), rv.at(N("tt3"))])
                    four("td", lambda i, hd, o: nc.tensor.transpose(o, TT[0:n, i, 0:n], ident[0:n, 0:n]),
                         [rv.at(N("tt4"))])
                    four("f", sq(OFF, TT), [rv.at(N("off"))])
                    four("tt5", sq(X, X2T), [ra.at(N("td")), ra.at(N("f"))])
                    pe.wait_ge(*rv.at(N("ak")))
                    pe.wait_ge(*ra.at(f"tr{t}"))
                    b = R(N("g1"))
                    for i, hd in enumerate(unit_heads(g)):
                        m = mm_(b[0:n, HD * i:HD * i + HD], AK[0:n, i, 0:n], tokV[0:n, hd // 2, hrows(hd)],
                                start=True, stop=True)
                    m.then_inc(*rp.step(N("g1")))
                    pe.wait_ge(*ra.at(N("g1")))
                    pe.wait_ge(*rv.at(N("tt5")))
                    b = R(N("w12"))
                    for i, hd in enumerate(unit_heads(g)):
                        mm_(b[0:n, P * i:P * i + HD], TT[0:n, i, 0:n], tokZ[0:n, hd // 2, hrows(hd)],
                            start=True, stop=True)
                        m = mm_(b[0:n, P * i + HD:P * i + P], TT[0:n, i, 0:n], GZ[0:n, i, :], start=True, stop=True)
                    m.then_inc(*rp.step(N("w12")))
                    pe.wait_ge(*ra.at(N("w12")))
                    pe.wait_ge(*rv.at(N("bk")))
                    b = R(N("q1"))
                    for i, hd in enumerate(unit_heads(g)):
                        m = mm_(b[hrows(hd), P * i:P * i + n], W12[0:n, hd, 0:HD], BB[0:n, i, 0:n],
                                start=True, stop=True)
                    m.then_inc(*rp.step(N("q1")))
                    b = R(N("q2"))
                    for i, hd in enumerate(unit_heads(g)):
                        o = b[hrows(hd), P * i:P * i + n]
                        mm_(o, W12[0:n, hd, HD:P], BB[0:n, i, 0:n], start=True, stop=False)
                        m = mm_(o, tokV[0:n, hd // 2, hrows(hd)], BK[0:n, i, 0:n], start=False, stop=True)
                    m.then_inc(*rp.step(N("q2")))
                for c in chunk_ids(t):
                    last = c == NCH - 1
                    q0 = CHUNK * (c % 4)
                    qn = min(CHUNK, T - CHUNK * c)
                    rows = slice(q0, q0 + qn)
                    tp = None
                    if not last:
                        for half in range(2):
                            b = R(f"m_{c}_{t}", half)
                            for i in range(4):
                                pr = 4 * half + i
                                for hd in (2 * pr, 2 * pr + 1):
                                    hr = hrows(hd)
                                    m = mm_(b[hr, P * i + hr.start:P * i + hr.stop], W12[rows, hd, 0:HD],
                                            tokB[rows, pr, hr], start=True, stop=True, tile_position=tpos(q0, hr))
                            m.then_inc(*rp.step(f"m_{c}_{t}", half))
                    if c > 0:
                        pe.wait_ge(*rv.at(f"s_{c - 1}_{(c - 1) // 4}"))
                    pe.wait_ge(*rv.at(f"q1_{UNITS - 1}_{t}"))
                    b = R(f"y_{c}_{t}")
                    for pr in range(PAIRS):
                        m = mm_(b[:, CHUNK * pr:CHUNK * pr + qn], S[:, pr, :], rT[:, pr, CHUNK * c:CHUNK * c + qn],
                                start=True, stop=True)
                    m.then_inc(*rp.step(f"y_{c}_{t}"))
                    if not last:
                        pe.wait_ge(*ra.at(f"m_{c}_{t}"))
                        for half in range(2):
                            b = R(f"s_{c}_{t}", half)
                            for i in range(4):
                                pr = 4 * half + i
                                mm_(b[:, P * i:P * i + P], M[:, pr, :], S[:, pr, :], start=True, stop=True)
                                for hd in (2 * pr, 2 * pr + 1):
                                    hr = hrows(hd)
                                    o = b[hr, P * i + hr.start:P * i + hr.stop]
                                    mm_(o, tokB[rows, pr, hr], W12[rows, hd, HD:P], start=False, stop=True,
                                        tile_position=tpos(q0, hr), skip_group_check=True)
                                    m = mm_(o, tokK[rows, pr, hr], tokV[rows, pr, hr], start=False, stop=True,
                                            tile_position=tpos(q0, hr), skip_group_check=True)
                            m.then_inc(*rp.step(f"s_{c}_{t}", half))
            for c in range(C8):
                pe.wait_ge(*rv.at(f"y_{NCH - 1}_{NT - 1}"))
                b = R("mean", c)
                mm_(b[:, 0:T], headones[:, :], yT[:, c, :], start=True, stop=True).then_inc(*rp.step("mean", c))
            for c in range(C8):
                pe.wait_ge(*ra.at("ysq", c))
                b = R("var", c)
                mm_(b[:, 0:T], headones[:, :], A[0][:, c, :], start=True, stop=True).then_inc(*rp.step("var", c))
            pe.wait_ge(*rv.at("yo"))
            for q in range(4):
                s = need(f"o{q}")
                for t, (r0, n) in enumerate(TILES):
                    b = R("o", 3 * q + t)
                    for c in range(C8):
                        m = mm_(b[0:n, 0:256], yT[:, c, r0:r0 + n], slot3(s)[:, c, :], start=(c == 0),
                                stop=(c == C8 - 1))
                    m.then_inc(*rp.step("o", 3 * q + t))

            def moe(l, prev_dve):
                st, ev = moe_pe[l], m_evac(l)
                pe.wait_ge(*prev_dve.end())
                for k in range(KC):
                    b = start(st, ev, "hT", k)
                    for t, (r0, n) in enumerate(TILES):
                        hv = h[0:n, t, :].rearrange("p (m k) -> p k m", k=KC)
                        m = nc.tensor.transpose(b[:, r0:r0 + n], hv[:, k, :], ident[0:n, 0:n])
                    m.then_inc(*st.step("hT", k))
                pe.wait_ge(*moe_dve[l].at("hT"))
                for t, (r0, n) in enumerate(TILES):
                    b = start(st, ev, "lg", t)
                    for k in range(KC):
                        m = mm_(b[0:n, 0:E], mhT[:, k, r0:r0 + n], router[:, l, k, :], start=(k == 0),
                                stop=(k == KC - 1))
                    m.then_inc(*st.step("lg", t))
                for u in range(4):
                    s = need(f"sh{u // 2}_{l}")
                    b = start(st, ev, "sg", u)
                    for k in range(KC):
                        w = ring[:, s, FF * k:FF * k + FF].rearrange("p (m j) -> p j m", j=2)
                        m = mm_(b[:, 0:T], w[:, u % 2, :], mhT[:, k, :], start=(k == 0), stop=(k == KC - 1))
                    m.then_inc(*st.step("sg", u))
                pe.wait_ge(*moe_dve[l].at("sel"))
                for t in range(NT + 1):
                    b = start(st, ev, "pos", t)
                    for t2 in range(min(t + 1, NT)):
                        m = mm_(b[:, 0:E], (before if t2 == t else allones)[:, :], sel[:, t2, :],
                                start=(t2 == 0), stop=(t2 == min(t, NT - 1)))
                    m.then_inc(*st.step("pos", t))
                s = need(f"sh2_{l}")
                pe.wait_ge(*moe_dve[l].at("sm"))
                for u in range(6):
                    r0, n = TILES[u // 2]
                    b = start(st, ev, "sd", u)
                    for j in range(2):
                        m = mm_(b[0:n, :], shm[:, j, r0:r0 + n], ring[:, s, D * j + 512 * (u % 2):][:, 0:512],
                                start=(j == 0), stop=(j == 1))
                    m.then_inc(*st.step("sd", u))
                pe.wait_ge(*moe_dve[l].end())
                pe.wait_ge(*moe_act[l].end())
                set_main(l)
                pe_experts(pe, main)
                run_spill(pe, l, lambda L, first: pe_experts(pe, L))

            moe(0, rv)

            pe.wait_ge(*end_dve[0].end())

            def G(name, u=0):
                return start(ap, a_evac, name, u)

            for k in range(KC):
                b = G("hT", k)
                for t, (r0, n) in enumerate(TILES):
                    hv = h[0:n, t, :].rearrange("p (m k) -> p k m", k=KC)
                    m = nc.tensor.transpose(b[:, r0:r0 + n], hv[:, k, :], ident[0:n, 0:n])
                m.then_inc(*ap.step("hT", k))
            pe.wait_ge(*av.at("hT"))
            for c in range(8):
                s = need(f"qkv{c // 2}")
                b = G("q", c)
                for k in range(KC):
                    m = mm_(b[:, 0:T], slot3(s)[:, k, P * (c % 2):P * (c % 2) + P], ahT[:, k, :], start=(k == 0),
                            stop=(k == KC - 1))
                m.then_inc(*ap.step("q", c))
            for g in range(KV):
                s = need("qkv4")
                b = G("k", g)
                for r in range(2):
                    for k in range(KC):
                        m = mm_(b[HD * r:HD * r + HD, 0:T], slot3(s)[:, k, HD * g:HD * g + HD], ahT[:, k, :],
                                start=(k == 0), stop=(k == KC - 1))
                m.then_inc(*ap.step("k", g))
            for c in range(2):
                s = need("qkv5")
                b = G("v", c)
                for k in range(KC):
                    m = mm_(b[:, 0:T], slot3(s)[:, k, P * c:P * c + P], ahT[:, k, :], start=(k == 0),
                            stop=(k == KC - 1))
                m.then_inc(*ap.step("v", c))
            pe.wait_ge(*aa.at("v"))
            for t, (r0, n) in enumerate(TILES):
                b = G("vt", t)
                for c in range(2):
                    m = nc.tensor.transpose(b[0:n, P * c:P * c + P], vcT[:, c, r0:r0 + n], ident[:, :])
                m.then_inc(*ap.step("vt", t))
            pe.wait_ge(bias_loaded, 16 * 6)
            pe.wait_ge(*av.at("vt"))
            for t, (r0, n) in enumerate(TILES):
                nk = NK[t]
                for g in range(KV):
                    for i, hd in enumerate(heads_of(g)):
                        b = G(f"sc{t}_{g}", i)
                        mm_(b[0:n, 0:nk], qT[hrows(hd), hd // 2, r0:r0 + n], kdT[hrows(hd), g, 0:nk], start=True,
                            stop=False)
                        mm_(b[0:n, 0:nk], anti[0:n, P - n:P], hank[t][0:n, hd, 0:nk], start=False,
                            stop=True).then_inc(*ap.step(f"sc{t}_{g}", i))
                    pe.wait_ge(*aa.at(f"ex{t}_{g}", 3))
                    for j in range(t + 1):
                        kj = TILES[j][1]
                        b = G(f"pt{t}_{g}", j)
                        for i in range(4):
                            m = nc.tensor.transpose(b[0:kj, n * i:n * i + n], prob[0:n, i, P * j:P * j + kj],
                                                    ident[0:n, 0:n])
                        m.then_inc(*ap.step(f"pt{t}_{g}", j))
                    pe.wait_ge(*av.at(f"pt{t}_{g}"))
                    b = G(f"pv{t}_{g}")
                    for i in range(4):
                        for j in range(t + 1):
                            kj = TILES[j][1]
                            m = mm_(b[0:n, HD * i:HD * i + HD], probT[0:kj, j, i, 0:n],
                                    vtok[0:kj, j, HD * g:HD * g + HD], start=(j == 0), stop=(j == t))
                    m.then_inc(*ap.step(f"pv{t}_{g}"))
            pe.wait_ge(*av.at(f"pv{NT - 1}_{KV - 1}"))
            for c in range(8):
                b = G("oT", c)
                for t, (r0, n) in enumerate(TILES):
                    m = nc.tensor.transpose(b[:, r0:r0 + n], otok[0:n, t, P * c:P * c + P], ident[0:n, 0:n])
                m.then_inc(*ap.step("oT", c))
            pe.wait_ge(*aa.at("oT"))
            for q in range(4):
                s = need(f"ao{q}")
                for t, (r0, n) in enumerate(TILES):
                    b = G("o", 3 * q + t)
                    for c in range(C8):
                        m = mm_(b[0:n, 0:256], oT[:, c, r0:r0 + n], slot3(s)[:, c, :], start=(c == 0),
                                stop=(c == C8 - 1))
                    m.then_inc(*ap.step("o", 3 * q + t))
            moe(1, av)

        @block.scalar
        def _(act):
            A_ = nc.scalar.activation

            def got(name, u=0, st=rp):
                act.wait_ge(*st.at(name, u))
                return psum_of(st, name, u)

            act.wait_ge(*rv.at("omk"))
            act.wait_ge(*consts.at("ones"))
            for nm, dst in (("r", rT), ("k", kT), ("v", vT)):
                for c in range(C8):
                    nc.scalar.copy(dst[:, c, :], got(nm, c)[:, 0:T]).then_inc(*ra.step(nm, c))
            act.wait_ge(*rp.at("bias"))
            A_(thid, got("wh")[0:LORA, 0:T], ACT.Tanh).then_inc(*ra.step("wh"))
            for c in range(C8):
                A_(wT[:, c, :], got("w", c)[:, 0:T], ACT.Sigmoid, bias=param(PW0, c)).then_inc(*ra.step("w", c))
            nc.scalar.copy(ahid, got("ah")[0:LORA, 0:T]).then_inc(*ra.step("ah"))
            for c in range(C8):
                A_(aT[:, c, :], got("a", c)[:, 0:T], ACT.Sigmoid, bias=param(PA0, c)).then_inc(*ra.step("a", c))
            A_(ghid[:, 0, :], got("gh", 0)[:, 0:T], ACT.Sigmoid).then_inc(*ra.step("gh", 0))
            A_(ghid[0:GLORA - P, 1, :], got("gh", 1)[0:GLORA - P, 0:T], ACT.Sigmoid).then_inc(*ra.step("gh", 1))
            for c in range(C8):
                nc.scalar.copy(gT[:, c, :], got("g", c)[:, 0:T]).then_inc(*ra.step("g", c))
            for c in range(C8):
                act.wait_ge(*rv.at("kk0", c))
                A_(tmpN(c), kkn[:, c, :], ACT.Square).then_inc(*ra.step("sq", c))
            for c in range(C8):
                b = got("n2", c)
                A_(tmpN(c), b[:, 0:T], ACT.Sqrt).then_inc(*ra.step("n2", c))
            for c in range(C8):
                act.wait_ge(*rv.at("cumx", c))
                A_(PMX[:, c, :], PMX[:, c, :], ACT.Exp, scale=-EXP_HALF).then_inc(*ra.step("pm", c))
            for c in range(C8):
                A_(PIN[:, c, :], cum[:, c, :], ACT.Exp, scale=EXP_HALF).then_inc(*ra.step("pi", c))
            act.wait_ge(*rv.at("kk"))
            for c in range(C8):
                A_(PEX[:, c, :], cum[:, c, :], ACT.Exp, scale=-EXP_HALF).then_inc(*ra.step("pp", c))
            for t, (r0, n) in enumerate(TILES):
                cols = slice(r0, r0 + n)
                if t == 0:
                    act.wait_ge(*rv.at("s0"))
                for j, dst in enumerate((tokB, tokK, tokV, tokZ)):
                    for half in range(2):
                        u = 2 * j + half
                        b = got(f"tr{t}", u)
                        nc.scalar.copy(dst[0:n, 4 * half:4 * half + 4, :],
                                       b[0:n, :].rearrange("p (i m) -> p i m", i=4)).then_inc(*ra.step(f"tr{t}", u))
                for g in range(UNITS):
                    def cp(name, dst, after=None):
                        nm = f"{name}_{g}_{t}"
                        b = got(nm)
                        if after:
                            act.wait_ge(*rp.at(f"{after}_{g}_{t}"))
                        nc.scalar.copy(dst[0:n, :, 0:n], b[0:n, :].rearrange("p (i m) -> p i m", i=4)[:, :, 0:n])\
                            .then_inc(*ra.step(nm))
                    cp("x2", X2)
                    cp("x2t", X2T)
                    cp("x4", X, "x2t")
                    cp("x4t", XT)
                    cp("x8", X2, "x4t")
                    cp("td", X, "x8")
                    cp("f", X2T)
                    nm = f"g1_{g}_{t}"
                    b = got(nm)
                    nc.scalar.copy(GZ[0:n], b[0:n, 0:4 * HD].rearrange("p (i m) -> p i m", i=4))\
                        .then_inc(*ra.step(nm))
                    nm = f"w12_{g}_{t}"
                    b = got(nm)
                    nc.scalar.copy(unit(W12, g, slice(0, n)), b[0:n, :].rearrange("p (i m) -> p i m", i=4))\
                        .then_inc(*ra.step(nm))
                    nm = f"q2_{g}_{t}"
                    b = got(nm)
                    hr, prs = hrows(g), slice(4 * (g // 2), 4 * (g // 2) + 4)
                    nc.scalar.copy(bT[hr, prs, cols], b[hr, :].rearrange("p (i m) -> p i m", i=4)[:, :, 0:n])\
                        .then_inc(*ra.step(nm))
                for c in chunk_ids(t):
                    if c == NCH - 1:
                        continue
                    if c > 0:
                        act.wait_ge(*rp.at(f"s_{c - 1}_{(c - 1) // 4}"))
                    for half in range(2):
                        b = got(f"m_{c}_{t}", half)
                        for r in range(2):
                            hr = slice(HD * r, HD * r + HD)
                            m = nc.scalar.copy(M[hr, 4 * half:4 * half + 4, hr],
                                               b[hr, :].rearrange("p (i m) -> p i m", i=4)[:, :, hr])
                        m.then_inc(*ra.step(f"m_{c}_{t}", half))
            for c in range(C8):
                act.wait_ge(*rv.at("ym", c))
                A_(A[0][:, c, :], yT[:, c, :], ACT.Square).then_inc(*ra.step("ysq", c))
            for c in range(C8):
                b = got("var", c)
                A_(A[0][:, c, :], b[:, 0:T], ACT.Sqrt, bias=eps[:, 1:2], scale=1.0 / HD).then_inc(*ra.step("std", c))

            def ln(sa, sv):
                act.wait_ge(*sv.at("ln", 2))
                A_(std, mv[:, :, 1], ACT.Sqrt, bias=eps[:, 0:1]).then_inc(*sa.step("ln"))

            ln(ra, rv)

            def moe(l, prev_dve):
                sa = moe_act[l]
                act.wait_ge(*prev_dve.end())
                act.wait_ge(*moe_dve[l].at("zero"))
                for t, (r0, n) in enumerate(TILES):
                    b = got("lg", t, moe_pe[l])
                    A_(score[0:n, t, :], b[0:n, 0:E], ACT.Sigmoid).then_inc(*sa.step("sc", t))
                for j in range(2):
                    b = got("sg", j, moe_pe[l])
                    A_(shid[:, j, :], b[:, 0:T], ACT.Silu).then_inc(*sa.step("sg", j))
                act.wait_ge(*moe_dve[l].end())
                set_main(l)
                act_experts(act, main)
                run_spill(act, l, lambda L, first: act_experts(act, L))
                ln(end_act[l], end_dve[l])

            moe(0, rv)
            act.wait_ge(*end_dve[0].end())
            act.wait_ge(bias_stored, 16)
            for t, (r0, n) in enumerate(TILES):
                off = T - (r0 + n)
                nk = NK[t]
                act.dma_start(hank[t][0:n, :, META:nk],
                              bass.AP(biasd.tensor, off + META, [[1, n], [2 * BIASLEN, HEADS], [1, nk - META]]))\
                    .then_inc(bias_loaded, 16)
                act.dma_start(hank[t][0:n, :, 0:META],
                              bass.AP(biasd.tensor, BIASLEN + off, [[1, n], [2 * BIASLEN, HEADS], [1, META]]))\
                    .then_inc(bias_loaded, 16)
            act.wait_ge(attn_loaded, 16 * 6)
            act.wait_ge(*av.at("sink"))
            for c in range(8):
                A_(qT[:, c, :], got("q", c, ap)[:, 0:T], ACT.Identity, bias=bq8[:, c:c + 1], scale=0.125)\
                    .then_inc(*aa.step("q", c))
            for g in range(KV):
                A_(kdT[:, g, :], got("k", g, ap)[:, 0:T], ACT.Identity, bias=bqkv[:, 8 + g:9 + g])\
                    .then_inc(*aa.step("k", g))
            for c in range(2):
                A_(vcT[:, c, :], got("v", c, ap)[:, 0:T], ACT.Identity, bias=bqkv[:, 12 + c:13 + c])\
                    .then_inc(*aa.step("v", c))
            for t, (r0, n) in enumerate(TILES):
                nk = NK[t]
                for g in range(KV):
                    act.wait_ge(*av.at(f"mx{t}_{g}", 3))
                    if (t, g) != (0, 0):
                        pt, pg = (t, g - 1) if g else (t - 1, KV - 1)
                        act.wait_ge(*ap.at(f"pt{pt}_{pg}"))
                    for i in range(4):
                        A_(prob[0:n, i, 0:nk], psum_of(ap, f"sc{t}_{g}", i)[0:n, 0:nk], ACT.Exp,
                           bias=negm[0:n, i:i + 1], accum_out=dens[0:n, i:i + 1]).then_inc(*aa.step(f"ex{t}_{g}", i))
                    A_(esink[0:n, :], esin[0:n, :], ACT.Exp).then_inc(*aa.step(f"ex{t}_{g}", 4))
            for c in range(8):
                nc.scalar.copy(oT[:, c, :], got("oT", c, ap)[:, 0:T]).then_inc(*aa.step("oT", c))
            ln(aa, av)
            moe(1, av)

        @block.vector
        def _(dve):
            V = nc.vector

            def got(name, u=0, st=rp):
                dve.wait_ge(*st.at(name, u))
                return psum_of(st, name, u)

            V.memset(relt_hidden, HIDDEN).then_inc(hidden_row, 1)
            V.tensor_copy(par, got("par")[:, 0:56]).then_inc(*rv.step("par"))
            dve.wait_ge(*rv.at("par"))
            V.tensor_scalar(omk, par[:, 8 * PKA:8 * PKA + 8], -1.0, 1.0, ALU.mult, ALU.add).then_inc(*rv.step("omk"))
            for k in range(KC):
                V.tensor_copy(hT[:, k, :], got("xT", k)[:, 0:T]).then_inc(*rv.step("xT", k))
            for j in range(4):
                V.tensor_copy(brow[:, j // 2, T * (j % 2):T * (j % 2) + T], got("bias", j)[0:HEADS, 0:T])\
                    .then_inc(*rv.step("bias", j))
            dve.wait_ge(*rv.at("xT"))
            V.tensor_tensor(xx[:, :, 1:T], hT[:, :, 0:T - 1], hT[:, :, 1:T], ALU.subtract).then_inc(*rv.step("xx", 0))
            V.tensor_scalar(xx[:, :, 0:1], hT[:, :, 0:1], -1.0, None, ALU.mult).then_inc(*rv.step("xx", 1))
            dve.wait_ge(*rv.at("xx"))
            prior = {3: "r", 1: "k", 4: "v", 5: "wh"}
            for m in (0, 2, 3, 1, 4, 5):
                if m in prior:
                    dve.wait_ge(*rp.at(prior[m]))
                for k in range(KC):
                    V.scalar_tensor_tensor(out=xm[MIXBUF[m]][:, k, :], in0=xx[:, k, :], scalar=mu[:, m, k:k + 1],
                                           in1=hT[:, k, :], op0=ALU.mult, op1=ALU.add).then_inc(*rv.step(f"mix{m}", k))
            dve.wait_ge(*rv.at("mix5"))
            dve.wait_ge(*ra.at("k"))
            for c in range(C8):
                V.tensor_scalar(kkn[:, c, :], kT[:, c, :], param(PKK, c), None, ALU.mult).then_inc(*rv.step("kk0", c))
            for c in range(C8):
                dve.wait_ge(*ra.at("w", c))
                V.tensor_tensor_scan(cum[:, c, :], notfirst[:, :], wT[:, c, :], 0.0, ALU.mult, ALU.add)\
                    .then_inc(*rv.step("cum", c))
            dve.wait_ge(*rp.at("gh"))
            for c in range(C8):
                dve.wait_ge(*rv.at("cum", c))
                V.tensor_tensor(PMX[:, c, :], cum[:, c, :], wT[:, c, :], ALU.subtract).then_inc(*rv.step("cumx", c))
            for c in range(C8):
                dve.wait_ge(*ra.at("n2", c))
                V.tensor_scalar(tmpN(c), tmpN(c), 1e-12, None, ALU.max).then_inc(rn_step, 1)
                dve.wait_ge(rn_step, c + 1)
                V.reciprocal(tmpN(c), tmpN(c)).then_inc(*rv.step("rn", c))
            for c in range(C8):
                dve.wait_ge(*rv.at("rn", c))
                V.tensor_tensor(kkn[:, c, :], kkn[:, c, :], tmpN(c), ALU.mult).then_inc(*rv.step("kk", c))
            dve.wait_ge(*ra.at("pp"))
            dve.wait_ge(*ra.at("g"))
            for c in range(C8):
                V.tensor_scalar(A[0][:, c, :], aT[:, c, :], param(PKA, c), omk[:, c:c + 1], ALU.mult, ALU.add)\
                    .then_inc(*rv.step("k2t", c))
            for c in range(C8):
                dve.wait_ge(*rv.at("k2t", c))
                V.tensor_tensor(kT[:, c, :], kT[:, c, :], A[0][:, c, :], ALU.mult).then_inc(*rv.step("k2", c))
            for c in range(C8):
                V.tensor_tensor(bT[:, c, :], kkn[:, c, :], aT[:, c, :], ALU.mult).then_inc(*rv.step("b", c))
            for c in range(C8):
                dve.wait_ge(*rv.at("k2", c))
                V.scalar_tensor_tensor(out=A[0][:, c, :], in0=rT[:, c, :], scalar=param(PRK, c), in1=kT[:, c, :],
                                       op0=ALU.mult, op1=ALU.mult).then_inc(*rv.step("rk", c))
            for c in range(C8):
                dve.wait_ge(*rv.at("b", c))
                V.scalar_tensor_tensor(out=zT[:, c, :], in0=kkn[:, c, :], scalar=-1.0, in1=PMX[:, c, :],
                                       op0=ALU.mult, op1=ALU.mult).then_inc(*rv.step("z", c))
            for c in range(C8):
                dve.wait_ge(*rv.at("z", c))
                V.tensor_tensor(bonus[:, c, :], got("bon", c)[:, 0:T], vT[:, c, :], ALU.mult)\
                    .then_inc(*rv.step("bonus", c))
            V.tensor_copy(pc[:, :, 0:NCH - 1],
                          PEX[:, :, 0:256].rearrange("p c (n s) -> p c n s", s=CHUNK)[:, :, :, CHUNK - 1])\
                .then_inc(*rv.step("pc", 0))
            V.tensor_copy(pc[:, :, NCH - 1:NCH], PEX[:, :, T - 1:T]).then_inc(*rv.step("pc", 1))
            for c in range(C8):
                V.tensor_tensor(bT[:, c, :], bT[:, c, :], PIN[:, c, :], ALU.mult).then_inc(*rv.step("bh", c))
            for c in range(C8):
                V.tensor_tensor(kT[:, c, :], kT[:, c, :], PIN[:, c, :], ALU.mult).then_inc(*rv.step("kh", c))
            dve.wait_ge(*rv.at("rk"))
            for c in range(C8):
                V.tensor_tensor(rT[:, c, :], rT[:, c, :], PEX[:, c, :], ALU.mult).then_inc(*rv.step("rh", c))
            dve.wait_ge(*rv.at("rh"))
            dve.wait_ge(bias_stored, 16)
            V.memset(M, 0.0)
            V.memset(S, 0.0).then_inc(*rv.step("s0"))
            dve.wait_ge(*rv.at("s0"))
            for t, (r0, n) in enumerate(TILES):
                cols = slice(r0, r0 + n)
                nch = -(-n // CHUNK)
                cs = min(CHUNK, n)
                if t:
                    dve.wait_ge(*rp.at(f"tr{t - 1}", 3))
                for nm, src, dst in (("bt", bT, btile), ("kt", kT, ktile)):
                    for c in range(C8):
                        m = V.tensor_tensor(dst[:, c, 0:n].rearrange("p (a s) -> p a s", s=cs),
                                            src[:, c, cols].rearrange("p (a s) -> p a s", s=cs),
                                            pc[:, c, 4 * t:4 * t + nch].unsqueeze(2).to_broadcast([P, nch, cs]),
                                            ALU.mult)
                    m.then_inc(*rv.step(f"{nm}{t}"))
                for g in range(UNITS):
                    N = lambda x: f"{x}_{g}_{t}"

                    def b4(name):
                        return got(N(name))[0:n, :].rearrange("p (i m) -> p i m", i=4)[:, :, 0:n]

                    def bc(mask):
                        return mask[0:n, 0:n].unsqueeze(1).to_broadcast([n, 4, n])

                    def masked_copy(name, step, dst, mask):
                        V.tensor_tensor(dst[0:n, :, 0:n], b4(name), bc(mask), ALU.mult).then_inc(*rv.step(N(step)))

                    if g or t:
                        pg, pt = (g - 1, t) if g else (UNITS - 1, t - 1)
                        dve.wait_ge(*rp.at(f"q2_{pg}_{pt}"))
                    masked_copy("ab", "ab", XT, up16)
                    dve.wait_ge(*rv.at(N("ab")))
                    V.tensor_tensor(TT[0:n, :, 0:n], XT[0:n, :, 0:n], bc(ident), ALU.add).then_inc(*rv.step(N("tt1")))
                    masked_copy("ba", "ba", X, low16)
                    masked_copy("ba", "off", OFF, lowoff)
                    masked_copy("ak", "ak", AK, up32)
                    masked_copy("bb", "bb", BB, up32d)
                    masked_copy("bk", "bk", BK, up32d)
                    for j in range(2, 6):
                        nm = f"tt{j}"
                        V.tensor_tensor(TT[0:n, :, 0:n], TT[0:n, :, 0:n], b4(nm), ALU.add).then_inc(*rv.step(N(nm)))
                    b = got(N("q1"))
                    hr, prs = hrows(g), slice(4 * (g // 2), 4 * (g // 2) + 4)
                    V.tensor_tensor(rT[hr, prs, cols], rT[hr, prs, cols],
                                    b[hr, :].rearrange("p (i m) -> p i m", i=4)[:, :, 0:n], ALU.add)\
                        .then_inc(*rv.step(N("q1")))
                for c in chunk_ids(t):
                    last = c == NCH - 1
                    qn = min(CHUNK, T - CHUNK * c)
                    cc = slice(CHUNK * c, CHUNK * c + qn)
                    if not last:
                        if c:
                            dve.wait_ge(*rv.at(f"s_{c - 1}_{(c - 1) // 4}"))
                        V.tensor_tensor(SP, S, pc[:, :, c:c + 1].to_broadcast([P, KC, P]), ALU.mult)\
                            .then_inc(*rv.step(f"sp_{c}_{t}"))
                    b = got(f"y_{c}_{t}")
                    dve.wait_ge(*ra.at(f"q2_{UNITS - 1}_{t}"))
                    V.tensor_tensor(yT[:, :, cc], bT[:, :, cc],
                                    b[:, 0:CHUNK * PAIRS].rearrange("p (c s) -> p c s", c=PAIRS)[:, :, 0:qn],
                                    ALU.add).then_inc(*rv.step(f"y_{c}_{t}"))
                    if not last:
                        dve.wait_ge(*rv.at(f"sp_{c}_{t}"))
                        dve.wait_ge(*rp.at(f"s_{c}_{t}"))
                        for half in range(2):
                            b = got(f"s_{c}_{t}", half)
                            V.tensor_tensor(S[:, 4 * half:4 * half + 4, :], SP[:, 4 * half:4 * half + 4, :],
                                            b.rearrange("p (i m) -> p i m", i=4), ALU.add)\
                                .then_inc(*rv.step(f"s_{c}_{t}", half))
            dve.wait_ge(*rv.at(f"y_{NCH - 1}_{NT - 1}"))
            dve.wait_ge(*rp.at("mean"))
            for c in range(C8):
                V.scalar_tensor_tensor(out=yT[:, c, :], in0=got("mean", c)[:, 0:T], scalar=-1.0 / HD,
                                       in1=yT[:, c, :], op0=ALU.mult, op1=ALU.add).then_inc(*rv.step("ym", c))
            for c in range(C8):
                dve.wait_ge(*ra.at("std", c))
                V.reciprocal(A[0][:, c, :], A[0][:, c, :]).then_inc(*rv.step("yr", c))
            for c in range(C8):
                dve.wait_ge(*rv.at("yr", c))
                V.tensor_tensor(yT[:, c, :], yT[:, c, :], A[0][:, c, :], ALU.mult).then_inc(*rv.step("yn", c))
            for c in range(C8):
                dve.wait_ge(*rv.at("yn", c))
                V.tensor_scalar(yT[:, c, :], yT[:, c, :], param(PLG, c), param(PLB, c), ALU.mult, ALU.add)\
                    .then_inc(*rv.step("yg", c))
            for c in range(C8):
                dve.wait_ge(*rv.at("yg", c))
                V.tensor_tensor(yT[:, c, :], yT[:, c, :], bonus[:, c, :], ALU.add).then_inc(*rv.step("yb", c))
            for c in range(C8):
                dve.wait_ge(*rv.at("yb", c))
                V.tensor_tensor(yT[:, c, :], yT[:, c, :], gT[:, c, :], ALU.mult).then_inc(*rv.step("yo", c))
            dve.wait_ge(*rv.at("yo"))
            dve.wait_ge(h_loaded, 64)

            def residual(steps, st, acc):
                for q in range(4):
                    for t, (r0, n) in enumerate(TILES):
                        b = got("o", 3 * q + t, st)
                        V.scalar_tensor_tensor(out=acc[0:n, t, 256 * q:256 * q + 256],
                                               in0=h[0:n, t, 256 * q:256 * q + 256], scalar=ALPHA,
                                               in1=b[0:n, 0:256], op0=ALU.mult, op1=ALU.add)\
                            .then_inc(*steps.step("res", 3 * q + t))

            def ln(steps, sa, acc, which):
                for t, (r0, n) in enumerate(TILES):
                    for j in range(2):
                        m = V.bn_stats(stat[0:n, t, 6 * j:6 * j + 6], acc[0:n, t, 512 * j:512 * j + 512])
                m.then_inc(*steps.step("ln", 0))
                dve.wait_ge(*steps.at("ln", 0))
                V.memset(mv, 1.0).then_inc(*steps.step("ln", 1))
                dve.wait_ge(*steps.at("ln", 1))
                for t, (r0, n) in enumerate(TILES):
                    m = V.bn_aggr(mv[0:n, t, :], stat[0:n, t, :])
                m.then_inc(*steps.step("ln", 2))
                dve.wait_ge(*sa.at("ln"))
                V.reciprocal(rstd, std).then_inc(*steps.step("ln", 3))
                dve.wait_ge(*steps.at("ln", 3))
                dve.wait_ge(ln_loaded, 32 * which)
                u = 4
                for j in range(2):
                    for t, (r0, n) in enumerate(TILES):
                        if j == 0:
                            m = V.tensor_scalar(acc[0:n, t, :], acc[0:n, t, :], mv[0:n, t, 0:1], rstd[0:n, t:t + 1],
                                                ALU.subtract, ALU.mult)
                        if j == 1:
                            m = V.tensor_tensor(acc[0:n, t, :], acc[0:n, t, :], lnrow[0:n, 0, :], ALU.mult)
                    m.then_inc(*steps.step("ln", u))
                    dve.wait_ge(*steps.at("ln", u))
                    u += 1
                for t, (r0, n) in enumerate(TILES):
                    V.tensor_tensor(h[0:n, t, :], acc[0:n, t, :], lnrow[0:n, 1, :], ALU.add)\
                        .then_inc(*steps.step("ln", u))
                    u += 1
                dve.wait_ge(*steps.at("ln"))

            residual(rv, rp, facc)
            dve.wait_ge(*rv.at("res"))
            ln(rv, ra, facc, 1)

            def moe(l):
                st = moe_dve[l]
                sp_ = moe_pe[l]

                def fin(ins, name, u=0):
                    ins.then_inc(*st.step(name, u))
                    dve.wait_ge(*st.at(name, u))

                V.memset(score, 0.0).then_inc(*st.step("zero", 0))
                V.memset(xg[0], 0.0).then_inc(*st.step("zero", 1))
                V.memset(xg[1], 0.0).then_inc(*st.step("zero", 2))
                V.memset(gate_s[0], 0.0).then_inc(*st.step("zero", 3))
                V.memset(values, 0.0).then_inc(*st.step("zero", 4))
                for k in range(KC):
                    V.tensor_copy(mhT[:, k, :], got("hT", k, sp_)[:, 0:T]).then_inc(*st.step("hT", k))
                dve.wait_ge(route_consts, l + 1)
                dve.wait_ge(*moe_act[l].at("sc"))
                fin(V.tensor_tensor(choice, score, rbias[:, l, :].unsqueeze(1).to_broadcast([P, NT, E]), ALU.add),
                    "choice")
                for t in range(NT):
                    for g in range(GROUPS):
                        V.max(top2[:, t, 8 * g:8 * g + 8], choice[:, t, GE * g:GE * g + GE])\
                            .then_inc(*st.step("top2", GROUPS * t + g))
                dve.wait_ge(*st.at("top2"))
                t2 = top2.rearrange("p t (g k) -> p t g k", k=8)
                fin(V.tensor_tensor(gsc, t2[:, :, :, 0], t2[:, :, :, 1], ALU.add), "gs")
                for t in range(NT):
                    a = gsc[:, t, :].unsqueeze(1).to_broadcast([P, GROUPS, GROUPS])
                    c = gsc[:, t, :].unsqueeze(2).to_broadcast([P, GROUPS, GROUPS])
                    fin(V.tensor_tensor(cmp1, a, c, ALU.is_gt), "rank", 5 * t)
                    fin(V.tensor_tensor(cmp2, a, c, ALU.is_equal), "rank", 5 * t + 1)
                    fin(V.tensor_tensor(cmp2, cmp2, tie, ALU.mult), "rank", 5 * t + 2)
                    fin(V.tensor_tensor(cmp1, cmp1, cmp2, ALU.add), "rank", 5 * t + 3)
                    fin(V.tensor_reduce(grank[:, t, :], cmp1, AX.X, ALU.add), "rank", 5 * t + 4)
                fin(V.tensor_scalar(keep, grank, TOP_GROUPS - 0.5, None, ALU.is_lt), "keep")
                fin(V.tensor_scalar(grank, keep, -HIDDEN, HIDDEN, ALU.mult, ALU.add), "hide")
                kb = keep.rearrange("p t g -> p (t g)").unsqueeze(2).to_broadcast([P, NT * GROUPS, GE])
                hb = grank.rearrange("p t g -> p (t g)").unsqueeze(2).to_broadcast([P, NT * GROUPS, GE])
                mk = masked.rearrange("p t (g e) -> p (t g) e", e=GE)
                fin(V.tensor_tensor(mk, choice.rearrange("p t (g e) -> p (t g) e", e=GE), kb, ALU.mult), "mask", 0)
                fin(V.tensor_tensor(mk, mk, hb, ALU.add), "mask", 1)
                for t in range(NT):
                    fin(V.max(top8[:, t, :], masked[:, t, :]), "top8", 2 * t)
                    fin(V.match_replace(taken[:, t, :], top8[:, t, :], masked[:, t, :], 2 * HIDDEN), "top8", 2 * t + 1)
                fin(V.tensor_tensor(sel, taken, masked, ALU.not_equal), "sel", 0)
                fin(V.tensor_tensor(sel, sel, rowok.unsqueeze(2).to_broadcast([P, NT, E]), ALU.mult), "sel", 1)
                dve.wait_ge(*moe_act[l].at("sg"))
                for j in range(2):
                    V.tensor_tensor(shm[:, j, :], shid[:, j, :], got("sg", 2 + j, sp_)[:, 0:T], ALU.mult)\
                        .then_inc(*st.step("sm", j))
                fin(V.tensor_tensor(gate, score, sel, ALU.mult), "g0")
                fin(V.tensor_reduce(gsum, gate, AX.X, ALU.add), "gsum")
                fin(V.tensor_scalar(rowbad, rowok, -1.0, 1.0, ALU.mult, ALU.add), "grec", 0)
                fin(V.tensor_tensor(gsum, gsum, rowbad, ALU.add), "grec", 1)
                fin(V.reciprocal(grec, gsum), "g1")
                v3 = values.rearrange("p t (e c) -> p t e c", c=3)
                fin(V.scalar_tensor_tensor(out=v3[:, :, :, 2], in0=gate, scalar=SCALE,
                                           in1=grec.unsqueeze(2).to_broadcast([P, NT, E]), op0=ALU.mult,
                                           op1=ALU.mult), "g2")
                for t in range(NT):
                    fin(V.tensor_tensor_scan(krank[:, t, :], allones[:, 0:E], sel[:, t, :], 0.0, ALU.mult, ALU.add),
                        "kr", t)
                fin(V.tensor_tensor(krank, krank, sel, ALU.subtract), "kr2")
                for t in range(NT):
                    fin(V.tensor_scalar(dest8[:, t:t + 1], tokid[:, t:t + 1], float(TOPK), -OUT_OF_RANGE,
                                        ALU.mult, ALU.add), "dest", t)
                for t in range(NT):
                    V.tensor_scalar(v3[:, t, :, 1], krank[:, t, :], dest8[:, t:t + 1], None, ALU.add)
                    V.tensor_scalar(v3[:, t, :, 0], sel[:, t, :], 0.0, tokid[:, t:t + 1], ALU.mult, ALU.add)\
                        .then_inc(*st.step("tok", t))
                dve.wait_ge(*st.at("tok"))
                for t in range(NT):
                    b = got("pos", t, sp_)
                    V.scalar_tensor_tensor(out=posm[:, t, :], in0=b[:, 0:E], scalar=1.0, in1=sel[:, t, :],
                                           op0=ALU.add, op1=ALU.mult).then_inc(*st.step("pos", t))
                dve.wait_ge(*st.at("pos"))
                fin(V.tensor_scalar(posm, posm, -1.0, None, ALU.add), "pos2")
                fin(V.tensor_reduce(most, got("pos", 3, sp_)[:, 0:E], AX.X, ALU.max), "max")
                V.tensor_scalar(v3[:, :, :, 0], v3[:, :, :, 0], -OUT_OF_RANGE, None, ALU.add)
                fin(V.tensor_copy(mosti_of[l], most), "maxi")
                for u in range(6):
                    r0, n = TILES[u // 2]
                    cs = slice(512 * (u % 2), 512 * (u % 2) + 512)
                    V.scalar_tensor_tensor(out=macc[0:n, u // 2, cs], in0=h[0:n, u // 2, cs], scalar=ALPHA,
                                           in1=got("sd", u, sp_)[0:n, :], op0=ALU.mult, op1=ALU.add)\
                        .then_inc(*st.step("sd", u))
                dve.wait_ge(*st.at("sd"))
                set_main(l)
                dve_experts(dve, main, 0)
                run_spill(dve, l, lambda L, first: dve_experts(dve, L, first))
                es = end_dve[l]
                for t, (r0, n) in enumerate(TILES):
                    dve.wait_ge(routed_loaded[t], 16 * (l + 1))
                    for k in range(TOPK):
                        V.tensor_tensor(macc[0:n, t, :], macc[0:n, t, :], rt[t % 2][0:n, k, :], ALU.add)\
                            .then_inc(*es.step("sum", TOPK * t + k))
                        dve.wait_ge(*es.at("sum", TOPK * t + k))
                ln(es, end_act[l], macc, 2 + 2 * l)

            moe(0)

            dve.wait_ge(attn_loaded, 16 * 6)
            V.tensor_scalar(bq8, bqkv[:, 0:8], 0.125, None, ALU.mult).then_inc(*av.step("sink"))
            for k in range(KC):
                V.tensor_copy(ahT[:, k, :], got("hT", k, ap)[:, 0:T]).then_inc(*av.step("hT", k))
            for t, (r0, n) in enumerate(TILES):
                V.tensor_copy(vtok[0:n, t, :], got("vt", t, ap)[0:n, 0:256]).then_inc(*av.step("vt", t))
            for t, (r0, n) in enumerate(TILES):
                nk = NK[t]
                for g in range(KV):
                    nm = f"mx{t}_{g}"
                    if (t, g) != (0, 0):
                        pt, pg = (t, g - 1) if g else (t - 1, KV - 1)
                        dve.wait_ge(*aa.at(f"ex{pt}_{pg}"))
                    for i in range(4):
                        b = got(f"sc{t}_{g}", i, ap)
                        m = V.tensor_reduce(negm[0:n, i:i + 1], b[0:n, 0:nk], AX.X, ALU.max)
                    m.then_inc(*av.step(nm, 0))
                    dve.wait_ge(*av.at(nm, 0))
                    V.tensor_tensor(negm[0:n, :], negm[0:n, :], sinks[0:n, 4 * g:4 * g + 4], ALU.max)\
                        .then_inc(*av.step(nm, 1))
                    dve.wait_ge(*av.at(nm, 1))
                    V.tensor_tensor(esin[0:n, :], sinks[0:n, 4 * g:4 * g + 4], negm[0:n, :], ALU.subtract)\
                        .then_inc(*av.step(nm, 2))
                    dve.wait_ge(*av.at(nm, 2))
                    V.tensor_scalar(negm[0:n, :], negm[0:n, :], -1.0, None, ALU.mult).then_inc(*av.step(nm, 3))
                    dn = f"den{t}_{g}"
                    dve.wait_ge(*aa.at(f"ex{t}_{g}", 4))
                    V.tensor_tensor(dens2[0:n, :], dens[0:n, :], esink[0:n, :], ALU.add).then_inc(*av.step(dn, 0))
                    dve.wait_ge(*av.at(dn, 0))
                    V.reciprocal(dens2[0:n, :], dens2[0:n, :]).then_inc(*av.step(dn, 1))
                    if (t, g) != (0, 0):
                        dve.wait_ge(*ap.at(f"pv{pt}_{pg}"))
                    for j in range(t + 1):
                        kj = TILES[j][1]
                        b = got(f"pt{t}_{g}", j, ap)
                        V.tensor_copy(probT[0:kj, j, :, 0:n], b[0:kj, 0:4 * n].rearrange("p (i m) -> p i m", i=4))\
                            .then_inc(*av.step(f"pt{t}_{g}", j))
                    b = got(f"pv{t}_{g}", 0, ap)
                    dve.wait_ge(*av.at(dn, 1))
                    for i in range(4):
                        V.tensor_scalar(otok[0:n, t, HD * (4 * g + i):HD * (4 * g + i) + HD],
                                        b[0:n, HD * i:HD * i + HD], dens2[0:n, i:i + 1], None, ALU.mult)\
                            .then_inc(*av.step(f"pv{t}_{g}", i))
            residual(av, ap, aacc)
            dve.wait_ge(*av.at("res"))
            for t, (r0, n) in enumerate(TILES):
                V.tensor_tensor(aacc[0:n, t, :], aacc[0:n, t, :], borow[0:n, :], ALU.add).then_inc(*av.step("bo", t))
            dve.wait_ge(*av.at("bo"))
            ln(av, aa, aacc, 3)
            moe(1)


_INS = ['x', 'meta', 'rel_bias', 'rwkv_mu', 'rwkv_w0', 'rwkv_w1', 'rwkv_w2', 'rwkv_a0', 'rwkv_a1', 'rwkv_a2',
        'rwkv_g1', 'rwkv_g2', 'rwkv_k_k', 'rwkv_k_a', 'rwkv_r_k', 'rwkv_w_r', 'rwkv_w_k', 'rwkv_w_v', 'rwkv_w_o',
        'rwkv_lnx_g', 'rwkv_lnx_b', 'attn_w_qkv', 'attn_b_qkv', 'attn_sinks', 'attn_w_o', 'attn_b_o', 'ln_mix_g',
        'ln_mix_b', 'ln_ffn_g', 'ln_ffn_b', 'moe_router', 'moe_bias', 'moe_w_gate', 'moe_w_up', 'moe_w_down',
        'shared_w_gate', 'shared_w_up', 'shared_w_down']


def kernel(**inputs):
    import numpy as _np
    import concourse.bacc as _bacc
    from concourse import mybir as _mybir
    from concourse.bass_utils import run_bass_kernel_spmd as _run

    nc = _bacc.Bacc("TRN2", target_bir_lowering=False, num_devices=1)
    arrays, aps = {}, {}
    for name in _INS:
        arrays[f"in_{name}"] = _np.ascontiguousarray(inputs[name])
    arrays["in_t5"] = t5_one_hot()
    for name, a in arrays.items():
        aps[name[3:]] = nc.dram_tensor(name, a.shape, _mybir.dt.from_np(a.dtype), kind="ExternalInput").ap()
    out = nc.dram_tensor("out_0", (1, SEQ, D), _mybir.dt.float32, kind="ExternalOutput").ap()
    hybrid_trunk(nc, aps, out)
    r = _run(nc, [arrays], core_ids=[0])
    return r.results[0]["out_0"]
```

```python
from contextlib import ExitStack

import numpy as np

import concourse.bass as bass
from concourse import mybir

ALU = mybir.AluOpType
ACT = mybir.ActivationFunctionType
AX = mybir.AxisListType
F32 = mybir.dt.float32
I32 = mybir.dt.int32

D = 1024
SEQ = 256
META = 16
T = SEQ + META
P = 128
KC = D // P
TILES = [(0, 128), (128, 128), (256, 16)]
NT = len(TILES)
HEADS = 16
HD = 64
PAIRS = HEADS // 2
CHUNK = 32
HALF = 16
NCH = -(-T // CHUNK)
LORA = 64
GLORA = 160
GN_EPS = 64e-5
LN_EPS = 1e-5
EXP_HALF = float(np.exp(-0.5))
ALPHA = float((2 * 2) ** 0.25)
KV = 4
GROUP = HEADS // KV
WINDOW = 128
BUCKETS = 32
QKV = (HEADS + 2 * KV) * HD
E = 64
TOPK = 8
GROUPS = 8
GE = E // GROUPS
TOP_GROUPS = 4
FF = 256
SCALE = 2.5
SLOTS = 64
UNROLL = 8
HEAD = 5
TAIL = 3
SETS = 4
RING = 6
SLOT = 2048
OUT_OF_RANGE = 65536.0
HIDDEN = -1.0e30
BIASLEN = 2 * T


class Steps:

    def __init__(self, sem, order):
        self.sem, self.first, self.units, n = sem, {}, dict(order), 0
        for name, units in order:
            self.first[name] = n
            n += units
        self.total, self.done = n, 0

    def index(self, name, u=0):
        assert 0 <= u < self.units[name], (name, u)
        return self.first[name] + u

    def at(self, name, u=None):
        return self.sem, self.index(name, self.units[name] - 1 if u is None else u) + 1

    def step(self, name, u=0):
        assert self.index(name, u) == self.done, (name, u, self.index(name, u), self.done)
        self.done += 1
        return self.sem, 1

    def end(self):
        return self.sem, self.total


def t5_one_hot():
    exact = BUCKETS // 2
    d = T - 1 - np.arange(BIASLEN)
    near = np.maximum(d, 1).astype(np.float32)
    ratio = np.log(near / np.float32(exact)) / np.float32(np.log(128 / exact))
    large = np.minimum(exact + (ratio * (BUCKETS - exact)).astype(np.int32), BUCKETS - 1)
    bucket = np.where(d < exact, np.maximum(d, 0), large)
    out = np.zeros((BUCKETS + 1, 2, BIASLEN), np.float32)
    for plane, hidden in enumerate(((d < 0) | (d >= WINDOW), d < 0)):
        out[np.where(hidden, BUCKETS, bucket), plane, np.arange(BIASLEN)] = 1.0
    return out


def hybrid_trunk(nc, I, out):
    with ExitStack() as ctx:
        def sb(name, shape, dt=F32):
            return ctx.enter_context(nc.sbuf_tensor(name, shape, dt))

        def sem(name):
            return ctx.enter_context(nc.semaphore(name))

        ps = ctx.enter_context(nc.psum_tensor("ps", [P, 8, 512], F32))

        ring = sb("ring", [P, RING, SLOT])
        h = sb("h", [P, NT, D])
        lnrow = sb("lnrow", [P, 2, D])
        router = sb("router", [P, 2, KC, E])
        rbias = sb("rbias", [P, 2, E])
        ident = sb("ident", [P, P])
        anti = sb("anti", [P, P])
        allones = sb("allones", [P, P])
        headones = sb("headones", [P, P])
        up16 = sb("up16", [P, P])
        up32 = sb("up32", [P, P])
        up32d = sb("up32d", [P, P])
        low16 = sb("low16", [P, P])
        lowoff = sb("lowoff", [P, P])
        before = sb("before", [P, P])
        notfirst = sb("notfirst", [P, T])
        small = sb("small", [P, 256])
        eps = sb("eps", [P, 2])
        most_tokens = sb("most_tokens", [P, 2], I32)
        arena = sb("arena", [P, 32300])

        def view(at, *shape, rows=P, dt=None):
            n = int(np.prod(shape))
            assert at + n <= 32300, (at, n)
            v = arena[0:rows, at:at + n]
            if dt is not None:
                v = v.bitcast(dt)
            if len(shape) == 2:
                v = v.rearrange("p (a b) -> p a b", a=shape[0])
            if len(shape) == 3:
                v = v.rearrange("p (a b c) -> p a b c", a=shape[0], b=shape[1])
            return v

        routed = [nc.dram_tensor(f"routed{l}", (T * TOPK, D), F32, kind="Internal").ap() for l in range(2)]
        biasd = nc.dram_tensor("biasd", (HEADS, 2, BIASLEN), F32, kind="Internal").ap()

        consts = Steps(sem("consts_ready"), [("ones", 3), ("made", 1)])
        x_loaded = sem("x_loaded")
        h_loaded = sem("h_loaded")
        params_loaded = sem("params_loaded")
        attn_loaded = sem("attn_loaded")
        ln_loaded = sem("ln_loaded")
        bias_stored = sem("bias_stored")
        bias_loaded = sem("bias_loaded")
        routed_loaded = [sem(f"routed_loaded{t}") for t in range(NT)]
        out_stored = sem("out_stored")
        hidden_row = sem("hidden_row")
        rn_step = sem("rn_step")
        route_consts = sem("route_consts")
        slot_loaded = [sem(f"slot_loaded{s}") for s in range(3 * SETS)]

        def per_tile(steps):
            return [(f"{n}{t}", u) for t in range(NT) for n, u in steps(t)]

        UNITS = 4

        def chunk_ids(t):
            return range(t * 4, min(t * 4 + 4, NCH))

        def rw_pe_tile(t):
            for g in range(UNITS):
                for n in ("ab", "ba", "ak", "bb", "bk", "x2", "x2t", "tt2", "x4", "x4t", "tt3", "x8", "tt4",
                          "td", "f", "tt5", "g1", "w12", "q1", "q2"):
                    yield f"{n}_{g}_", 1

        def rw_order(t, who):
            o = []
            if who == "pe":
                o += [("tr", 8)]
                o += list(rw_pe_tile(t))
            if who == "dve":
                o += [("bt", 1), ("kt", 1)]
                for g in range(UNITS):
                    o += [(f"{n}_{g}_", 1) for n in ("ab", "tt1", "ba", "off", "ak", "bb", "bk", "tt2", "tt3",
                                                     "tt4", "tt5", "q1")]
            if who == "act":
                o += [("tr", 8)]
                for g in range(UNITS):
                    o += [(f"{n}_{g}_", 1) for n in ("x2", "x2t", "x4", "x4t", "x8", "td", "f", "g1", "w12",
                                                     "q2")]
            for c in chunk_ids(t):
                last = c == NCH - 1
                if who == "pe":
                    o += ([] if last else [(f"m_{c}_", 2)]) + [(f"y_{c}_", 1)] + ([] if last else [(f"s_{c}_", 2)])
                if who == "act" and not last:
                    o += [(f"m_{c}_", 2)]
                if who == "dve":
                    o += ([] if last else [(f"sp_{c}_", 1)]) + [(f"y_{c}_", 1)] + ([] if last else [(f"s_{c}_", 2)])
            return o

        C8 = KC
        rp = Steps(sem("rwkv_pe"), [("par", 1), ("xT", C8), ("bias", 4), ("r", C8), ("k", C8), ("v", C8),
                                    ("wh", 1), ("w", C8), ("ah", 1), ("a", C8), ("gh", 2), ("g", C8),
                                    ("n2", C8), ("bon", C8)]
                   + per_tile(lambda t: rw_order(t, "pe"))
                   + [("mean", C8), ("var", C8), ("o", 12)])
        ra = Steps(sem("rwkv_act"), [("r", C8), ("k", C8), ("v", C8), ("wh", 1), ("w", C8), ("ah", 1),
                                     ("a", C8), ("gh", 2), ("g", C8), ("sq", C8), ("n2", C8), ("pm", C8), ("pi", C8),
                                     ("pp", C8)]
                   + per_tile(lambda t: rw_order(t, "act"))
                   + [("ysq", C8), ("std", C8), ("ln", 1)])
        rv = Steps(sem("rwkv_dve"), [("par", 1), ("omk", 1), ("xT", C8), ("bias", 4), ("xx", 2),
                                     ("mix0", C8), ("mix2", C8), ("mix3", C8), ("mix1", C8), ("mix4", C8),
                                     ("mix5", C8), ("kk0", C8), ("cum", C8), ("cumx", C8), ("rn", C8), ("kk", C8),
                                     ("k2t", C8), ("k2", C8), ("b", C8), ("rk", C8), ("z", C8), ("bonus", C8), ("pc", 2),
                                     ("bh", C8), ("kh", C8), ("rh", C8), ("s0", 1)]
                   + per_tile(lambda t: rw_order(t, "dve"))
                   + [("ym", C8), ("yr", C8), ("yn", C8), ("yg", C8), ("yb", C8), ("yo", C8), ("res", 12),
                      ("ln", 9)])

        moe_pe = [Steps(sem(f"route_pe{l}"), [("hT", KC), ("lg", NT), ("sg", 4), ("pos", 4), ("sd", 6)])
                  for l in range(2)]
        moe_act = [Steps(sem(f"route_act{l}"), [("sc", NT), ("sg", 2)]) for l in range(2)]
        moe_dve = [Steps(sem(f"route_dve{l}"),
                         [("zero", 2), ("hT", KC), ("choice", 1), ("top2", 24), ("gs", 1), ("rank", 15), ("keep", 1),
                          ("hide", 1), ("mask", 2), ("top8", 6), ("sel", 2), ("sm", 2), ("g0", 1), ("gsum", 1),
                          ("grec", 2), ("g1", 1),
                          ("g2", 1), ("kr", 3), ("kr2", 1), ("dest", 3), ("tok", 3), ("pos", 3), ("pos2", 1),
                          ("max", 1), ("maxi", 1), ("sd", 6)]) for l in range(2)]
        end_act = [Steps(sem(f"combine_act{l}"), [("ln", 1)]) for l in range(2)]
        end_dve = [Steps(sem(f"combine_dve{l}"), [("sum", 8 * NT), ("ln", 9)]) for l in range(2)]

        NK = [128, 256, 272]
        ab_pe = [("hT", KC), ("q", 8), ("k", 4), ("v", 2), ("vt", 3)]
        ab_act = [("q", 8), ("k", 4), ("v", 2)]
        ab_dve = [("sink", 1), ("hT", KC), ("vt", 3)]
        for t in range(NT):
            for g in range(KV):
                ab_pe += [(f"sc{t}_{g}", 4), (f"pt{t}_{g}", t + 1), (f"pv{t}_{g}", 1)]
                ab_act += [(f"ex{t}_{g}", 5)]
                ab_dve += [(f"mx{t}_{g}", 4), (f"den{t}_{g}", 2), (f"pt{t}_{g}", t + 1), (f"pv{t}_{g}", 4)]
        ab_pe += [("oT", 8), ("o", 12)]
        ab_act += [("oT", 8), ("ln", 1)]
        ab_dve += [("res", 12), ("bo", 3), ("ln", 9)]
        ap, aa, av = (Steps(sem("attn_pe"), ab_pe), Steps(sem("attn_act"), ab_act), Steps(sem("attn_dve"), ab_dve))

        slot_count = [0] * (3 * SETS)
        slot_free = [None] * (3 * SETS)
        landed = {}
        fills = {}

        def w_split(w, n0, n):
            return w[:, n0:n0 + n].rearrange("(p k) n -> p k n", k=KC)

        def w_nat(w, n0, n):
            return w[:, n0:n0 + n].rearrange("(c p) n -> p c n", p=P)

        def slot3(s, k=KC):
            return ring[:, s, :].rearrange("p (k n) -> p k n", k=k)

        def plan(group, name, slot, pieces, released_by):
            fills.setdefault(group, []).append((slot, pieces, slot_free[slot]))
            slot_count[slot] += 16 * len(pieces)
            landed[name] = (slot_loaded[slot], slot_count[slot], slot)
            slot_free[slot] = released_by

        n = 0
        for what, w in (("r", I["rwkv_w_r"]), ("k", I["rwkv_w_k"]), ("v", I["rwkv_w_v"])):
            for q in range(4):
                plan("rwkv", f"{what}{q}", n % RING, [(slot3(n % RING), w_split(w[0], 256 * q, 256))],
                     rp.at(what, 2 * q + 1))
                n += 1
        s = n % RING
        plan("rwkv", "w", s, [(ring[:, s, 0:512], I["rwkv_w1"][0].rearrange("(p k) n -> p (k n)", k=KC)),
                              (ring[0:LORA, s, 512:1536], I["rwkv_w2"][0])], rp.at("w"))
        s = (n + 1) % RING
        plan("rwkv", "a", s, [(ring[:, s, 0:512], I["rwkv_a1"][0].rearrange("(p k) n -> p (k n)", k=KC)),
                              (ring[0:LORA, s, 512:1536], I["rwkv_a2"][0])], rp.at("a"))
        s = (n + 2) % RING
        plan("rwkv", "g1", s, [(ring[:, s, 0:KC * GLORA], I["rwkv_g1"][0].rearrange("(p k) n -> p (k n)", k=KC))],
             rp.at("gh"))
        s = (n + 3) % RING
        plan("rwkv", "g2", s, [(ring[:, s, 0:1024], I["rwkv_g2"][0, 0:P]),
                               (ring[0:GLORA - P, s, 1024:2048], I["rwkv_g2"][0, P:GLORA])], rp.at("g"))
        n += 4
        for q in range(4):
            plan("rwkv", f"o{q}", n % RING, [(slot3(n % RING), w_nat(I["rwkv_w_o"][0], 256 * q, 256))],
                 rp.at("o", 3 * q + 2))
            n += 1

        def plan_shared(l):
            for j, w in enumerate((I["shared_w_gate"], I["shared_w_up"])):
                plan(f"moe{l}", f"sh{j}_{l}", 3 + j, [(ring[:, 3 + j, :], w[l].rearrange("(p k) n -> p (k n)", k=KC))],
                     moe_pe[l].at("sg"))
            plan(f"moe{l}", f"sh2_{l}", 5,
                 [(ring[:, 5, :], I["shared_w_down"][l].rearrange("(p j) n -> p (j n)", j=2))], moe_pe[l].at("sd"))

        class Main:
            onehot, values, index = sem("onehot_made"), sem("values_picked"), sem("index_ready")
            x, x_copied = sem("x_picked"), sem("x_copied")
            xt, xt_copied = sem("x_turned"), sem("xt_copied")
            gu, gu_copied, turned = sem("gate_up_done"), sem("gate_up_copied"), sem("gate_up_turned")
            silu, hid = sem("silu_done"), sem("hidden_ready")
            down, y_a, y_v = sem("down_done"), sem("y_scaled_act"), sem("y_scaled_dve")
            scattered = [sem(f"scattered{b}") for b in range(4)]
            base, slot_base, entry_free = 0, None, None

        class Spill:

            def __init__(self, l):
                def s(n):
                    return sem(f"spill{l}_{n}")
                self.onehot, self.values, self.index = s("onehot"), s("values"), s("index")
                self.x, self.x_copied, self.gu, self.gu_copied = s("x"), s("x_copied"), s("gu"), s("gu_copied")
                self.xt, self.xt_copied = s("xt"), s("xt_copied")
                self.turned, self.silu, self.hid = s("turned"), s("silu"), s("hid")
                self.down, self.y_a, self.y_v = s("down"), s("y_a"), s("y_v")
                self.scattered = s("scattered")
                self.weights = [sem(f"spill{l}_weights{s}") for s in range(3)]

        main = Main
        spill = [Spill(l) for l in range(2)]
        main_slots = []

        def plan_experts(l):
            for s in range(RING, 3 * SETS):
                slot_free[s] = (rv if l == 0 else av).end()
            main_slots.append((list(slot_count), list(slot_free)))
            done = (l + 1) * E
            for s in range(3 * SETS):
                slot_count[s] += 16 * (E // SETS)
                slot_free[s] = (main.down if s % 3 == 2 else main.gu, done)

        plan_shared(0)
        plan_experts(0)
        n = 0
        for q in range(6):
            plan("attn", f"qkv{q}", n % RING, [(slot3(n % RING), w_split(I["attn_w_qkv"][0], 256 * q, 256))],
                 ap.at("q", 2 * q + 1) if q < 4 else ap.at("k") if q == 4 else ap.at("v"))
            n += 1
        for q in range(4):
            plan("attn", f"ao{q}", n % RING, [(slot3(n % RING), w_nat(I["attn_w_o"][0], 256 * q, 256))],
                 ap.at("o", 3 * q + 2))
            n += 1
        plan_shared(1)
        plan_experts(1)

        A = [view(2176 * i, KC, T) for i in range(10)]
        hT, cum = A[0], A[0]
        xx, kkn, zT = A[1], A[1], A[1]
        xm = [A[2], A[3]]
        rT, kT, vT, wT, aT, gT = A[4], A[5], A[6], A[7], A[8], A[9]
        PEX, PIN, PMX = A[2], A[7], A[3]
        bT, bonus, yT = A[8], A[3], A[1]
        btile = view(0, KC, P)
        ktile = view(1024, KC, P)
        tokB, tokK = view(2 * 2176, KC, P), view(2 * 2176 + 1024, KC, P)
        tokV, tokZ = view(7 * 2176, KC, P), view(7 * 2176 + 1024, KC, P)
        W12 = view(21760, HEADS, 2 * HD)
        UX = 21760 + 2048
        X, XT, X2, X2T, OFF, TT, AK, BB, BK = (view(UX + 512 * i, 4, P) for i in range(9))
        GZ = view(UX + 9 * 512, 4, HD)
        S = view(UX + 9 * 512 + 256, KC, P)
        SP = view(UX + 9 * 512 + 1280, KC, P)
        M = view(UX + 9 * 512 + 2304, KC, P)
        assert UX + 9 * 512 + 2304 + 1024 <= 32300
        x0 = view(UX, NT, D)
        facc = view(2 * 2176, NT, D)
        prow = view(UX + 3072, P, rows=56)
        onehot = view(UX + 3200, 2, BIASLEN, rows=BUCKETS + 1)
        relt = view(UX + 3200 + 2 * BIASLEN, HEADS, rows=BUCKETS + 1)
        brow = view(UX + 3200 + 2 * BIASLEN + 16, 2, BIASLEN, rows=HEADS)
        thid = view(UX, T, rows=LORA)
        ahid = view(UX + 272, T, rows=LORA)
        ghid = view(UX + 544, 2, T)
        tmp = [view(UX + 1088 + 272 * i, T) for i in range(2)]
        par = small[:, 0:56]
        omk = small[:, 56:64]
        mu = small[:, 64:112].rearrange("p (m k) -> p m k", m=6)
        pc = small[:, 112:112 + KC * NCH].rearrange("p (c n) -> p c n", c=KC)
        stat = small[:, 184:184 + 36].rearrange("p (t s) -> p t s", t=NT)
        mv = small[:, 220:226].rearrange("p (t s) -> p t s", t=NT)
        std = small[:, 226:229]
        rstd = small[:, 229:232]
        (PW0, PA0, PKK, PKA, PRK, PLG, PLB) = range(7)

        relt_hidden = relt[BUCKETS:BUCKETS + 1, :]
        MIXBUF = {0: 0, 2: 1, 3: 0, 1: 1, 4: 0, 5: 1}

        def tmpN(c):
            return A[2][:, c, :]

        def unit(arr, g, rows):
            return arr[rows].rearrange("p (a i r) m -> p a r i m", a=2, r=2)[:, g // 2, g % 2]

        def tpos(row, cols):
            return (row, cols.start)

        def param(i, c):
            return par[:, 8 * i + c:8 * i + c + 1]

        block = ctx.enter_context(nc.Block())

        def psum_of(steps, name, u=0):
            return ps[:, steps.index(name, u) % 8, :]

        def bank_free(eng, steps, evac, name, u=0):
            i = steps.index(name, u) - 8
            if i < 0:
                return
            for nm, first in steps.first.items():
                if first <= i < first + steps.units[nm]:
                    eng.wait_ge(*evac(nm, i - first))

        def r_evac(nm, u):
            base = nm.split("_")[0].rstrip("0123456789") if nm.startswith("tr") else nm.split("_")[0]
            if base == "ba":
                return rv.at(nm.replace("ba", "off"), u)
            if nm in rv.first and (nm not in ra.first):
                return rv.at(nm, u)
            if nm in ("r", "k", "v", "wh", "w", "ah", "a", "gh", "g", "n2") or base == "tr":
                return ra.at(nm, u)
            if nm == "bon":
                return rv.at("bonus", u)
            if nm == "mean":
                return rv.at("ym", u)
            if nm == "var":
                return ra.at("std", u)
            if nm == "o":
                return rv.at("res", u)
            return ra.at(nm, u)

        def m_evac(l):
            def f(nm, u):
                if nm == "lg":
                    return moe_act[l].at("sc", u)
                if nm == "sg":
                    return moe_dve[l].at("sm", u % 2)
                return moe_dve[l].at(nm, min(u, moe_dve[l].units[nm] - 1)) if nm != "pos" else \
                    (moe_dve[l].at("pos", u) if u < 3 else moe_dve[l].at("max"))
            return f

        def a_evac(nm, u):
            if nm in ("q", "k", "v", "oT"):
                return aa.at(nm, u)
            if nm.startswith("sc"):
                return aa.at("ex" + nm[2:], u)
            if nm == "o":
                return av.at("res", u)
            if nm.startswith("pv"):
                return av.at(nm)
            return av.at(nm, u)

        def phase_start(eng, *ends):
            for e in ends:
                eng.wait_ge(*e)

        def heads_of(g):
            return [4 * g + i for i in range(4)]

        def unit_heads(g):
            return [8 * (g // 2) + 2 * i + g % 2 for i in range(4)]

        def hrows(head):
            return slice(HD * (head % 2), HD * (head % 2) + HD)

        scaled_count = nc.gpsimd.alloc_register("scaled_count")
        copied_count, hidden_count, x_copied_count = (nc.tensor.alloc_register(n) for n in
                                                      ("copied_count", "hidden_count", "x_copied_count"))
        scattered_count = nc.sync.alloc_register("scattered_count")

        mhT = view(0, KC, T)
        macc = view(2176, NT, D)
        ysc = [view(5248 + 1024 * b, D, rows=SLOTS) for b in range(4)]
        xs = view(9344, 4 * P)
        xgT = view(9856, KC, SLOTS)
        guc = view(10368, 2 * P)
        silu = view(10624, 2, SLOTS)
        hidT = [view(10752 + 128 * b, 2, SLOTS) for b in range(2)]
        hot = [view(11008 + 384 * b, NT, 2 * SLOTS) for b in range(2)]
        sidx = [view(11776 + b, 1, rows=SLOTS, dt=I32) for b in range(8)]
        gate_s = [view(11784 + b, 1) for b in range(8)]
        iota_s = view(12928, 2 * SLOTS)
        more_slots = view(20000, 3 * SETS - RING, SLOT)
        values = view(13056, NT, E * 2)
        posm = view(13648, NT, E)
        score = view(13840, NT, E)
        choice = view(14032, NT, E)
        top2 = view(14224, NT, GROUPS * 8)
        gsc = view(14416, NT, GROUPS)
        cmp1 = view(14440, GROUPS, GROUPS)
        cmp2 = view(14504, GROUPS, GROUPS)
        grank = view(14568, NT, GROUPS)
        keep = view(14592, NT, GROUPS)
        masked = view(14616, NT, E)
        top8 = view(14808, NT, 8)
        taken = view(14832, NT, E)
        sel = view(15024, NT, E)
        gsum = view(15216, NT)
        grec = view(15220, NT)
        krank = view(15224, NT, E)
        tokid = view(15416, NT)
        tie = view(15420, GROUPS, GROUPS)
        rowok = view(15484, NT)
        most = view(15488, 1)
        mosti_of = [most_tokens[:, l:l + 1] for l in range(2)]
        shid = view(15492, 2, T)
        shm = view(16036, 2, T)
        gate = view(16580, NT, E)
        rt = [view(17000 + 8192 * 0, TOPK, D), view(5248, TOPK, D)]

        tie2i = view(16772, 2 * SLOTS + NT, dt=I32)
        dest8 = view(16904, NT)
        rowbad = view(16908, NT)

        ahT = view(0, KC, T)
        qT = view(2176, KC, T)
        kdT = view(4352, KV, T)
        vcT = view(5440, 2, T)
        vtok = view(5984, NT, KV * HD)
        hank = [view(6752, HEADS, NK[0]), view(8800, HEADS, NK[1]), view(12896, HEADS, NK[2])]
        prob = view(17248, 4, T)
        probT = view(18336, NT, 4, P)
        otok = view(19872, NT, D)
        oT = view(22944, KC, T)
        aacc = view(25120, NT, D)
        borow = view(28192, D)
        bqkv = view(29216, 14)
        sinks = view(29232, HEADS)
        bq8 = view(29248, 8)
        negm, dens, dens2, esink, esin = (view(29256 + 4 * i, 4) for i in range(5))

        bV, bX, bU, bG, bR, bY = 0, 1, 2, 3, 4, (5, 6)

        def num(e, times=1, add=0, per=1):
            i, k = e
            v = times * (k // per) + add
            return v if isinstance(i, int) else i * (UNROLL * times // per) + v

        def wait(eng, s, value):
            if not isinstance(value, int) or value > 0:
                eng.wait_ge(s, value)

        def plus(e, k):
            return (e[0], e[1] + k)

        def column(array, e, width=1):
            at = num(e, width)
            return array[:, :, at:at + width] if isinstance(at, int) else array[:, :, bass.ds(at, width)]

        def e_slots(e):
            s0 = 3 * (0, 2, 3, 1)[e[1] % SETS]
            return s0, s0 + 1, s0 + 2

        def slot_of(s):
            return ring[:, s, :] if s < RING else more_slots[:, s - RING, :]

        def expert_weights(l, at):
            def one(w):
                return w[l][at:at + 1, :, :] if isinstance(at, int) else w[l][bass.ds(at, 1), :, :]
            return (one(I["moe_w_gate"]).rearrange("a (p k) n -> p (a k n)", k=KC),
                    one(I["moe_w_up"]).rearrange("a (p k) n -> p (a k n)", k=KC),
                    one(I["moe_w_down"]).rearrange("a (j p) n -> p (a j) n", p=P))

        def slot_view(s):
            return slot_of(s).rearrange("p (j n) -> p j n", j=2) if s % 3 == 2 else slot_of(s)

        def mm_pick(dst, hot, vals):
            for t, (_, n) in enumerate(TILES):
                mm = nc.tensor.matmul(dst[:, 0:2], hot[0:n, t, :], vals[0:n, t, :], start=(t == 0),
                                      stop=(t == NT - 1))
            return mm

        def mm_x(dst, hot):
            for t, (_, n) in enumerate(TILES):
                hv = h[0:n, t, :].rearrange("p (m k) -> p k m", k=KC)
                for half in range(2):
                    mm = nc.tensor.matmul(dst[SLOTS * half:SLOTS * half + SLOTS, :], hot[0:n, t, 0:SLOTS],
                                          hv[:, 4 * half:4 * half + 4, :], start=(t == 0), stop=(t == NT - 1))
            return mm

        def mm_turn_x(dst):
            for j in range(4):
                mm = nc.tensor.transpose(dst[:, P * j:P * j + P], xs[:, P * j:P * j + P], ident[:, :])
            return mm

        def copy_xt():
            return nc.vector.tensor_copy(xgT.rearrange("p (r j) m -> p j r m", r=2),
                                         ps[:, bU, :].rearrange("p (j r m) -> p j r m", j=4, r=2))

        def mm_gate_up(dst, s):
            for k in range(KC):
                for j in range(2):
                    mm = nc.tensor.matmul(dst[SLOTS * j:SLOTS * j + SLOTS, 0:FF], xgT[:, k, :],
                                          slot_of(s + j)[:, FF * k:FF * k + FF], start=(k == 0), stop=(k == KC - 1))
            return mm

        def mm_turn(dst):
            for j in range(2):
                mm = nc.tensor.transpose(dst[:, P * j:P * j + P], guc[:, P * j:P * j + P], ident[:, :])
            return mm

        def turned_part(which):
            return ps[:, bR, 0:2 * P].rearrange("p (j m) -> p j m", j=2)[:, :, SLOTS * which:SLOTS * which + SLOTS]

        def mm_down(dst, s, hid):
            for j in range(2):
                for half in range(2):
                    mm = nc.tensor.matmul(dst[SLOTS * half:SLOTS * half + SLOTS, :], hid[:, j, :],
                                          slot_of(s)[:, D * j + 512 * half:D * j + 512 * half + 512],
                                          start=(j == 0), stop=(j == 1))
            return mm

        def mark_slots(hot, pos, first_slot):
            return nc.vector.scalar_tensor_tensor(
                out=hot, in0=iota_s.unsqueeze(1).to_broadcast([P, NT, 2 * SLOTS]), scalar=float(first_slot),
                in1=pos.to_broadcast([P, NT, 2 * SLOTS]), op0=ALU.add, op1=ALU.is_equal)

        def take_index(picked, s, gate_of):
            nc.vector.tensor_scalar(s, picked[0:SLOTS, 0:1], OUT_OF_RANGE, None, ALU.add)
            return nc.vector.tensor_copy(gate_of, picked[:, 1:2])

        def scatter(l, src, index):
            return nc.gpsimd.indirect_dma_start(
                out=routed[l], out_offset=bass.IndirectOffsetOnAxis(ap=index, axis=0), in_=src, in_offset=None,
                bounds_check=T * TOPK - 1, oob_is_err=False)

        def sp_expert(sp, L, l, e):
            slots = e_slots(e)
            first = isinstance(e[0], int) and e[1] < SETS
            for j, (s, src) in enumerate(zip(slots, expert_weights(l, num(e)))):
                if first:
                    if L.entry_free[s]:
                        sp.wait_ge(*L.entry_free[s])
                elif j == 0:
                    sp.wait_ge(L.gu, num(plus(e, -SETS), 1, L.base + 1))
                elif j == 2:
                    sp.wait_ge(L.down, num(plus(e, -SETS), 1, L.base + 1))
                sp.dma_start(slot_view(s), src).then_inc(slot_loaded[s], 16)

        def pe_x(pe, L, e):
            pe.wait_ge(L.onehot, num(e, 1, L.base + 1))
            wait(pe, L.x_copied, num(e, 1, L.base))
            wait(pe, L.index, num(e, 1, L.base))
            mm_x(ps[:, bX, :], hot[e[1] % 2]).then_inc(L.x, 1)
            mm_pick(ps[:, bV, :], hot[e[1] % 2], column(values, e, 2)).then_inc(L.values, 1)

        def pe_turn_x(pe, L, l, e):
            copied = num(e, 1, L.base + 1)
            if not isinstance(copied, int):
                pe.reg_add(x_copied_count, x_copied_count, 1)
                copied = x_copied_count
            pe.wait_ge(*moe_dve[l].at("zero"))
            pe.wait_ge(L.x_copied, copied)
            mm_turn_x(ps[:, bU, :]).then_inc(L.xt, 1)

        def pe_expert(pe, L, l, e, this=True):
            after, two_after, prev = ahead(e, 1), ahead(e, 2), e_before(e)
            if this:
                s0, s1, _ = e_slots(e)
                pe.wait_ge(L.xt_copied, num(e, 1, L.base + 1))
                pe.wait_ge(slot_loaded[s0], num(e, 16, L.slot_base[s0] + 16, per=SETS))
                pe.wait_ge(slot_loaded[s1], num(e, 16, L.slot_base[s1] + 16, per=SETS))
                wait(pe, L.gu_copied, num(e, 1, L.base))
                mm_gate_up(ps[:, bG, :], s0).then_inc(L.gu, 1)
            if this and after:
                pe_turn_x(pe, L, l, plus(e, 1))
            if this and two_after:
                pe_x(pe, L, plus(e, 2))
            if this:
                copied, hidden = num(e, 1, L.base + 1), num(e, 1, L.base)
                if not isinstance(copied, int):
                    pe.reg_add(copied_count, copied_count, 1)
                    pe.reg_add(hidden_count, hidden_count, 1)
                    copied, hidden = copied_count, hidden_count
                pe.wait_ge(*moe_dve[l].at("zero"))
                pe.wait_ge(L.gu_copied, copied)
                wait(pe, L.hid, hidden)
                mm_turn(ps[:, bR, :]).then_inc(L.turned, 1)
            if prev:
                q = plus(e, -1)
                s2 = e_slots(q)[2]
                pe.wait_ge(L.hid, num(q, 1, L.base + 1))
                pe.wait_ge(slot_loaded[s2], num(q, 16, L.slot_base[s2] + 16, per=SETS))
                wait(pe, L.y_a, num(q, 1, L.base - 1))
                wait(pe, L.y_v, num(q, 1, L.base - 1))
                mm_down(ps[:, bY[q[1] % 2], :], s2, hidT[q[1] % 2]).then_inc(L.down, 1)

        def act_copy_x(act, L, e):
            act.wait_ge(L.x, num(e, 1, L.base + 1))
            wait(act, L.xt, num(e, 1, L.base))
            nc.scalar.copy(xs, ps[:, bX, :]).then_inc(L.x_copied, 1)

        def act_expert(act, L, e, this=True):
            two_after, prev = ahead(e, 2), e_before(e)
            if this:
                act.wait_ge(L.gu, num(e, 1, L.base + 1))
                wait(act, L.turned, num(e, 1, L.base))
                nc.scalar.copy(guc, ps[:, bG, 0:FF]).then_inc(L.gu_copied, 1)
            if this and two_after:
                act_copy_x(act, L, plus(e, 2))
            if this:
                act.wait_ge(L.turned, num(e, 1, L.base + 1))
                wait(act, L.hid, num(e, 1, L.base))
                nc.scalar.activation(silu, turned_part(0), ACT.Silu).then_inc(L.silu, 1)
            if prev:
                q = plus(e, -1)
                act.wait_ge(L.down, num(q, 1, L.base + 1))
                act.wait_ge(L.index, num(q, 1, L.base + 1))
                wait(act, L.scattered[q[1] % 4], num(q, 16, 4 * L.base, per=4))
                nc.scalar.activation(ysc[q[1] % 4][:, 512:1024], ps[SLOTS:P, bY[q[1] % 2], :], ACT.Copy,
                                     scale=gate_s[q[1] % 8][SLOTS:P]).then_inc(L.y_a, 1)

        def dve_mark(dve, L, e):
            wait(dve, L.values, num(e, 1, L.base - 1))
            mark_slots(hot[e[1] % 2], column(posm, e), 0).then_inc(L.onehot, 1)

        def dve_index(dve, L, e):
            k = e[1] % 8
            dve.wait_ge(L.values, num(e, 1, L.base + 1))
            wait(dve, L.scattered[e[1] % 4], num(e, 16, 4 * L.base - 16, per=4))
            take_index(ps[:, bV, :], sidx[k], gate_s[k]).then_inc(L.index, 1)

        def dve_copy_xt(dve, L, e):
            dve.wait_ge(L.xt, num(e, 1, L.base + 1))
            wait(dve, L.gu, num(e, 1, L.base))
            copy_xt().then_inc(L.xt_copied, 1)

        def dve_expert(dve, L, e, this=True):
            if this and ahead(e, 3):
                dve_mark(dve, L, plus(e, 3))
            if this and ahead(e, 1):
                dve_copy_xt(dve, L, plus(e, 1))
            if this and ahead(e, 2):
                dve_index(dve, L, plus(e, 2))
            prev = e_before(e)
            if this:
                dve.wait_ge(L.silu, num(e, 1, L.base + 1))
                wait(dve, L.down, num(e, 1, L.base - 1))
                nc.vector.tensor_tensor(hidT[e[1] % 2], silu, turned_part(1), ALU.mult).then_inc(L.hid, 1)
            if prev:
                q = plus(e, -1)
                dve.wait_ge(L.down, num(q, 1, L.base + 1))
                dve.wait_ge(L.index, num(q, 1, L.base + 1))
                wait(dve, L.scattered[q[1] % 4], num(q, 16, 4 * L.base, per=4))
                nc.vector.tensor_scalar(ysc[q[1] % 4][:, 0:512], ps[0:SLOTS, bY[q[1] % 2], :],
                                        gate_s[q[1] % 8][0:SLOTS], None, ALU.mult).then_inc(L.y_v, 1)

        def pool_scatter(pool, L, l, e):
            scaled = num(e, 1, L.base + 1)
            if not isinstance(scaled, int):
                pool.reg_add(scaled_count, scaled_count, 1)
                scaled = scaled_count
            pool.wait_ge(*moe_dve[l].at("zero"))
            pool.wait_ge(L.y_a, scaled)
            pool.wait_ge(L.y_v, scaled)
            scatter(l, ysc[e[1] % 4], sidx[e[1] % 8]).then_inc(L.scattered[e[1] % 4], 16)

        def over_experts(eng, body):
            for k in range(HEAD):
                body((0, k))
            with eng.Fori(0, (E - HEAD - TAIL) // UNROLL) as i:
                for j in range(UNROLL):
                    body((i, HEAD + j))
            for k in range(E - TAIL, E):
                body((0, k))

        def ahead(e, k):
            return not isinstance(e[0], int) or e[1] + k < E

        def e_before(e):
            return not isinstance(e[0], int) or e[1] >= 1

        def sp_experts(sp, L, l):
            over_experts(sp, lambda e: sp_expert(sp, L, l, e))

        def pe_experts(pe, L, l):
            pe.reg_mov(copied_count, num((0, HEAD - 1), 1, L.base + 1))
            pe.reg_mov(hidden_count, num((0, HEAD - 1), 1, L.base))
            pe.reg_mov(x_copied_count, num((0, HEAD), 1, L.base + 1))
            pe_x(pe, L, (0, 0))
            pe_turn_x(pe, L, l, (0, 0))
            pe_x(pe, L, (0, 1))
            over_experts(pe, lambda e: pe_expert(pe, L, l, e))
            pe_expert(pe, L, l, (0, E), this=False)

        def act_experts(act, L):
            act_copy_x(act, L, (0, 0))
            act_copy_x(act, L, (0, 1))
            over_experts(act, lambda e: act_expert(act, L, e))
            act_expert(act, L, (0, E), this=False)

        def dve_experts(dve, L):
            dve_mark(dve, L, (0, 0))
            dve_mark(dve, L, (0, 1))
            dve_index(dve, L, (0, 0))
            dve_copy_xt(dve, L, (0, 0))
            dve_mark(dve, L, (0, 2))
            dve_index(dve, L, (0, 1))
            over_experts(dve, lambda e: dve_expert(dve, L, e))
            dve_expert(dve, L, (0, E), this=False)

        def pool_experts(pool, L, l):
            pool.reg_mov(scaled_count, num((0, HEAD - 2), 1, L.base + 1))
            over_experts(pool, lambda e: pool_scatter(pool, L, l, plus(e, -1)) if e_before(e) else None)
            pool_scatter(pool, L, l, (0, E - 1))

        def all_scattered(eng, l):
            for s in main.scattered:
                eng.wait_ge(s, 4 * E * (l + 1))

        SPILLS = range(SLOTS, T, SLOTS)

        def run_spill(eng, l, body, counted=None):
            X = spill[l]
            eng.wait_ge(*moe_dve[l].at("maxi"))
            count = eng.value_load(mosti_of[l][0:1, 0:1], min_val=0, max_val=T)
            for p, first_slot in enumerate(SPILLS):
                with eng.If(count > first_slot):
                    with eng.Fori(0, E) as e:
                        n = e + p * E
                        body(X, e, n, first_slot)
                        if counted is not None:
                            eng.reg_add(counted, counted, 16)
                            eng.wait_ge(*moe_dve[l].at("zero"))
                        eng.wait_ge(X.scattered, n * 16 + 16 if counted is None else counted)

        def sp_spill(sp, l):
            sp.wait_ge(main.down, E * (l + 1))

            def body(X, e, n, first_slot):
                for s, src in zip(range(3), expert_weights(l, e)):
                    sp.dma_start(slot_view(s), src).then_inc(X.weights[s], 16)
            sp.reg_mov(scattered_count, 0)
            run_spill(sp, l, body, scattered_count)

        def pe_spill(pe, l):
            def body(X, e, n, first_slot):
                pe.wait_ge(X.onehot, n + 1)
                mm_x(ps[:, bX, :], hot[0]).then_inc(X.x, 1)
                mm_pick(ps[:, bV, :], hot[0], values[:, :, bass.ds(e * 2, 2)]).then_inc(X.values, 1)
                pe.reg_add(copied_count, copied_count, 1)
                pe.wait_ge(*moe_dve[l].at("zero"))
                pe.wait_ge(X.x_copied, copied_count)
                mm_turn_x(ps[:, bU, :]).then_inc(X.xt, 1)
                pe.wait_ge(X.xt_copied, n + 1)
                pe.wait_ge(X.weights[0], n * 16 + 16)
                pe.wait_ge(X.weights[1], n * 16 + 16)
                mm_gate_up(ps[:, bG, :], 0).then_inc(X.gu, 1)
                pe.wait_ge(*moe_dve[l].at("zero"))
                pe.wait_ge(X.gu_copied, copied_count)
                mm_turn(ps[:, bR, :]).then_inc(X.turned, 1)
                pe.wait_ge(X.hid, n + 1)
                pe.wait_ge(X.weights[2], n * 16 + 16)
                mm_down(ps[:, bY[0], :], 2, hidT[0]).then_inc(X.down, 1)
            pe.reg_mov(copied_count, 0)
            run_spill(pe, l, body)

        def act_spill(act, l):
            def body(X, e, n, first_slot):
                act.wait_ge(X.x, n + 1)
                nc.scalar.copy(xs, ps[:, bX, :]).then_inc(X.x_copied, 1)
                act.wait_ge(X.gu, n + 1)
                nc.scalar.copy(guc, ps[:, bG, 0:FF]).then_inc(X.gu_copied, 1)
                act.wait_ge(X.turned, n + 1)
                nc.scalar.activation(silu, turned_part(0), ACT.Silu).then_inc(X.silu, 1)
                act.wait_ge(X.down, n + 1)
                act.wait_ge(X.index, n + 1)
                nc.scalar.activation(ysc[0][:, 512:1024], ps[SLOTS:P, bY[0], :], ACT.Copy, scale=gate_s[0][SLOTS:P])\
                    .then_inc(X.y_a, 1)
            run_spill(act, l, body)

        def dve_spill(dve, l):
            def body(X, e, n, first_slot):
                mark_slots(hot[0], posm[:, :, bass.ds(e, 1)], first_slot).then_inc(X.onehot, 1)
                dve.wait_ge(X.values, n + 1)
                take_index(ps[:, bV, :], sidx[0], gate_s[0]).then_inc(X.index, 1)
                dve.wait_ge(X.xt, n + 1)
                copy_xt().then_inc(X.xt_copied, 1)
                dve.wait_ge(X.silu, n + 1)
                nc.vector.tensor_tensor(hidT[0], silu, turned_part(1), ALU.mult).then_inc(X.hid, 1)
                dve.wait_ge(X.down, n + 1)
                dve.wait_ge(X.index, n + 1)
                nc.vector.tensor_scalar(ysc[0][:, 0:512], ps[0:SLOTS, bY[0], :], gate_s[0][0:SLOTS], None, ALU.mult)\
                    .then_inc(X.y_v, 1)
            all_scattered(dve, l)
            run_spill(dve, l, body)

        def pool_spill(pool, l):
            def body(X, e, n, first_slot):
                pool.reg_add(scaled_count, scaled_count, 1)
                pool.wait_ge(*moe_dve[l].at("zero"))
                pool.wait_ge(X.y_a, scaled_count)
                pool.wait_ge(X.y_v, scaled_count)
                scatter(l, ysc[0], sidx[0]).then_inc(X.scattered, 16)
            pool.reg_mov(scaled_count, 0)
            run_spill(pool, l, body)

        def set_main(l):
            main.base = l * E
            main.slot_base, main.entry_free = main_slots[l]

        @block.sync
        def _(sp):
            def static(group):
                for slot, pieces, free in fills[group]:
                    if free:
                        sp.wait_ge(*free)
                    for dst, src in pieces:
                        sp.dma_start(dst, src).then_inc(slot_loaded[slot], 16)

            sp.dma_start(x0[0:META, 0, :], I["meta"]).then_inc(x_loaded, 16)
            sp.dma_start(x0[META:P, 0, :], I["x"][0, 0:P - META, :]).then_inc(x_loaded, 16)
            sp.dma_start(x0[:, 1, :], I["x"][0, P - META:2 * P - META, :]).then_inc(x_loaded, 16)
            sp.dma_start(x0[0:16, 2, :], I["x"][0, 2 * P - META:SEQ, :]).then_inc(x_loaded, 16)
            static("rwkv")
            for l in range(2):
                static(f"moe{l}")
                set_main(l)
                sp_experts(sp, main, l)
                sp_spill(sp, l)
                if l == 0:
                    static("attn")

        @block.gpsimd
        def _(pool):
            nc.gpsimd.memset(ident[:, :], 0.0).then_inc(*consts.step("ones", 0))
            for m in (up16, up32, up32d, low16, lowoff, before, allones, headones):
                last = nc.gpsimd.memset(m[:, :], 1.0)
            last.then_inc(*consts.step("ones", 1))
            nc.gpsimd.memset(anti[:, :], 0.0)
            nc.gpsimd.memset(notfirst[:, :], 1.0)
            nc.gpsimd.memset(eps[:, 0:1], LN_EPS)
            nc.gpsimd.memset(eps[:, 1:2], GN_EPS).then_inc(*consts.step("ones", 2))
            pool.wait_ge(*consts.at("ones"))
            made = sem("mask_step")
            count = [0]

            def select(m, blk, op, base, cm, pattern, fill=0.0):
                v = m if blk is None else m.rearrange("p (b n) -> p b n", n=blk)
                nc.gpsimd.affine_select(out=v, in_=v, compare_op=op, fill=fill, base=base, pattern=pattern,
                                        channel_multiplier=cm).then_inc(made, 1)
                count[0] += 1
                pool.wait_ge(made, count[0])

            def same_block(m, blk):
                nb = P // blk
                select(m[:, :], blk, ALU.is_ge, 0, 1, [[-blk, nb], [0, blk]])
                select(m[:, :], blk, ALU.is_ge, blk - 1, -1, [[blk, nb], [0, blk]])

            select(ident[:, :], None, ALU.not_equal, 0, 1, [[-1, P]], 1.0)
            select(anti[:, :], None, ALU.not_equal, -(P - 1), 1, [[1, P]], 1.0)
            same_block(headones, HD)
            for m, op, blk in ((up16, ALU.is_gt, HALF), (up32, ALU.is_gt, CHUNK), (up32d, ALU.is_ge, CHUNK)):
                select(m[:, :], None, op, 0, -1, [[1, P]])
                same_block(m, blk)
            select(before[:, :], None, ALU.is_gt, 0, -1, [[1, P]])
            select(low16[:, :], None, ALU.is_gt, 0, 1, [[-1, P]])
            same_block(low16, HALF)
            same_block(lowoff, CHUNK)
            select(lowoff[:, :], HALF, ALU.is_ge, -HALF, 1, [[-HALF, P // HALF], [0, HALF]])
            select(notfirst[:, 0:256], CHUNK, ALU.is_gt, 0, 0, [[0, 256 // CHUNK], [1, CHUNK]])
            select(notfirst[:, 256:T], None, ALU.is_gt, 0, 0, [[1, T - 256]])
            pool.nop().then_inc(*consts.step("made"))

            def row(src):
                return src.rearrange("(a n) -> a n", a=1).to_broadcast([P, src.shape[0]])

            vecs = (I["rwkv_w0"][0], I["rwkv_a0"][0], I["rwkv_k_k"][0], I["rwkv_k_a"][0],
                    I["rwkv_r_k"][0].rearrange("h n -> (h n)"), I["rwkv_lnx_g"][0], I["rwkv_lnx_b"][0])
            for i, v in enumerate(vecs):
                pool.dma_start(prow[8 * i:8 * i + 8, :], v.rearrange("(c p) -> c p", p=P)).then_inc(params_loaded, 16)
            pool.dma_start(mu, I["rwkv_mu"][0].rearrange("m (p k) -> p m k", k=KC)).then_inc(params_loaded, 16)
            pool.dma_start(onehot, I["t5"]).then_inc(params_loaded, 16)
            pool.dma_start(relt[0:BUCKETS, :], I["rel_bias"]).then_inc(params_loaded, 16)
            for l in range(2):
                pool.dma_start(router[:, l], I["moe_router"][l].rearrange("(p k) n -> p k n", k=KC))\
                    .then_inc(params_loaded, 16)
                pool.dma_start(rbias[:, l, :], row(I["moe_bias"][l])).then_inc(params_loaded, 16)

            def load_ln(g, b):
                pool.dma_start(lnrow[:, 0, :], row(g)).then_inc(ln_loaded, 16)
                pool.dma_start(lnrow[:, 1, :], row(b)).then_inc(ln_loaded, 16)

            load_ln(I["ln_mix_g"][0], I["ln_mix_b"][0])
            pool.wait_ge(*rv.at("bias"))
            pool.dma_start(biasd, brow).then_inc(bias_stored, 16)
            pool.dma_start(h[0:META, 0, :], I["meta"]).then_inc(h_loaded, 16)
            pool.dma_start(h[META:P, 0, :], I["x"][0, 0:P - META, :]).then_inc(h_loaded, 16)
            pool.dma_start(h[:, 1, :], I["x"][0, P - META:2 * P - META, :]).then_inc(h_loaded, 16)
            pool.dma_start(h[0:16, 2, :], I["x"][0, 2 * P - META:SEQ, :]).then_inc(h_loaded, 16)

            for l in range(2):
                before_dve = rv if l == 0 else av
                pool.wait_ge(*before_dve.end())
                load_ln(I["ln_ffn_g"][l], I["ln_ffn_b"][l])
                nc.gpsimd.iota(tie2i[:, 0:2 * SLOTS], [[0, 2], [1, SLOTS]], base=0, channel_multiplier=0)\
                    .then_inc(made, 1)
                nc.gpsimd.iota(tie2i[:, 2 * SLOTS:2 * SLOTS + NT], [[P, NT]], base=0, channel_multiplier=1).then_inc(made, 1)
                count[0] += 2
                pool.wait_ge(made, count[0])
                nc.gpsimd.tensor_copy(iota_s, tie2i[:, 0:2 * SLOTS]).then_inc(made, 1)
                nc.gpsimd.tensor_copy(tokid, tie2i[:, 2 * SLOTS:2 * SLOTS + NT]).then_inc(made, 1)
                nc.gpsimd.memset(rowok, 1.0).then_inc(made, 1)
                nc.gpsimd.memset(tie, 1.0).then_inc(made, 1)
                count[0] += 4
                pool.wait_ge(made, count[0])
                select(rowok[:, 2:3], None, ALU.is_gt, 16, -1, [[0, 1]])
                nc.gpsimd.affine_select(out=tie, in_=tie, compare_op=ALU.is_gt, fill=0.0, base=0,
                                        pattern=[[1, GROUPS], [-1, GROUPS]], channel_multiplier=0)\
                    .then_inc(route_consts, 1)
                set_main(l)
                pool_experts(pool, main, l)
                pool_spill(pool, l)
                all_scattered(pool, l)
                rv3 = routed[l].rearrange("(t k) d -> t k d", k=TOPK)
                for t, (r0, n) in enumerate(TILES):
                    if t == 2:
                        pool.wait_ge(*end_dve[l].at("sum", 7))
                    pool.dma_start(rt[t % 2][0:n], rv3[r0:r0 + n]).then_inc(routed_loaded[t], 16)
                if l == 0:
                    pool.wait_ge(*end_dve[0].end())
                    load_ln(I["ln_mix_g"][1], I["ln_mix_b"][1])
                    pool.dma_start(bqkv[:, 0:8], I["attn_b_qkv"][0, 0:HEADS * HD].rearrange("(c p) -> p c", p=P),
                                   allow_slow_non_contiguous=True).then_inc(attn_loaded, 16)
                    bk = I["attn_b_qkv"][0, HEADS * HD:(HEADS + KV) * HD].rearrange("(g p) -> p g", p=HD)
                    for r in range(2):
                        pool.dma_start(bqkv[HD * r:HD * r + HD, 8:12], bk,
                                       allow_slow_non_contiguous=True).then_inc(attn_loaded, 16)
                    pool.dma_start(bqkv[:, 12:14], I["attn_b_qkv"][0, (HEADS + KV) * HD:QKV]
                                   .rearrange("(c p) -> p c", p=P), allow_slow_non_contiguous=True)\
                        .then_inc(attn_loaded, 16)
                    pool.dma_start(sinks, row(I["attn_sinks"][0])).then_inc(attn_loaded, 16)
                    pool.dma_start(borow, row(I["attn_b_o"][0])).then_inc(attn_loaded, 16)
            pool.wait_ge(*end_dve[1].end())
            o = out[0]
            pool.dma_start(o[0:P - META, :], h[META:P, 0, :]).then_inc(out_stored, 16)
            pool.dma_start(o[P - META:2 * P - META, :], h[:, 1, :]).then_inc(out_stored, 16)
            pool.dma_start(o[2 * P - META:SEQ, :], h[0:16, 2, :]).then_inc(out_stored, 16)
            pool.wait_ge(out_stored, 48)

        @block.tensor
        def _(pe):
            mm_ = nc.tensor.matmul

            def need(name):
                s, v, slot = landed[name]
                pe.wait_ge(s, v)
                return slot

            def start(steps, evac, name, u=0):
                bank_free(pe, steps, evac, name, u)
                return psum_of(steps, name, u)

            def R(name, u=0):
                return start(rp, r_evac, name, u)

            pe.wait_ge(*consts.at("made"))
            pe.wait_ge(params_loaded, 16 * 14)
            b = R("par")
            nc.tensor.transpose(b[:, 0:56], prow[0:56, :], ident[0:56, 0:56]).then_inc(*rp.step("par"))
            pe.wait_ge(x_loaded, 64)
            for k in range(KC):
                b = R("xT", k)
                for t, (r0, n) in enumerate(TILES):
                    xv = x0[0:n, t, :].rearrange("p (m k) -> p k m", k=KC)
                    m = nc.tensor.transpose(b[:, r0:r0 + n], xv[:, k, :], ident[0:n, 0:n])
                m.then_inc(*rp.step("xT", k))
            pe.wait_ge(hidden_row, 1)
            for j in range(4):
                b = R("bias", j)
                mm_(b[0:HEADS, 0:T], relt[:, :], onehot[:, j // 2, T * (j % 2):T * (j % 2) + T], start=True,
                    stop=True).then_inc(*rp.step("bias", j))

            def proj(name, mix):
                pe.wait_ge(*rv.at(f"mix{mix}"))
                for c in range(C8):
                    s = need(f"{name}{c // 2}")
                    b = R(name, c)
                    for k in range(KC):
                        m = mm_(b[:, 0:T], slot3(s)[:, k, P * (c % 2):P * (c % 2) + P], xm[MIXBUF[mix]][:, k, :],
                                start=(k == 0), stop=(k == KC - 1))
                    m.then_inc(*rp.step(name, c))

            proj("r", 0)
            proj("k", 2)
            proj("v", 3)
            for nm, mix, wn, dst in (("w", 1, LORA, thid), ("a", 4, LORA, ahid)):
                pe.wait_ge(*rv.at(f"mix{mix}"))
                s = need(nm)
                b = R(nm + "h")
                for k in range(KC):
                    m = mm_(b[0:LORA, 0:T], ring[:, s, LORA * k:LORA * k + LORA], xm[MIXBUF[mix]][:, k, :],
                            start=(k == 0), stop=(k == KC - 1))
                m.then_inc(*rp.step(nm + "h"))
                pe.wait_ge(*ra.at(nm + "h"))
                for c in range(C8):
                    b = R(nm, c)
                    mm_(b[:, 0:T], ring[0:LORA, s, 512 + P * c:512 + P * c + P], dst, start=True,
                        stop=True).then_inc(*rp.step(nm, c))
            pe.wait_ge(*rv.at("mix5"))
            s = need("g1")
            for j, (m0, mn) in enumerate(((0, P), (P, GLORA - P))):
                b = R("gh", j)
                for k in range(KC):
                    m = mm_(b[0:mn, 0:T], ring[:, s, GLORA * k + m0:GLORA * k + m0 + mn], xm[MIXBUF[5]][:, k, :],
                            start=(k == 0), stop=(k == KC - 1))
                m.then_inc(*rp.step("gh", j))
            pe.wait_ge(*ra.at("gh"))
            s = need("g2")
            for c in range(C8):
                b = R("g", c)
                mm_(b[:, 0:T], ring[:, s, P * c:P * c + P], ghid[:, 0, :], start=True, stop=False)
                mm_(b[:, 0:T], ring[0:GLORA - P, s, D + P * c:D + P * c + P], ghid[0:GLORA - P, 1, :],
                    start=False, stop=True).then_inc(*rp.step("g", c))
            for c in range(C8):
                pe.wait_ge(*ra.at("sq", c))
                b = R("n2", c)
                mm_(b[:, 0:T], headones[:, :], tmpN(c), start=True, stop=True).then_inc(*rp.step("n2", c))
            for c in range(C8):
                pe.wait_ge(*rv.at("rk", c))
                b = R("bon", c)
                mm_(b[:, 0:T], headones[:, :], A[0][:, c, :], start=True, stop=True).then_inc(*rp.step("bon", c))

            for t, (r0, n) in enumerate(TILES):
                cols = slice(r0, r0 + n)
                for j, (src, w) in enumerate(((btile, "bt"), (ktile, "kt"), (vT, None), (zT, None))):
                    if w:
                        pe.wait_ge(*rv.at(f"{w}{t}"))
                    for half in range(2):
                        u = 2 * j + half
                        b = R(f"tr{t}", u)
                        for i in range(4):
                            c = 4 * half + i
                            a_in = src[:, c, 0:n] if w else src[:, c, cols]
                            m = nc.tensor.transpose(b[0:n, P * i:P * i + P], a_in, ident[:, :])
                        m.then_inc(*rp.step(f"tr{t}", u))
                for g in range(UNITS):
                    N = lambda x: f"{x}_{g}_{t}"

                    def four(name, f, after=()):
                        for w in after:
                            pe.wait_ge(*w)
                        b = R(N(name))
                        for i, hd in enumerate(unit_heads(g)):
                            m = f(i, hd, b[0:n, P * i:P * i + n])
                        m.then_inc(*rp.step(N(name)))

                    def ch(arr, hd):
                        return arr[hrows(hd), hd // 2, cols]

                    four("ab", lambda i, hd, o: mm_(o, ch(bT, hd), ch(zT, hd), start=True, stop=True),
                         [rv.at("s0")])
                    four("ba", lambda i, hd, o: mm_(o, ch(zT, hd), ch(bT, hd), start=True, stop=True))
                    four("ak", lambda i, hd, o: mm_(o, ch(kT, hd), ch(zT, hd), start=True, stop=True))
                    four("bb", lambda i, hd, o: mm_(o, ch(bT, hd), ch(rT, hd), start=True, stop=True))
                    four("bk", lambda i, hd, o: mm_(o, ch(kT, hd), ch(rT, hd), start=True, stop=True))

                    def sq(lhs, rhs):
                        return lambda i, hd, o: mm_(o, lhs[0:n, i, 0:n], rhs[0:n, i, 0:n], start=True, stop=True)

                    four("x2", sq(XT, X), [rv.at(N("ba"))])
                    four("x2t", sq(X, XT))
                    four("tt2", sq(X2, TT), [ra.at(N("x2")), rv.at(N("tt1"))])
                    four("x4", sq(X2T, X2), [ra.at(N("x2t"))])
                    four("x4t", sq(X2, X2T))
                    four("tt3", sq(X, TT), [ra.at(N("x4")), rv.at(N("tt2"))])
                    four("x8", sq(XT, X), [ra.at(N("x4t"))])
                    four("tt4", sq(X2, TT), [ra.at(N("x8")), rv.at(N("tt3"))])
                    four("td", lambda i, hd, o: nc.tensor.transpose(o, TT[0:n, i, 0:n], ident[0:n, 0:n]),
                         [rv.at(N("tt4"))])
                    four("f", sq(OFF, TT), [rv.at(N("off"))])
                    four("tt5", sq(X, X2T), [ra.at(N("td")), ra.at(N("f"))])
                    pe.wait_ge(*rv.at(N("ak")))
                    pe.wait_ge(*ra.at(f"tr{t}"))
                    b = R(N("g1"))
                    for i, hd in enumerate(unit_heads(g)):
                        m = mm_(b[0:n, HD * i:HD * i + HD], AK[0:n, i, 0:n], tokV[0:n, hd // 2, hrows(hd)],
                                start=True, stop=True)
                    m.then_inc(*rp.step(N("g1")))
                    pe.wait_ge(*ra.at(N("g1")))
                    pe.wait_ge(*rv.at(N("tt5")))
                    b = R(N("w12"))
                    for i, hd in enumerate(unit_heads(g)):
                        mm_(b[0:n, P * i:P * i + HD], TT[0:n, i, 0:n], tokZ[0:n, hd // 2, hrows(hd)],
                            start=True, stop=True)
                        m = mm_(b[0:n, P * i + HD:P * i + P], TT[0:n, i, 0:n], GZ[0:n, i, :], start=True, stop=True)
                    m.then_inc(*rp.step(N("w12")))
                    pe.wait_ge(*ra.at(N("w12")))
                    pe.wait_ge(*rv.at(N("bk")))
                    b = R(N("q1"))
                    for i, hd in enumerate(unit_heads(g)):
                        m = mm_(b[hrows(hd), P * i:P * i + n], W12[0:n, hd, 0:HD], BB[0:n, i, 0:n],
                                start=True, stop=True)
                    m.then_inc(*rp.step(N("q1")))
                    b = R(N("q2"))
                    for i, hd in enumerate(unit_heads(g)):
                        o = b[hrows(hd), P * i:P * i + n]
                        mm_(o, W12[0:n, hd, HD:P], BB[0:n, i, 0:n], start=True, stop=False)
                        m = mm_(o, tokV[0:n, hd // 2, hrows(hd)], BK[0:n, i, 0:n], start=False, stop=True)
                    m.then_inc(*rp.step(N("q2")))
                for c in chunk_ids(t):
                    last = c == NCH - 1
                    q0 = CHUNK * (c % 4)
                    qn = min(CHUNK, T - CHUNK * c)
                    rows = slice(q0, q0 + qn)
                    tp = None
                    if not last:
                        for half in range(2):
                            b = R(f"m_{c}_{t}", half)
                            for i in range(4):
                                pr = 4 * half + i
                                for hd in (2 * pr, 2 * pr + 1):
                                    hr = hrows(hd)
                                    m = mm_(b[hr, P * i + hr.start:P * i + hr.stop], W12[rows, hd, 0:HD],
                                            tokB[rows, pr, hr], start=True, stop=True, tile_position=tpos(q0, hr))
                            m.then_inc(*rp.step(f"m_{c}_{t}", half))
                    if c > 0:
                        pe.wait_ge(*rv.at(f"s_{c - 1}_{(c - 1) // 4}"))
                    pe.wait_ge(*rv.at(f"q1_{UNITS - 1}_{t}"))
                    b = R(f"y_{c}_{t}")
                    for pr in range(PAIRS):
                        m = mm_(b[:, CHUNK * pr:CHUNK * pr + qn], S[:, pr, :], rT[:, pr, CHUNK * c:CHUNK * c + qn],
                                start=True, stop=True)
                    m.then_inc(*rp.step(f"y_{c}_{t}"))
                    if not last:
                        pe.wait_ge(*ra.at(f"m_{c}_{t}"))
                        for half in range(2):
                            b = R(f"s_{c}_{t}", half)
                            for i in range(4):
                                pr = 4 * half + i
                                mm_(b[:, P * i:P * i + P], M[:, pr, :], S[:, pr, :], start=True, stop=True)
                                for hd in (2 * pr, 2 * pr + 1):
                                    hr = hrows(hd)
                                    o = b[hr, P * i + hr.start:P * i + hr.stop]
                                    mm_(o, tokB[rows, pr, hr], W12[rows, hd, HD:P], start=False, stop=True,
                                        tile_position=tpos(q0, hr), skip_group_check=True)
                                    m = mm_(o, tokK[rows, pr, hr], tokV[rows, pr, hr], start=False, stop=True,
                                            tile_position=tpos(q0, hr), skip_group_check=True)
                            m.then_inc(*rp.step(f"s_{c}_{t}", half))
            for c in range(C8):
                pe.wait_ge(*rv.at(f"y_{NCH - 1}_{NT - 1}"))
                b = R("mean", c)
                mm_(b[:, 0:T], headones[:, :], yT[:, c, :], start=True, stop=True).then_inc(*rp.step("mean", c))
            for c in range(C8):
                pe.wait_ge(*ra.at("ysq", c))
                b = R("var", c)
                mm_(b[:, 0:T], headones[:, :], A[0][:, c, :], start=True, stop=True).then_inc(*rp.step("var", c))
            pe.wait_ge(*rv.at("yo"))
            for q in range(4):
                s = need(f"o{q}")
                for t, (r0, n) in enumerate(TILES):
                    b = R("o", 3 * q + t)
                    for c in range(C8):
                        m = mm_(b[0:n, 0:256], yT[:, c, r0:r0 + n], slot3(s)[:, c, :], start=(c == 0),
                                stop=(c == C8 - 1))
                    m.then_inc(*rp.step("o", 3 * q + t))

            def moe(l, prev_dve):
                st, ev = moe_pe[l], m_evac(l)
                pe.wait_ge(*prev_dve.end())
                for k in range(KC):
                    b = start(st, ev, "hT", k)
                    for t, (r0, n) in enumerate(TILES):
                        hv = h[0:n, t, :].rearrange("p (m k) -> p k m", k=KC)
                        m = nc.tensor.transpose(b[:, r0:r0 + n], hv[:, k, :], ident[0:n, 0:n])
                    m.then_inc(*st.step("hT", k))
                pe.wait_ge(*moe_dve[l].at("hT"))
                for t, (r0, n) in enumerate(TILES):
                    b = start(st, ev, "lg", t)
                    for k in range(KC):
                        m = mm_(b[0:n, 0:E], mhT[:, k, r0:r0 + n], router[:, l, k, :], start=(k == 0),
                                stop=(k == KC - 1))
                    m.then_inc(*st.step("lg", t))
                for u in range(4):
                    s = need(f"sh{u // 2}_{l}")
                    b = start(st, ev, "sg", u)
                    for k in range(KC):
                        w = ring[:, s, FF * k:FF * k + FF].rearrange("p (m j) -> p j m", j=2)
                        m = mm_(b[:, 0:T], w[:, u % 2, :], mhT[:, k, :], start=(k == 0), stop=(k == KC - 1))
                    m.then_inc(*st.step("sg", u))
                pe.wait_ge(*moe_dve[l].at("sel"))
                for t in range(NT + 1):
                    b = start(st, ev, "pos", t)
                    for t2 in range(min(t + 1, NT)):
                        m = mm_(b[:, 0:E], (before if t2 == t else allones)[:, :], sel[:, t2, :],
                                start=(t2 == 0), stop=(t2 == min(t, NT - 1)))
                    m.then_inc(*st.step("pos", t))
                s = need(f"sh2_{l}")
                pe.wait_ge(*moe_dve[l].at("sm"))
                for u in range(6):
                    r0, n = TILES[u // 2]
                    b = start(st, ev, "sd", u)
                    for j in range(2):
                        m = mm_(b[0:n, :], shm[:, j, r0:r0 + n], ring[:, s, D * j + 512 * (u % 2):][:, 0:512],
                                start=(j == 0), stop=(j == 1))
                    m.then_inc(*st.step("sd", u))
                pe.wait_ge(*moe_dve[l].end())
                pe.wait_ge(*moe_act[l].end())
                set_main(l)
                pe_experts(pe, main, l)
                pe_spill(pe, l)

            moe(0, rv)

            pe.wait_ge(*end_dve[0].end())

            def G(name, u=0):
                return start(ap, a_evac, name, u)

            for k in range(KC):
                b = G("hT", k)
                for t, (r0, n) in enumerate(TILES):
                    hv = h[0:n, t, :].rearrange("p (m k) -> p k m", k=KC)
                    m = nc.tensor.transpose(b[:, r0:r0 + n], hv[:, k, :], ident[0:n, 0:n])
                m.then_inc(*ap.step("hT", k))
            pe.wait_ge(*av.at("hT"))
            for c in range(8):
                s = need(f"qkv{c // 2}")
                b = G("q", c)
                for k in range(KC):
                    m = mm_(b[:, 0:T], slot3(s)[:, k, P * (c % 2):P * (c % 2) + P], ahT[:, k, :], start=(k == 0),
                            stop=(k == KC - 1))
                m.then_inc(*ap.step("q", c))
            for g in range(KV):
                s = need("qkv4")
                b = G("k", g)
                for r in range(2):
                    for k in range(KC):
                        m = mm_(b[HD * r:HD * r + HD, 0:T], slot3(s)[:, k, HD * g:HD * g + HD], ahT[:, k, :],
                                start=(k == 0), stop=(k == KC - 1))
                m.then_inc(*ap.step("k", g))
            for c in range(2):
                s = need("qkv5")
                b = G("v", c)
                for k in range(KC):
                    m = mm_(b[:, 0:T], slot3(s)[:, k, P * c:P * c + P], ahT[:, k, :], start=(k == 0),
                            stop=(k == KC - 1))
                m.then_inc(*ap.step("v", c))
            pe.wait_ge(*aa.at("v"))
            for t, (r0, n) in enumerate(TILES):
                b = G("vt", t)
                for c in range(2):
                    m = nc.tensor.transpose(b[0:n, P * c:P * c + P], vcT[:, c, r0:r0 + n], ident[:, :])
                m.then_inc(*ap.step("vt", t))
            pe.wait_ge(bias_loaded, 16 * 6)
            pe.wait_ge(*av.at("vt"))
            for t, (r0, n) in enumerate(TILES):
                nk = NK[t]
                for g in range(KV):
                    for i, hd in enumerate(heads_of(g)):
                        b = G(f"sc{t}_{g}", i)
                        mm_(b[0:n, 0:nk], qT[hrows(hd), hd // 2, r0:r0 + n], kdT[hrows(hd), g, 0:nk], start=True,
                            stop=False)
                        mm_(b[0:n, 0:nk], anti[0:n, P - n:P], hank[t][0:n, hd, 0:nk], start=False,
                            stop=True).then_inc(*ap.step(f"sc{t}_{g}", i))
                    pe.wait_ge(*aa.at(f"ex{t}_{g}", 3))
                    for j in range(t + 1):
                        kj = TILES[j][1]
                        b = G(f"pt{t}_{g}", j)
                        for i in range(4):
                            m = nc.tensor.transpose(b[0:kj, n * i:n * i + n], prob[0:n, i, P * j:P * j + kj],
                                                    ident[0:n, 0:n])
                        m.then_inc(*ap.step(f"pt{t}_{g}", j))
                    pe.wait_ge(*av.at(f"pt{t}_{g}"))
                    b = G(f"pv{t}_{g}")
                    for i in range(4):
                        for j in range(t + 1):
                            kj = TILES[j][1]
                            m = mm_(b[0:n, HD * i:HD * i + HD], probT[0:kj, j, i, 0:n],
                                    vtok[0:kj, j, HD * g:HD * g + HD], start=(j == 0), stop=(j == t))
                    m.then_inc(*ap.step(f"pv{t}_{g}"))
            pe.wait_ge(*av.at(f"pv{NT - 1}_{KV - 1}"))
            for c in range(8):
                b = G("oT", c)
                for t, (r0, n) in enumerate(TILES):
                    m = nc.tensor.transpose(b[:, r0:r0 + n], otok[0:n, t, P * c:P * c + P], ident[0:n, 0:n])
                m.then_inc(*ap.step("oT", c))
            pe.wait_ge(*aa.at("oT"))
            for q in range(4):
                s = need(f"ao{q}")
                for t, (r0, n) in enumerate(TILES):
                    b = G("o", 3 * q + t)
                    for c in range(C8):
                        m = mm_(b[0:n, 0:256], oT[:, c, r0:r0 + n], slot3(s)[:, c, :], start=(c == 0),
                                stop=(c == C8 - 1))
                    m.then_inc(*ap.step("o", 3 * q + t))
            moe(1, av)

        @block.scalar
        def _(act):
            A_ = nc.scalar.activation

            def got(name, u=0, st=rp):
                act.wait_ge(*st.at(name, u))
                return psum_of(st, name, u)

            act.wait_ge(*rv.at("omk"))
            act.wait_ge(*consts.at("ones"))
            for nm, dst in (("r", rT), ("k", kT), ("v", vT)):
                for c in range(C8):
                    nc.scalar.copy(dst[:, c, :], got(nm, c)[:, 0:T]).then_inc(*ra.step(nm, c))
            act.wait_ge(*rp.at("bias"))
            A_(thid, got("wh")[0:LORA, 0:T], ACT.Tanh).then_inc(*ra.step("wh"))
            for c in range(C8):
                A_(wT[:, c, :], got("w", c)[:, 0:T], ACT.Sigmoid, bias=param(PW0, c)).then_inc(*ra.step("w", c))
            nc.scalar.copy(ahid, got("ah")[0:LORA, 0:T]).then_inc(*ra.step("ah"))
            for c in range(C8):
                A_(aT[:, c, :], got("a", c)[:, 0:T], ACT.Sigmoid, bias=param(PA0, c)).then_inc(*ra.step("a", c))
            A_(ghid[:, 0, :], got("gh", 0)[:, 0:T], ACT.Sigmoid).then_inc(*ra.step("gh", 0))
            A_(ghid[0:GLORA - P, 1, :], got("gh", 1)[0:GLORA - P, 0:T], ACT.Sigmoid).then_inc(*ra.step("gh", 1))
            for c in range(C8):
                nc.scalar.copy(gT[:, c, :], got("g", c)[:, 0:T]).then_inc(*ra.step("g", c))
            for c in range(C8):
                act.wait_ge(*rv.at("kk0", c))
                A_(tmpN(c), kkn[:, c, :], ACT.Square).then_inc(*ra.step("sq", c))
            for c in range(C8):
                b = got("n2", c)
                A_(tmpN(c), b[:, 0:T], ACT.Sqrt).then_inc(*ra.step("n2", c))
            for c in range(C8):
                act.wait_ge(*rv.at("cumx", c))
                A_(PMX[:, c, :], PMX[:, c, :], ACT.Exp, scale=-EXP_HALF).then_inc(*ra.step("pm", c))
            for c in range(C8):
                A_(PIN[:, c, :], cum[:, c, :], ACT.Exp, scale=EXP_HALF).then_inc(*ra.step("pi", c))
            act.wait_ge(*rv.at("kk"))
            for c in range(C8):
                A_(PEX[:, c, :], cum[:, c, :], ACT.Exp, scale=-EXP_HALF).then_inc(*ra.step("pp", c))
            for t, (r0, n) in enumerate(TILES):
                cols = slice(r0, r0 + n)
                if t == 0:
                    act.wait_ge(*rv.at("s0"))
                for j, dst in enumerate((tokB, tokK, tokV, tokZ)):
                    for half in range(2):
                        u = 2 * j + half
                        b = got(f"tr{t}", u)
                        nc.scalar.copy(dst[0:n, 4 * half:4 * half + 4, :],
                                       b[0:n, :].rearrange("p (i m) -> p i m", i=4)).then_inc(*ra.step(f"tr{t}", u))
                for g in range(UNITS):
                    def cp(name, dst, after=None):
                        nm = f"{name}_{g}_{t}"
                        b = got(nm)
                        if after:
                            act.wait_ge(*rp.at(f"{after}_{g}_{t}"))
                        nc.scalar.copy(dst[0:n, :, 0:n], b[0:n, :].rearrange("p (i m) -> p i m", i=4)[:, :, 0:n])\
                            .then_inc(*ra.step(nm))
                    cp("x2", X2)
                    cp("x2t", X2T)
                    cp("x4", X, "x2t")
                    cp("x4t", XT)
                    cp("x8", X2, "x4t")
                    cp("td", X, "x8")
                    cp("f", X2T)
                    nm = f"g1_{g}_{t}"
                    b = got(nm)
                    nc.scalar.copy(GZ[0:n], b[0:n, 0:4 * HD].rearrange("p (i m) -> p i m", i=4))\
                        .then_inc(*ra.step(nm))
                    nm = f"w12_{g}_{t}"
                    b = got(nm)
                    nc.scalar.copy(unit(W12, g, slice(0, n)), b[0:n, :].rearrange("p (i m) -> p i m", i=4))\
                        .then_inc(*ra.step(nm))
                    nm = f"q2_{g}_{t}"
                    b = got(nm)
                    hr, prs = hrows(g), slice(4 * (g // 2), 4 * (g // 2) + 4)
                    nc.scalar.copy(bT[hr, prs, cols], b[hr, :].rearrange("p (i m) -> p i m", i=4)[:, :, 0:n])\
                        .then_inc(*ra.step(nm))
                for c in chunk_ids(t):
                    if c == NCH - 1:
                        continue
                    if c > 0:
                        act.wait_ge(*rp.at(f"s_{c - 1}_{(c - 1) // 4}"))
                    for half in range(2):
                        b = got(f"m_{c}_{t}", half)
                        for r in range(2):
                            hr = slice(HD * r, HD * r + HD)
                            m = nc.scalar.copy(M[hr, 4 * half:4 * half + 4, hr],
                                               b[hr, :].rearrange("p (i m) -> p i m", i=4)[:, :, hr])
                        m.then_inc(*ra.step(f"m_{c}_{t}", half))
            for c in range(C8):
                act.wait_ge(*rv.at("ym", c))
                A_(A[0][:, c, :], yT[:, c, :], ACT.Square).then_inc(*ra.step("ysq", c))
            for c in range(C8):
                b = got("var", c)
                A_(A[0][:, c, :], b[:, 0:T], ACT.Sqrt, bias=eps[:, 1:2], scale=1.0 / HD).then_inc(*ra.step("std", c))

            def ln(sa, sv):
                act.wait_ge(*sv.at("ln", 2))
                A_(std, mv[:, :, 1], ACT.Sqrt, bias=eps[:, 0:1]).then_inc(*sa.step("ln"))

            ln(ra, rv)

            def moe(l, prev_dve):
                sa = moe_act[l]
                act.wait_ge(*prev_dve.end())
                act.wait_ge(*moe_dve[l].at("zero"))
                for t, (r0, n) in enumerate(TILES):
                    b = got("lg", t, moe_pe[l])
                    A_(score[0:n, t, :], b[0:n, 0:E], ACT.Sigmoid).then_inc(*sa.step("sc", t))
                for j in range(2):
                    b = got("sg", j, moe_pe[l])
                    A_(shid[:, j, :], b[:, 0:T], ACT.Silu).then_inc(*sa.step("sg", j))
                act.wait_ge(*moe_dve[l].end())
                set_main(l)
                act_experts(act, main)
                act_spill(act, l)
                ln(end_act[l], end_dve[l])

            moe(0, rv)
            act.wait_ge(*end_dve[0].end())
            act.wait_ge(bias_stored, 16)
            for t, (r0, n) in enumerate(TILES):
                off = T - (r0 + n)
                nk = NK[t]
                act.dma_start(hank[t][0:n, :, META:nk],
                              bass.AP(biasd.tensor, off + META, [[1, n], [2 * BIASLEN, HEADS], [1, nk - META]]))\
                    .then_inc(bias_loaded, 16)
                act.dma_start(hank[t][0:n, :, 0:META],
                              bass.AP(biasd.tensor, BIASLEN + off, [[1, n], [2 * BIASLEN, HEADS], [1, META]]))\
                    .then_inc(bias_loaded, 16)
            act.wait_ge(attn_loaded, 16 * 6)
            act.wait_ge(*av.at("sink"))
            for c in range(8):
                A_(qT[:, c, :], got("q", c, ap)[:, 0:T], ACT.Identity, bias=bq8[:, c:c + 1], scale=0.125)\
                    .then_inc(*aa.step("q", c))
            for g in range(KV):
                A_(kdT[:, g, :], got("k", g, ap)[:, 0:T], ACT.Identity, bias=bqkv[:, 8 + g:9 + g])\
                    .then_inc(*aa.step("k", g))
            for c in range(2):
                A_(vcT[:, c, :], got("v", c, ap)[:, 0:T], ACT.Identity, bias=bqkv[:, 12 + c:13 + c])\
                    .then_inc(*aa.step("v", c))
            for t, (r0, n) in enumerate(TILES):
                nk = NK[t]
                for g in range(KV):
                    act.wait_ge(*av.at(f"mx{t}_{g}", 3))
                    if (t, g) != (0, 0):
                        pt, pg = (t, g - 1) if g else (t - 1, KV - 1)
                        act.wait_ge(*ap.at(f"pt{pt}_{pg}"))
                    for i in range(4):
                        A_(prob[0:n, i, 0:nk], psum_of(ap, f"sc{t}_{g}", i)[0:n, 0:nk], ACT.Exp,
                           bias=negm[0:n, i:i + 1], accum_out=dens[0:n, i:i + 1]).then_inc(*aa.step(f"ex{t}_{g}", i))
                    A_(esink[0:n, :], esin[0:n, :], ACT.Exp).then_inc(*aa.step(f"ex{t}_{g}", 4))
            for c in range(8):
                nc.scalar.copy(oT[:, c, :], got("oT", c, ap)[:, 0:T]).then_inc(*aa.step("oT", c))
            ln(aa, av)
            moe(1, av)

        @block.vector
        def _(dve):
            V = nc.vector

            def got(name, u=0, st=rp):
                dve.wait_ge(*st.at(name, u))
                return psum_of(st, name, u)

            V.memset(relt_hidden, HIDDEN).then_inc(hidden_row, 1)
            V.tensor_copy(par, got("par")[:, 0:56]).then_inc(*rv.step("par"))
            dve.wait_ge(*rv.at("par"))
            V.tensor_scalar(omk, par[:, 8 * PKA:8 * PKA + 8], -1.0, 1.0, ALU.mult, ALU.add).then_inc(*rv.step("omk"))
            for k in range(KC):
                V.tensor_copy(hT[:, k, :], got("xT", k)[:, 0:T]).then_inc(*rv.step("xT", k))
            for j in range(4):
                V.tensor_copy(brow[:, j // 2, T * (j % 2):T * (j % 2) + T], got("bias", j)[0:HEADS, 0:T])\
                    .then_inc(*rv.step("bias", j))
            dve.wait_ge(*rv.at("xT"))
            V.tensor_tensor(xx[:, :, 1:T], hT[:, :, 0:T - 1], hT[:, :, 1:T], ALU.subtract).then_inc(*rv.step("xx", 0))
            V.tensor_scalar(xx[:, :, 0:1], hT[:, :, 0:1], -1.0, None, ALU.mult).then_inc(*rv.step("xx", 1))
            dve.wait_ge(*rv.at("xx"))
            prior = {3: "r", 1: "k", 4: "v", 5: "wh"}
            for m in (0, 2, 3, 1, 4, 5):
                if m in prior:
                    dve.wait_ge(*rp.at(prior[m]))
                for k in range(KC):
                    V.scalar_tensor_tensor(out=xm[MIXBUF[m]][:, k, :], in0=xx[:, k, :], scalar=mu[:, m, k:k + 1],
                                           in1=hT[:, k, :], op0=ALU.mult, op1=ALU.add).then_inc(*rv.step(f"mix{m}", k))
            dve.wait_ge(*rv.at("mix5"))
            dve.wait_ge(*ra.at("k"))
            for c in range(C8):
                V.tensor_scalar(kkn[:, c, :], kT[:, c, :], param(PKK, c), None, ALU.mult).then_inc(*rv.step("kk0", c))
            for c in range(C8):
                dve.wait_ge(*ra.at("w", c))
                V.tensor_tensor_scan(cum[:, c, :], notfirst[:, :], wT[:, c, :], 0.0, ALU.mult, ALU.add)\
                    .then_inc(*rv.step("cum", c))
            dve.wait_ge(*rp.at("gh"))
            for c in range(C8):
                dve.wait_ge(*rv.at("cum", c))
                V.tensor_tensor(PMX[:, c, :], cum[:, c, :], wT[:, c, :], ALU.subtract).then_inc(*rv.step("cumx", c))
            for c in range(C8):
                dve.wait_ge(*ra.at("n2", c))
                V.tensor_scalar(tmpN(c), tmpN(c), 1e-12, None, ALU.max).then_inc(rn_step, 1)
                dve.wait_ge(rn_step, c + 1)
                V.reciprocal(tmpN(c), tmpN(c)).then_inc(*rv.step("rn", c))
            for c in range(C8):
                dve.wait_ge(*rv.at("rn", c))
                V.tensor_tensor(kkn[:, c, :], kkn[:, c, :], tmpN(c), ALU.mult).then_inc(*rv.step("kk", c))
            dve.wait_ge(*ra.at("pp"))
            dve.wait_ge(*ra.at("g"))
            for c in range(C8):
                V.tensor_scalar(A[0][:, c, :], aT[:, c, :], param(PKA, c), omk[:, c:c + 1], ALU.mult, ALU.add)\
                    .then_inc(*rv.step("k2t", c))
            for c in range(C8):
                dve.wait_ge(*rv.at("k2t", c))
                V.tensor_tensor(kT[:, c, :], kT[:, c, :], A[0][:, c, :], ALU.mult).then_inc(*rv.step("k2", c))
            for c in range(C8):
                V.tensor_tensor(bT[:, c, :], kkn[:, c, :], aT[:, c, :], ALU.mult).then_inc(*rv.step("b", c))
            for c in range(C8):
                dve.wait_ge(*rv.at("k2", c))
                V.scalar_tensor_tensor(out=A[0][:, c, :], in0=rT[:, c, :], scalar=param(PRK, c), in1=kT[:, c, :],
                                       op0=ALU.mult, op1=ALU.mult).then_inc(*rv.step("rk", c))
            for c in range(C8):
                dve.wait_ge(*rv.at("b", c))
                V.scalar_tensor_tensor(out=zT[:, c, :], in0=kkn[:, c, :], scalar=-1.0, in1=PMX[:, c, :],
                                       op0=ALU.mult, op1=ALU.mult).then_inc(*rv.step("z", c))
            for c in range(C8):
                dve.wait_ge(*rv.at("z", c))
                V.tensor_tensor(bonus[:, c, :], got("bon", c)[:, 0:T], vT[:, c, :], ALU.mult)\
                    .then_inc(*rv.step("bonus", c))
            V.tensor_copy(pc[:, :, 0:NCH - 1],
                          PEX[:, :, 0:256].rearrange("p c (n s) -> p c n s", s=CHUNK)[:, :, :, CHUNK - 1])\
                .then_inc(*rv.step("pc", 0))
            V.tensor_copy(pc[:, :, NCH - 1:NCH], PEX[:, :, T - 1:T]).then_inc(*rv.step("pc", 1))
            for c in range(C8):
                V.tensor_tensor(bT[:, c, :], bT[:, c, :], PIN[:, c, :], ALU.mult).then_inc(*rv.step("bh", c))
            for c in range(C8):
                V.tensor_tensor(kT[:, c, :], kT[:, c, :], PIN[:, c, :], ALU.mult).then_inc(*rv.step("kh", c))
            dve.wait_ge(*rv.at("rk"))
            for c in range(C8):
                V.tensor_tensor(rT[:, c, :], rT[:, c, :], PEX[:, c, :], ALU.mult).then_inc(*rv.step("rh", c))
            dve.wait_ge(*rv.at("rh"))
            dve.wait_ge(bias_stored, 16)
            V.memset(M, 0.0)
            V.memset(S, 0.0).then_inc(*rv.step("s0"))
            dve.wait_ge(*rv.at("s0"))
            for t, (r0, n) in enumerate(TILES):
                cols = slice(r0, r0 + n)
                nch = -(-n // CHUNK)
                cs = min(CHUNK, n)
                if t:
                    dve.wait_ge(*rp.at(f"tr{t - 1}", 3))
                for nm, src, dst in (("bt", bT, btile), ("kt", kT, ktile)):
                    for c in range(C8):
                        m = V.tensor_tensor(dst[:, c, 0:n].rearrange("p (a s) -> p a s", s=cs),
                                            src[:, c, cols].rearrange("p (a s) -> p a s", s=cs),
                                            pc[:, c, 4 * t:4 * t + nch].unsqueeze(2).to_broadcast([P, nch, cs]),
                                            ALU.mult)
                    m.then_inc(*rv.step(f"{nm}{t}"))
                for g in range(UNITS):
                    N = lambda x: f"{x}_{g}_{t}"

                    def b4(name):
                        return got(N(name))[0:n, :].rearrange("p (i m) -> p i m", i=4)[:, :, 0:n]

                    def bc(mask):
                        return mask[0:n, 0:n].unsqueeze(1).to_broadcast([n, 4, n])

                    def masked_copy(name, step, dst, mask):
                        V.tensor_tensor(dst[0:n, :, 0:n], b4(name), bc(mask), ALU.mult).then_inc(*rv.step(N(step)))

                    if g or t:
                        pg, pt = (g - 1, t) if g else (UNITS - 1, t - 1)
                        dve.wait_ge(*rp.at(f"q2_{pg}_{pt}"))
                    masked_copy("ab", "ab", XT, up16)
                    dve.wait_ge(*rv.at(N("ab")))
                    V.tensor_tensor(TT[0:n, :, 0:n], XT[0:n, :, 0:n], bc(ident), ALU.add).then_inc(*rv.step(N("tt1")))
                    masked_copy("ba", "ba", X, low16)
                    masked_copy("ba", "off", OFF, lowoff)
                    masked_copy("ak", "ak", AK, up32)
                    masked_copy("bb", "bb", BB, up32d)
                    masked_copy("bk", "bk", BK, up32d)
                    for j in range(2, 6):
                        nm = f"tt{j}"
                        V.tensor_tensor(TT[0:n, :, 0:n], TT[0:n, :, 0:n], b4(nm), ALU.add).then_inc(*rv.step(N(nm)))
                    b = got(N("q1"))
                    hr, prs = hrows(g), slice(4 * (g // 2), 4 * (g // 2) + 4)
                    V.tensor_tensor(rT[hr, prs, cols], rT[hr, prs, cols],
                                    b[hr, :].rearrange("p (i m) -> p i m", i=4)[:, :, 0:n], ALU.add)\
                        .then_inc(*rv.step(N("q1")))
                for c in chunk_ids(t):
                    last = c == NCH - 1
                    qn = min(CHUNK, T - CHUNK * c)
                    cc = slice(CHUNK * c, CHUNK * c + qn)
                    if not last:
                        if c:
                            dve.wait_ge(*rv.at(f"s_{c - 1}_{(c - 1) // 4}"))
                        V.tensor_tensor(SP, S, pc[:, :, c:c + 1].to_broadcast([P, KC, P]), ALU.mult)\
                            .then_inc(*rv.step(f"sp_{c}_{t}"))
                    b = got(f"y_{c}_{t}")
                    dve.wait_ge(*ra.at(f"q2_{UNITS - 1}_{t}"))
                    V.tensor_tensor(yT[:, :, cc], bT[:, :, cc],
                                    b[:, 0:CHUNK * PAIRS].rearrange("p (c s) -> p c s", c=PAIRS)[:, :, 0:qn],
                                    ALU.add).then_inc(*rv.step(f"y_{c}_{t}"))
                    if not last:
                        dve.wait_ge(*rv.at(f"sp_{c}_{t}"))
                        dve.wait_ge(*rp.at(f"s_{c}_{t}"))
                        for half in range(2):
                            b = got(f"s_{c}_{t}", half)
                            V.tensor_tensor(S[:, 4 * half:4 * half + 4, :], SP[:, 4 * half:4 * half + 4, :],
                                            b.rearrange("p (i m) -> p i m", i=4), ALU.add)\
                                .then_inc(*rv.step(f"s_{c}_{t}", half))
            dve.wait_ge(*rv.at(f"y_{NCH - 1}_{NT - 1}"))
            dve.wait_ge(*rp.at("mean"))
            for c in range(C8):
                V.scalar_tensor_tensor(out=yT[:, c, :], in0=got("mean", c)[:, 0:T], scalar=-1.0 / HD,
                                       in1=yT[:, c, :], op0=ALU.mult, op1=ALU.add).then_inc(*rv.step("ym", c))
            for c in range(C8):
                dve.wait_ge(*ra.at("std", c))
                V.reciprocal(A[0][:, c, :], A[0][:, c, :]).then_inc(*rv.step("yr", c))
            for c in range(C8):
                dve.wait_ge(*rv.at("yr", c))
                V.tensor_tensor(yT[:, c, :], yT[:, c, :], A[0][:, c, :], ALU.mult).then_inc(*rv.step("yn", c))
            for c in range(C8):
                dve.wait_ge(*rv.at("yn", c))
                V.tensor_scalar(yT[:, c, :], yT[:, c, :], param(PLG, c), param(PLB, c), ALU.mult, ALU.add)\
                    .then_inc(*rv.step("yg", c))
            for c in range(C8):
                dve.wait_ge(*rv.at("yg", c))
                V.tensor_tensor(yT[:, c, :], yT[:, c, :], bonus[:, c, :], ALU.add).then_inc(*rv.step("yb", c))
            for c in range(C8):
                dve.wait_ge(*rv.at("yb", c))
                V.tensor_tensor(yT[:, c, :], yT[:, c, :], gT[:, c, :], ALU.mult).then_inc(*rv.step("yo", c))
            dve.wait_ge(*rv.at("yo"))
            dve.wait_ge(h_loaded, 64)

            def residual(steps, st, acc):
                for q in range(4):
                    for t, (r0, n) in enumerate(TILES):
                        b = got("o", 3 * q + t, st)
                        V.scalar_tensor_tensor(out=acc[0:n, t, 256 * q:256 * q + 256],
                                               in0=h[0:n, t, 256 * q:256 * q + 256], scalar=ALPHA,
                                               in1=b[0:n, 0:256], op0=ALU.mult, op1=ALU.add)\
                            .then_inc(*steps.step("res", 3 * q + t))

            def ln(steps, sa, acc, which):
                for t, (r0, n) in enumerate(TILES):
                    for j in range(2):
                        m = V.bn_stats(stat[0:n, t, 6 * j:6 * j + 6], acc[0:n, t, 512 * j:512 * j + 512])
                m.then_inc(*steps.step("ln", 0))
                dve.wait_ge(*steps.at("ln", 0))
                V.memset(mv, 1.0).then_inc(*steps.step("ln", 1))
                dve.wait_ge(*steps.at("ln", 1))
                for t, (r0, n) in enumerate(TILES):
                    m = V.bn_aggr(mv[0:n, t, :], stat[0:n, t, :])
                m.then_inc(*steps.step("ln", 2))
                dve.wait_ge(*sa.at("ln"))
                V.reciprocal(rstd, std).then_inc(*steps.step("ln", 3))
                dve.wait_ge(*steps.at("ln", 3))
                dve.wait_ge(ln_loaded, 32 * which)
                u = 4
                for j in range(2):
                    for t, (r0, n) in enumerate(TILES):
                        if j == 0:
                            m = V.tensor_scalar(acc[0:n, t, :], acc[0:n, t, :], mv[0:n, t, 0:1], rstd[0:n, t:t + 1],
                                                ALU.subtract, ALU.mult)
                        if j == 1:
                            m = V.tensor_tensor(acc[0:n, t, :], acc[0:n, t, :], lnrow[0:n, 0, :], ALU.mult)
                    m.then_inc(*steps.step("ln", u))
                    dve.wait_ge(*steps.at("ln", u))
                    u += 1
                for t, (r0, n) in enumerate(TILES):
                    V.tensor_tensor(h[0:n, t, :], acc[0:n, t, :], lnrow[0:n, 1, :], ALU.add)\
                        .then_inc(*steps.step("ln", u))
                    u += 1
                dve.wait_ge(*steps.at("ln"))

            residual(rv, rp, facc)
            dve.wait_ge(*rv.at("res"))
            ln(rv, ra, facc, 1)

            def moe(l):
                st = moe_dve[l]
                sp_ = moe_pe[l]

                def fin(ins, name, u=0):
                    ins.then_inc(*st.step(name, u))
                    dve.wait_ge(*st.at(name, u))

                V.memset(score, 0.0).then_inc(*st.step("zero", 0))
                V.memset(values, 0.0).then_inc(*st.step("zero", 1))
                for k in range(KC):
                    V.tensor_copy(mhT[:, k, :], got("hT", k, sp_)[:, 0:T]).then_inc(*st.step("hT", k))
                dve.wait_ge(route_consts, l + 1)
                dve.wait_ge(*moe_act[l].at("sc"))
                fin(V.tensor_tensor(choice, score, rbias[:, l, :].unsqueeze(1).to_broadcast([P, NT, E]), ALU.add),
                    "choice")
                for t in range(NT):
                    for g in range(GROUPS):
                        V.max(top2[:, t, 8 * g:8 * g + 8], choice[:, t, GE * g:GE * g + GE])\
                            .then_inc(*st.step("top2", GROUPS * t + g))
                dve.wait_ge(*st.at("top2"))
                t2 = top2.rearrange("p t (g k) -> p t g k", k=8)
                fin(V.tensor_tensor(gsc, t2[:, :, :, 0], t2[:, :, :, 1], ALU.add), "gs")
                for t in range(NT):
                    a = gsc[:, t, :].unsqueeze(1).to_broadcast([P, GROUPS, GROUPS])
                    c = gsc[:, t, :].unsqueeze(2).to_broadcast([P, GROUPS, GROUPS])
                    fin(V.tensor_tensor(cmp1, a, c, ALU.is_gt), "rank", 5 * t)
                    fin(V.tensor_tensor(cmp2, a, c, ALU.is_equal), "rank", 5 * t + 1)
                    fin(V.tensor_tensor(cmp2, cmp2, tie, ALU.mult), "rank", 5 * t + 2)
                    fin(V.tensor_tensor(cmp1, cmp1, cmp2, ALU.add), "rank", 5 * t + 3)
                    fin(V.tensor_reduce(grank[:, t, :], cmp1, AX.X, ALU.add), "rank", 5 * t + 4)
                fin(V.tensor_scalar(keep, grank, TOP_GROUPS - 0.5, None, ALU.is_lt), "keep")
                fin(V.tensor_scalar(grank, keep, -HIDDEN, HIDDEN, ALU.mult, ALU.add), "hide")
                kb = keep.rearrange("p t g -> p (t g)").unsqueeze(2).to_broadcast([P, NT * GROUPS, GE])
                hb = grank.rearrange("p t g -> p (t g)").unsqueeze(2).to_broadcast([P, NT * GROUPS, GE])
                mk = masked.rearrange("p t (g e) -> p (t g) e", e=GE)
                fin(V.tensor_tensor(mk, choice.rearrange("p t (g e) -> p (t g) e", e=GE), kb, ALU.mult), "mask", 0)
                fin(V.tensor_tensor(mk, mk, hb, ALU.add), "mask", 1)
                for t in range(NT):
                    fin(V.max(top8[:, t, :], masked[:, t, :]), "top8", 2 * t)
                    fin(V.match_replace(taken[:, t, :], top8[:, t, :], masked[:, t, :], 2 * HIDDEN), "top8", 2 * t + 1)
                fin(V.tensor_tensor(sel, taken, masked, ALU.not_equal), "sel", 0)
                fin(V.tensor_tensor(sel, sel, rowok.unsqueeze(2).to_broadcast([P, NT, E]), ALU.mult), "sel", 1)
                dve.wait_ge(*moe_act[l].at("sg"))
                for j in range(2):
                    V.tensor_tensor(shm[:, j, :], shid[:, j, :], got("sg", 2 + j, sp_)[:, 0:T], ALU.mult)\
                        .then_inc(*st.step("sm", j))
                fin(V.tensor_tensor(gate, score, sel, ALU.mult), "g0")
                fin(V.tensor_reduce(gsum, gate, AX.X, ALU.add), "gsum")
                fin(V.tensor_scalar(rowbad, rowok, -1.0, 1.0, ALU.mult, ALU.add), "grec", 0)
                fin(V.tensor_tensor(gsum, gsum, rowbad, ALU.add), "grec", 1)
                fin(V.reciprocal(grec, gsum), "g1")
                v3 = values.rearrange("p t (e c) -> p t e c", c=2)
                fin(V.scalar_tensor_tensor(out=v3[:, :, :, 1], in0=gate, scalar=SCALE,
                                           in1=grec.unsqueeze(2).to_broadcast([P, NT, E]), op0=ALU.mult,
                                           op1=ALU.mult), "g2")
                for t in range(NT):
                    fin(V.tensor_tensor_scan(krank[:, t, :], allones[:, 0:E], sel[:, t, :], 0.0, ALU.mult, ALU.add),
                        "kr", t)
                fin(V.tensor_tensor(krank, krank, sel, ALU.subtract), "kr2")
                for t in range(NT):
                    fin(V.tensor_scalar(dest8[:, t:t + 1], tokid[:, t:t + 1], float(TOPK), -OUT_OF_RANGE,
                                        ALU.mult, ALU.add), "dest", t)
                for t in range(NT):
                    V.tensor_scalar(v3[:, t, :, 0], krank[:, t, :], dest8[:, t:t + 1], None, ALU.add)\
                        .then_inc(*st.step("tok", t))
                dve.wait_ge(*st.at("tok"))
                for t in range(NT):
                    b = got("pos", t, sp_)
                    V.scalar_tensor_tensor(out=posm[:, t, :], in0=b[:, 0:E], scalar=1.0, in1=sel[:, t, :],
                                           op0=ALU.add, op1=ALU.mult).then_inc(*st.step("pos", t))
                dve.wait_ge(*st.at("pos"))
                fin(V.tensor_scalar(posm, posm, -1.0, None, ALU.add), "pos2")
                fin(V.tensor_reduce(most, got("pos", 3, sp_)[:, 0:E], AX.X, ALU.max), "max")
                fin(V.tensor_copy(mosti_of[l], most), "maxi")
                for u in range(6):
                    r0, n = TILES[u // 2]
                    cs = slice(512 * (u % 2), 512 * (u % 2) + 512)
                    V.scalar_tensor_tensor(out=macc[0:n, u // 2, cs], in0=h[0:n, u // 2, cs], scalar=ALPHA,
                                           in1=got("sd", u, sp_)[0:n, :], op0=ALU.mult, op1=ALU.add)\
                        .then_inc(*st.step("sd", u))
                dve.wait_ge(*st.at("sd"))
                set_main(l)
                dve_experts(dve, main)
                dve_spill(dve, l)
                es = end_dve[l]
                for t, (r0, n) in enumerate(TILES):
                    dve.wait_ge(routed_loaded[t], 16 * (l + 1))
                    for k in range(TOPK):
                        V.tensor_tensor(macc[0:n, t, :], macc[0:n, t, :], rt[t % 2][0:n, k, :], ALU.add)\
                            .then_inc(*es.step("sum", TOPK * t + k))
                        dve.wait_ge(*es.at("sum", TOPK * t + k))
                ln(es, end_act[l], macc, 2 + 2 * l)

            moe(0)

            dve.wait_ge(attn_loaded, 16 * 6)
            V.tensor_scalar(bq8, bqkv[:, 0:8], 0.125, None, ALU.mult).then_inc(*av.step("sink"))
            for k in range(KC):
                V.tensor_copy(ahT[:, k, :], got("hT", k, ap)[:, 0:T]).then_inc(*av.step("hT", k))
            for t, (r0, n) in enumerate(TILES):
                V.tensor_copy(vtok[0:n, t, :], got("vt", t, ap)[0:n, 0:256]).then_inc(*av.step("vt", t))
            for t, (r0, n) in enumerate(TILES):
                nk = NK[t]
                for g in range(KV):
                    nm = f"mx{t}_{g}"
                    if (t, g) != (0, 0):
                        pt, pg = (t, g - 1) if g else (t - 1, KV - 1)
                        dve.wait_ge(*aa.at(f"ex{pt}_{pg}"))
                    for i in range(4):
                        b = got(f"sc{t}_{g}", i, ap)
                        m = V.tensor_reduce(negm[0:n, i:i + 1], b[0:n, 0:nk], AX.X, ALU.max)
                    m.then_inc(*av.step(nm, 0))
                    dve.wait_ge(*av.at(nm, 0))
                    V.tensor_tensor(negm[0:n, :], negm[0:n, :], sinks[0:n, 4 * g:4 * g + 4], ALU.max)\
                        .then_inc(*av.step(nm, 1))
                    dve.wait_ge(*av.at(nm, 1))
                    V.tensor_tensor(esin[0:n, :], sinks[0:n, 4 * g:4 * g + 4], negm[0:n, :], ALU.subtract)\
                        .then_inc(*av.step(nm, 2))
                    dve.wait_ge(*av.at(nm, 2))
                    V.tensor_scalar(negm[0:n, :], negm[0:n, :], -1.0, None, ALU.mult).then_inc(*av.step(nm, 3))
                    dn = f"den{t}_{g}"
                    dve.wait_ge(*aa.at(f"ex{t}_{g}", 4))
                    V.tensor_tensor(dens2[0:n, :], dens[0:n, :], esink[0:n, :], ALU.add).then_inc(*av.step(dn, 0))
                    dve.wait_ge(*av.at(dn, 0))
                    V.reciprocal(dens2[0:n, :], dens2[0:n, :]).then_inc(*av.step(dn, 1))
                    if (t, g) != (0, 0):
                        dve.wait_ge(*ap.at(f"pv{pt}_{pg}"))
                    for j in range(t + 1):
                        kj = TILES[j][1]
                        b = got(f"pt{t}_{g}", j, ap)
                        V.tensor_copy(probT[0:kj, j, :, 0:n], b[0:kj, 0:4 * n].rearrange("p (i m) -> p i m", i=4))\
                            .then_inc(*av.step(f"pt{t}_{g}", j))
                    b = got(f"pv{t}_{g}", 0, ap)
                    dve.wait_ge(*av.at(dn, 1))
                    for i in range(4):
                        V.tensor_scalar(otok[0:n, t, HD * (4 * g + i):HD * (4 * g + i) + HD],
                                        b[0:n, HD * i:HD * i + HD], dens2[0:n, i:i + 1], None, ALU.mult)\
                            .then_inc(*av.step(f"pv{t}_{g}", i))
            residual(av, ap, aacc)
            dve.wait_ge(*av.at("res"))
            for t, (r0, n) in enumerate(TILES):
                V.tensor_tensor(aacc[0:n, t, :], aacc[0:n, t, :], borow[0:n, :], ALU.add).then_inc(*av.step("bo", t))
            dve.wait_ge(*av.at("bo"))
            ln(av, aa, aacc, 3)
            moe(1)


_INS = ['x', 'meta', 'rel_bias', 'rwkv_mu', 'rwkv_w0', 'rwkv_w1', 'rwkv_w2', 'rwkv_a0', 'rwkv_a1', 'rwkv_a2',
        'rwkv_g1', 'rwkv_g2', 'rwkv_k_k', 'rwkv_k_a', 'rwkv_r_k', 'rwkv_w_r', 'rwkv_w_k', 'rwkv_w_v', 'rwkv_w_o',
        'rwkv_lnx_g', 'rwkv_lnx_b', 'attn_w_qkv', 'attn_b_qkv', 'attn_sinks', 'attn_w_o', 'attn_b_o', 'ln_mix_g',
        'ln_mix_b', 'ln_ffn_g', 'ln_ffn_b', 'moe_router', 'moe_bias', 'moe_w_gate', 'moe_w_up', 'moe_w_down',
        'shared_w_gate', 'shared_w_up', 'shared_w_down']


def kernel(**inputs):
    import numpy as _np
    import concourse.bacc as _bacc
    from concourse import mybir as _mybir
    from concourse.bass_utils import run_bass_kernel_spmd as _run

    nc = _bacc.Bacc("TRN2", target_bir_lowering=False, num_devices=1)
    arrays, aps = {}, {}
    for name in _INS:
        arrays[f"in_{name}"] = _np.ascontiguousarray(inputs[name])
    arrays["in_t5"] = t5_one_hot()
    for name, a in arrays.items():
        aps[name[3:]] = nc.dram_tensor(name, a.shape, _mybir.dt.from_np(a.dtype), kind="ExternalInput").ap()
    out = nc.dram_tensor("out_0", (1, SEQ, D), _mybir.dt.float32, kind="ExternalOutput").ap()
    hybrid_trunk(nc, aps, out)
    r = _run(nc, [arrays], core_ids=[0])
    return r.results[0]["out_0"]
```

```python
from contextlib import ExitStack

import numpy as np

import concourse.bass as bass
from concourse import mybir

ALU = mybir.AluOpType
ACT = mybir.ActivationFunctionType
AX = mybir.AxisListType
F32 = mybir.dt.float32
I32 = mybir.dt.int32

D = 1024
SEQ = 256
META = 16
T = SEQ + META
P = 128
KC = D // P
TILES = [(0, 128), (128, 128), (256, 16)]
NT = len(TILES)
HEADS = 16
HD = 64
PAIRS = HEADS // 2
CHUNK = 32
HALF = 16
NCH = -(-T // CHUNK)
LORA = 64
GLORA = 160
GN_EPS = 64e-5
LN_EPS = 1e-5
EXP_HALF = float(np.exp(-0.5))
ALPHA = float((2 * 2) ** 0.25)
KV = 4
GROUP = HEADS // KV
WINDOW = 128
BUCKETS = 32
QKV = (HEADS + 2 * KV) * HD
E = 64
TOPK = 8
GROUPS = 8
GE = E // GROUPS
TOP_GROUPS = 4
FF = 256
SCALE = 2.5
SLOTS = 64
UNROLL = 8
HEAD = 5
TAIL = 3
LN_STEPS = 8
SETS = 4
RING = 6
SLOT = 2048
OUT_OF_RANGE = 65536.0
HIDDEN = -1.0e30
BIASLEN = 2 * T


class Steps:

    def __init__(self, sem, order):
        self.sem, self.first, self.units, n = sem, {}, dict(order), 0
        for name, units in order:
            self.first[name] = n
            n += units
        self.total, self.done = n, 0

    def index(self, name, u=0):
        assert 0 <= u < self.units[name], (name, u)
        return self.first[name] + u

    def at(self, name, u=None):
        return self.sem, self.index(name, self.units[name] - 1 if u is None else u) + 1

    def step(self, name, u=0):
        assert self.index(name, u) == self.done, (name, u, self.index(name, u), self.done)
        self.done += 1
        return self.sem, 1

    def end(self):
        return self.sem, self.total


def t5_one_hot():
    exact = BUCKETS // 2
    d = T - 1 - np.arange(BIASLEN)
    near = np.maximum(d, 1).astype(np.float32)
    ratio = np.log(near / np.float32(exact)) / np.float32(np.log(128 / exact))
    large = np.minimum(exact + (ratio * (BUCKETS - exact)).astype(np.int32), BUCKETS - 1)
    bucket = np.where(d < exact, np.maximum(d, 0), large)
    out = np.zeros((BUCKETS + 1, 2, BIASLEN), np.float32)
    for plane, hidden in enumerate(((d < 0) | (d >= WINDOW), d < 0)):
        out[np.where(hidden, BUCKETS, bucket), plane, np.arange(BIASLEN)] = 1.0
    return out


def hybrid_trunk(nc, I, out):
    with ExitStack() as ctx:
        def sb(name, shape, dt=F32):
            return ctx.enter_context(nc.sbuf_tensor(name, shape, dt))

        def sem(name):
            return ctx.enter_context(nc.semaphore(name))

        ps = ctx.enter_context(nc.psum_tensor("ps", [P, 8, 512], F32))

        ring = sb("ring", [P, RING, SLOT])
        h = sb("h", [P, NT, D])
        lnrow = sb("lnrow", [P, 2, D])
        router = sb("router", [P, 2, KC, E])
        rbias = sb("rbias", [P, 2, E])
        ident = sb("ident", [P, P])
        anti = sb("anti", [P, P])
        allones = sb("allones", [P, P])
        headones = sb("headones", [P, P])
        up16 = sb("up16", [P, P])
        up32 = sb("up32", [P, P])
        up32d = sb("up32d", [P, P])
        low16 = sb("low16", [P, P])
        lowoff = sb("lowoff", [P, P])
        before = sb("before", [P, P])
        notfirst = sb("notfirst", [P, T])
        small = sb("small", [P, 256])
        eps = sb("eps", [P, 2])
        most_tokens = sb("most_tokens", [P, 2], I32)
        arena = sb("arena", [P, 32300])

        def view(at, *shape, rows=P, dt=None):
            n = int(np.prod(shape))
            assert at + n <= 32300, (at, n)
            v = arena[0:rows, at:at + n]
            if dt is not None:
                v = v.bitcast(dt)
            if len(shape) == 2:
                v = v.rearrange("p (a b) -> p a b", a=shape[0])
            if len(shape) == 3:
                v = v.rearrange("p (a b c) -> p a b c", a=shape[0], b=shape[1])
            return v

        routed = [nc.dram_tensor(f"routed{l}", (T * TOPK, D), F32, kind="Internal").ap() for l in range(2)]
        biasd = nc.dram_tensor("biasd", (HEADS, 2, BIASLEN), F32, kind="Internal").ap()

        consts = Steps(sem("consts_ready"), [("ones", 4), ("ident", 1), ("made", 1)])
        x_loaded = sem("x_loaded")
        h_loaded = sem("h_loaded")
        params_loaded = sem("params_loaded")
        attn_loaded = sem("attn_loaded")
        ln_loaded = sem("ln_loaded")
        bias_stored = sem("bias_stored")
        bias_loaded = sem("bias_loaded")
        few_loaded = sem("few_loaded")
        routed_loaded = [[sem(f"routed_loaded{t}_{j}") for j in range(TOPK // 2)] for t in range(NT - 1)]
        out_stored = sem("out_stored")
        hidden_row = sem("hidden_row")
        rn_step = sem("rn_step")
        kh_made = sem("kh_made")
        bonus_shifted = sem("bonus_shifted")
        route_consts = sem("route_consts")
        slot_loaded = [sem(f"slot_loaded{s}") for s in range(3 * SETS)]

        def per_tile(steps):
            return [(f"{n}{t}", u) for t in range(NT) for n, u in steps(t)]

        UNITS = 4

        def chunk_ids(t):
            return range(t * 4, min(t * 4 + 4, NCH))

        def carried(t):
            return [c for c in chunk_ids(t) if c < NCH - 1]

        def one_block(t):
            return TILES[t][1] <= HALF

        UNIT_STEPS = {
            "pe": ("ab", "ba", "ak", "bb", "bk", "x2", "x2t", "tt2", "x4", "x4t", "tt3", "x8", "tt4", "td", "f",
                   "tt5", "g1", "w12", "q1", "q2"),
            "dve": ("ab", "tt1", "ba", "off", "ak", "bb", "bk", "tt2", "tt3", "tt4", "tt5", "q1"),
            "act": ("x2", "x2t", "x4", "x4t", "x8", "td", "f", "g1", "w12", "q2")}

        def rw_order(t, who):
            o = [("bt", 1), ("kt", 1)] if who == "dve" else [("tr", 8)]
            for pair in range(UNITS // 2):
                for n in UNIT_STEPS[who]:
                    if not (one_block(t) and n in ("off", "td", "f", "tt5")):
                        o += [(f"{n}_{g}_", 1) for g in (2 * pair, 2 * pair + 1)]
            live = len(carried(t))
            if live:
                o += {"pe": [("m_", live), ("kv_", live)], "act": [("m_", live)], "dve": [("kv_", live)]}[who]
            for c in chunk_ids(t):
                on = c in carried(t)
                if who == "pe":
                    o += [(f"y_{c}_", 1)] + ([(f"s_{c}_", 1)] if on else [])
                if who == "dve":
                    o += ([(f"sp_{c}_", 2)] if on else []) + [(f"y_{c}_", 1)] + ([(f"s_{c}_", 1)] if on else [])
            return o

        C8 = KC
        rp = Steps(sem("rwkv_pe"), [("par", 1), ("xT", C8), ("bias", 4), ("r", C8), ("k", C8), ("v", C8),
                                    ("wh", 1), ("w", C8), ("ah", 1), ("a", C8), ("gh", 2), ("g", C8),
                                    ("n2", C8), ("bon", C8)]
                   + per_tile(lambda t: rw_order(t, "pe"))
                   + [("mean", C8), ("var", C8), ("o", 12)])
        ra = Steps(sem("rwkv_act"), [("r", C8), ("k", C8), ("v", C8), ("wh", 1), ("w", C8), ("ah", 1),
                                     ("a", C8), ("gh", 2), ("kk0", C8), ("sq", C8), ("g", C8), ("n2", C8), ("pm", C8), ("pi", C8),
                                     ("pp", C8), ("k2t", C8)]
                   + per_tile(lambda t: rw_order(t, "act"))
                   + [("ysq", C8), ("std", C8), ("ln", 1)])
        rv = Steps(sem("rwkv_dve"), [("par", 1), ("omk", 1), ("xT", C8), ("bias", 4), ("xx", 2),
                                     ("mix0", C8), ("mix2", C8), ("mix3", C8), ("mix1", C8), ("mix4", C8),
                                     ("mix5", C8), ("cum", C8), ("cumx", C8), ("rn", C8), ("kk", C8),
                                     ("k2", C8), ("b", C8), ("rk", C8), ("z", C8), ("bonus", C8), ("pc", 2),
                                     ("bh", C8), ("rh", C8), ("s0", 1)]
                   + per_tile(lambda t: rw_order(t, "dve"))
                   + [("ym", C8), ("yr", C8), ("yn", C8), ("yb", C8), ("yo", C8), ("res", 12),
                      ("ln", LN_STEPS)])

        moe_pe = [Steps(sem(f"route_pe{l}"), [("hT", KC), ("lg", NT), ("sg", 4), ("pos", 4), ("sd", 6)])
                  for l in range(2)]
        moe_act = [Steps(sem(f"route_act{l}"), [("sc", NT), ("sg", 2)]) for l in range(2)]
        moe_dve = [Steps(sem(f"route_dve{l}"),
                         [("zero", 2), ("hT", KC), ("choice", 1), ("top2", 24), ("gs", 1), ("rank", 15), ("keep", 1),
                          ("hide", 1), ("mask", 2), ("top8", 6), ("sel", 2), ("sm", 2), ("g0", 1), ("gsum", 1),
                          ("grec", 2), ("g1", 1),
                          ("g2", 1), ("kr", 3), ("kr2", 1), ("dest", 3), ("tok", 3), ("pos", 3), ("pos2", 1),
                          ("max", 1), ("maxi", 1), ("sd", 6)]) for l in range(2)]
        end_act = [Steps(sem(f"combine_act{l}"), [("ln", 1)]) for l in range(2)]
        end_pe = [Steps(sem(f"combine_pe{l}"), [("few", 2)]) for l in range(2)]
        end_dve = [Steps(sem(f"combine_dve{l}"), [("few", 2), ("sum", TOPK * (NT - 1)), ("ln", LN_STEPS)])
                   for l in range(2)]

        NK = [128, 256, 272]
        ab_pe = [("hT", KC), ("q", 8), ("k", 4), ("v", 2), ("vt", 3)]
        ab_act = [("q", 8), ("k", 4), ("v", 2)]
        ab_dve = [("sink", 1), ("hT", KC), ("vt", 3)]
        BATCHES = [(t, g) for t in range(NT) for g in range(KV)]
        for b, (t, g) in enumerate(BATCHES):
            ahead_of = BATCHES[0:2] if b == 0 else BATCHES[b + 1:b + 2]
            ab_pe += [(f"sc{u}_{v}", 4) for u, v in ahead_of]
            ab_dve += [(f"mx{u}_{v}", 4) for u, v in ahead_of]
            ab_pe += [(f"pt{t}_{g}", t + 1), (f"pv{t}_{g}", 1)]
            ab_act += [(f"ex{t}_{g}", 5)]
            ab_dve += [(f"den{t}_{g}", 2), (f"pt{t}_{g}", t + 1), (f"pv{t}_{g}", 4)]
        ab_pe += [("oT", 8), ("o", 12)]
        ab_act += [("oT", 8), ("ln", 1)]
        ab_dve += [("res", 12), ("bo", 3), ("ln", LN_STEPS)]
        ap, aa, av = (Steps(sem("attn_pe"), ab_pe), Steps(sem("attn_act"), ab_act), Steps(sem("attn_dve"), ab_dve))

        slot_count = [0] * (3 * SETS)
        slot_free = [None] * (3 * SETS)
        landed = {}
        fills = {}

        def w_split(w, n0, n):
            return w[:, n0:n0 + n].rearrange("(p k) n -> p k n", k=KC)

        def w_nat(w, n0, n):
            return w[:, n0:n0 + n].rearrange("(c p) n -> p c n", p=P)

        def slot3(s, k=KC):
            return ring[:, s, :].rearrange("p (k n) -> p k n", k=k)

        def plan(group, name, slot, pieces, released_by):
            fills.setdefault(group, []).append((slot, pieces, slot_free[slot]))
            slot_count[slot] += 16 * len(pieces)
            landed[name] = (slot_loaded[slot], slot_count[slot], slot)
            slot_free[slot] = released_by

        n = 0
        for what, w in (("r", I["rwkv_w_r"]), ("k", I["rwkv_w_k"]), ("v", I["rwkv_w_v"])):
            for q in range(4):
                plan("rwkv", f"{what}{q}", n % RING, [(slot3(n % RING), w_split(w[0], 256 * q, 256))],
                     rp.at(what, 2 * q + 1))
                n += 1
        s = n % RING
        plan("rwkv", "w", s, [(ring[:, s, 0:512], I["rwkv_w1"][0].rearrange("(p k) n -> p (k n)", k=KC)),
                              (ring[0:LORA, s, 512:1536], I["rwkv_w2"][0])], rp.at("w"))
        s = (n + 1) % RING
        plan("rwkv", "a", s, [(ring[:, s, 0:512], I["rwkv_a1"][0].rearrange("(p k) n -> p (k n)", k=KC)),
                              (ring[0:LORA, s, 512:1536], I["rwkv_a2"][0])], rp.at("a"))
        s = (n + 2) % RING
        plan("rwkv", "g1", s, [(ring[:, s, 0:KC * GLORA], I["rwkv_g1"][0].rearrange("(p k) n -> p (k n)", k=KC))],
             rp.at("gh"))
        scratch_slot = s
        slot_free[s] = rp.at(f"q2_{UNITS - 1}_{NT - 1}")
        s = (n + 3) % RING
        plan("rwkv", "g2", s, [(ring[:, s, 0:1024], I["rwkv_g2"][0, 0:P]),
                               (ring[0:GLORA - P, s, 1024:2048], I["rwkv_g2"][0, P:GLORA])], rp.at("g"))
        n += 4
        for q in range(4):
            plan("rwkv", f"o{q}", n % RING, [(slot3(n % RING), w_nat(I["rwkv_w_o"][0], 256 * q, 256))],
                 rp.at("o", 3 * q + 2))
            n += 1

        def plan_shared(l):
            for j, w in enumerate((I["shared_w_gate"], I["shared_w_up"])):
                plan(f"moe{l}", f"sh{j}_{l}", 3 + j, [(ring[:, 3 + j, :], w[l].rearrange("(p k) n -> p (k n)", k=KC))],
                     moe_pe[l].at("sg"))
            plan(f"moe{l}", f"sh2_{l}", 5,
                 [(ring[:, 5, :], I["shared_w_down"][l].rearrange("(p j) n -> p (j n)", j=2))], moe_pe[l].at("sd"))

        class Main:
            onehot, values, index = sem("onehot_made"), sem("values_picked"), sem("index_ready")
            x, x_copied = sem("x_picked"), sem("x_copied")
            xt, xt_copied = sem("x_turned"), sem("xt_copied")
            gu, gu_copied, turned = sem("gate_up_done"), sem("gate_up_copied"), sem("gate_up_turned")
            silu, hid = sem("silu_done"), sem("hidden_ready")
            down, y_a, y_v = sem("down_done"), sem("y_scaled_act"), sem("y_scaled_dve")
            scattered = [sem(f"scattered{b}") for b in range(4)]
            base, slot_base, entry_free = 0, None, None

        class Spill:

            def __init__(self, l):
                def s(n):
                    return sem(f"spill{l}_{n}")
                self.onehot, self.values, self.index = s("onehot"), s("values"), s("index")
                self.x, self.x_copied, self.gu, self.gu_copied = s("x"), s("x_copied"), s("gu"), s("gu_copied")
                self.xt, self.xt_copied = s("xt"), s("xt_copied")
                self.turned, self.silu, self.hid = s("turned"), s("silu"), s("hid")
                self.down, self.y_a, self.y_v = s("down"), s("y_a"), s("y_v")
                self.scattered = s("scattered")
                self.weights = [sem(f"spill{l}_weights{s}") for s in range(3)]

        main = Main
        spill = [Spill(l) for l in range(2)]
        main_slots = []

        def plan_experts(l):
            for s in range(RING, 3 * SETS):
                slot_free[s] = (rv if l == 0 else av).end()
            main_slots.append((list(slot_count), list(slot_free)))
            done = (l + 1) * E
            for s in range(3 * SETS):
                slot_count[s] += 16 * (E // SETS)
                slot_free[s] = (main.down if s % 3 == 2 else main.gu, done)

        plan_shared(0)
        plan_experts(0)
        n = 0
        for q in range(6):
            plan("attn", f"qkv{q}", n % RING, [(slot3(n % RING), w_split(I["attn_w_qkv"][0], 256 * q, 256))],
                 ap.at("q", 2 * q + 1) if q < 4 else ap.at("k") if q == 4 else ap.at("v"))
            n += 1
        for q in range(4):
            plan("attn", f"ao{q}", n % RING, [(slot3(n % RING), w_nat(I["attn_w_o"][0], 256 * q, 256))],
                 ap.at("o", 3 * q + 2))
            n += 1
        plan_shared(1)
        plan_experts(1)

        A = [view(2176 * i, KC, T) for i in range(10)]
        hT, cum = A[0], A[0]
        xx, kkn, zT = A[1], A[1], A[1]
        xm = [A[2], A[3]]
        rT, kT, vT, wT, aT, gT = A[4], A[5], A[6], A[7], A[8], A[9]
        PEX, PIN, PMX = A[2], A[7], A[3]
        bT, bonus, yT = A[8], A[3], A[1]
        btile = view(0, KC, P)
        ktile = view(1024, KC, P)
        tokB, tokK = view(2 * 2176, KC, P), view(2 * 2176 + 1024, KC, P)
        tokV, tokZ = view(7 * 2176, KC, P), view(7 * 2176 + 1024, KC, P)
        W12 = view(21760, HEADS, 2 * HD)
        UX = 21760 + 2048
        def matrices(slots):
            return [v.rearrange("p (a b) -> p a b", a=4) for v in slots]

        in_h = [h[:, i // 2, 512 * (i % 2):512 * (i % 2) + 512] for i in range(6)]
        in_slot = [ring[:, scratch_slot, 512 * i:512 * i + 512] for i in range(3)]
        (X, XT, X2, X2T, OFF, TT, AK, BB, BK) = zip([view(UX + 512 * i, 4, P) for i in range(9)],
                                                    matrices(in_h + in_slot))
        GZ = (view(UX + 9 * 512, 4, HD),
              ring[:, scratch_slot, 3 * 512:3 * 512 + 4 * HD].rearrange("p (a b) -> p a b", a=4))
        S = view(UX + 9 * 512 + 256, PAIRS, HD)
        SP = view(UX + 9 * 512 + 768, PAIRS, HD)
        M = [view(UX + 512 * i, PAIRS, HD) for i in range(4)]
        KVS = [view(UX + 2048 + 512 * i, PAIRS, HD) for i in range(4)]
        assert UX + 9 * 512 + 1280 <= 32300
        x0 = view(UX, NT, D)
        facc = view(2 * 2176, NT, D)
        prow = view(UX + 3072, P, rows=56)
        onehot = view(UX + 3200, 2, BIASLEN, rows=BUCKETS + 1)
        relt = view(UX + 3200 + 2 * BIASLEN, HEADS, rows=BUCKETS + 1)
        brow = view(UX + 3200 + 2 * BIASLEN + 16, 2, BIASLEN, rows=HEADS)
        thid = view(UX, T, rows=LORA)
        ahid = view(UX + 272, T, rows=LORA)
        ghid = view(UX + 544, 2, T)
        tmp = [view(UX + 1088 + 272 * i, T) for i in range(2)]
        par = small[:, 0:56]
        omk = small[:, 56:64]
        mu = small[:, 64:112].rearrange("p (m k) -> p m k", m=6)
        pc = small[:, 112:112 + KC * NCH].rearrange("p (c n) -> p c n", c=KC)
        stat = small[:, 184:184 + 36].rearrange("p (t s) -> p t s", t=NT)
        mv = small[:, 220:226].rearrange("p (t s) -> p t s", t=NT)
        std = small[:, 226:229]
        rstd = small[:, 229:232]
        (PW0, PA0, PKK, PKA, PRK, PLG, PLB) = range(7)

        relt_hidden = relt[BUCKETS:BUCKETS + 1, :]
        MIXBUF = {0: 0, 2: 1, 3: 0, 1: 1, 4: 0, 5: 1}

        def tmpN(c):
            return A[2][:, c, :]

        def unit(arr, g, rows):
            return arr[rows].rearrange("p (a i r) m -> p a r i m", a=2, r=2)[:, g // 2, g % 2]

        def tpos(row, cols):
            return (row, cols.start)

        def param(i, c):
            return par[:, 8 * i + c:8 * i + c + 1]

        block = ctx.enter_context(nc.Block())

        def psum_of(steps, name, u=0):
            return ps[:, steps.index(name, u) % 8, :]

        def bank_free(eng, steps, evac, name, u=0):
            i = steps.index(name, u) - 8
            if i < 0:
                return
            for nm, first in steps.first.items():
                if first <= i < first + steps.units[nm]:
                    eng.wait_ge(*evac(nm, i - first))

        def r_evac(nm, u):
            base = nm.split("_")[0].rstrip("0123456789") if nm.startswith("tr") else nm.split("_")[0]
            if base == "ba" and not one_block(int(nm[-1])):
                return rv.at(nm.replace("ba", "off"), u)
            if nm in rv.first and (nm not in ra.first):
                return rv.at(nm, u)
            if nm in ("r", "k", "v", "wh", "w", "ah", "a", "gh", "g", "n2") or base == "tr":
                return ra.at(nm, u)
            if nm == "bon":
                return rv.at("bonus", u)
            if nm == "mean":
                return rv.at("ym", u)
            if nm == "var":
                return ra.at("std", u)
            if nm == "o":
                return rv.at("res", u)
            return ra.at(nm, u)

        def m_evac(l):
            def f(nm, u):
                if nm == "lg":
                    return moe_act[l].at("sc", u)
                if nm == "sg":
                    return moe_dve[l].at("sm", u % 2)
                return moe_dve[l].at(nm, min(u, moe_dve[l].units[nm] - 1)) if nm != "pos" else \
                    (moe_dve[l].at("pos", u) if u < 3 else moe_dve[l].at("max"))
            return f

        def a_evac(nm, u):
            if nm in ("q", "k", "v", "oT"):
                return aa.at(nm, u)
            if nm.startswith("sc"):
                return aa.at("ex" + nm[2:], u)
            if nm == "o":
                return av.at("res", u)
            if nm.startswith("pv"):
                return av.at(nm)
            return av.at(nm, u)

        def phase_start(eng, *ends):
            for e in ends:
                eng.wait_ge(*e)

        def heads_of(g):
            return [4 * g + i for i in range(4)]

        def unit_heads(g):
            return [8 * (g // 2) + 2 * i + g % 2 for i in range(4)]

        def hrows(head):
            return slice(HD * (head % 2), HD * (head % 2) + HD)

        scaled_count = nc.gpsimd.alloc_register("scaled_count")
        copied_count, hidden_count, x_copied_count = (nc.tensor.alloc_register(n) for n in
                                                      ("copied_count", "hidden_count", "x_copied_count"))
        scattered_count = nc.sync.alloc_register("scattered_count")

        mhT = view(0, KC, T)
        macc = view(2176, NT, D)
        ysc = [view(5248 + 1024 * b, D, rows=SLOTS) for b in range(4)]
        xs = view(9344, 4 * P)
        xgT = view(9856, KC, SLOTS)
        guc = view(10368, 2 * P)
        silu = view(10624, 2, SLOTS)
        hidT = [view(10752 + 128 * b, 2, SLOTS) for b in range(2)]
        hot = [view(11008 + 384 * b, NT, 2 * SLOTS) for b in range(2)]
        sidx = [view(11776 + b, 1, rows=SLOTS, dt=I32) for b in range(8)]
        gate_s = [view(11784 + b, 1) for b in range(8)]
        iota_s = view(12928, 2 * SLOTS)
        more_slots = view(20000, 3 * SETS - RING, SLOT)
        values = view(13056, NT, E * 2)
        posm = view(13648, NT, E)
        score = view(13840, NT, E)
        choice = view(14032, NT, E)
        top2 = view(14224, NT, GROUPS * 8)
        gsc = view(14416, NT, GROUPS)
        cmp1 = view(14440, GROUPS, GROUPS)
        cmp2 = view(14504, GROUPS, GROUPS)
        grank = view(14568, NT, GROUPS)
        keep = view(14592, NT, GROUPS)
        masked = view(14616, NT, E)
        top8 = view(14808, NT, 8)
        taken = view(14832, NT, E)
        sel = view(15024, NT, E)
        gsum = view(15216, NT)
        grec = view(15220, NT)
        krank = view(15224, NT, E)
        tokid = view(15416, NT)
        tie = view(15420, GROUPS, GROUPS)
        rowok = view(15484, NT)
        most = view(15488, 1)
        mosti_of = [most_tokens[:, l:l + 1] for l in range(2)]
        shid = view(15492, 2, T)
        shm = view(16036, 2, T)
        gate = view(16580, NT, E)
        rt = [view(17000, TOPK, D), view(5248, TOPK, D)]
        few = view(25192, D)
        few_sum = small[:, 232:232 + META]

        tie2i = view(16772, 2 * SLOTS + NT, dt=I32)
        dest8 = view(16904, NT)
        rowbad = view(16908, NT)

        ahT = view(0, KC, T)
        qT = view(2176, KC, T)
        kdT = view(4352, KV, T)
        vcT = view(5440, 2, T)
        vtok = view(5984, NT, KV * HD)
        hank = [view(6752, HEADS, NK[0]), view(8800, HEADS, NK[1]), view(12896, HEADS, NK[2])]
        prob = [view(17248, 4, T), view(29300, 4, T)]
        probT = view(18336, NT, 4, P)
        otok = view(19872, NT, D)
        oT = view(22944, KC, T)
        aacc = view(25120, NT, D)
        borow = view(28192, D)
        bqkv = view(29216, 14)
        sinks = view(29232, HEADS)
        bq8 = view(29248, 8)
        negm, dens, dens2, esink, esin = ([view(29256 + 20 * b + 4 * i, 4) for b in range(2)] for i in range(5))

        bV, bX, bU, bG, bR, bY = 0, 1, 2, 3, 4, (5, 6)

        def num(e, times=1, add=0, per=1):
            i, k = e
            v = times * (k // per) + add
            return v if isinstance(i, int) else i * (UNROLL * times // per) + v

        def wait(eng, s, value):
            if not isinstance(value, int) or value > 0:
                eng.wait_ge(s, value)

        def plus(e, k):
            return (e[0], e[1] + k)

        def column(array, e, width=1):
            at = num(e, width)
            return array[:, :, at:at + width] if isinstance(at, int) else array[:, :, bass.ds(at, width)]

        def e_slots(e):
            s0 = 3 * (0, 2, 3, 1)[e[1] % SETS]
            return s0, s0 + 1, s0 + 2

        def slot_of(s):
            return ring[:, s, :] if s < RING else more_slots[:, s - RING, :]

        def expert_weights(l, at):
            def one(w):
                return w[l][at:at + 1, :, :] if isinstance(at, int) else w[l][bass.ds(at, 1), :, :]
            return (one(I["moe_w_gate"]).rearrange("a (p k) n -> p (a k n)", k=KC),
                    one(I["moe_w_up"]).rearrange("a (p k) n -> p (a k n)", k=KC),
                    one(I["moe_w_down"]).rearrange("a (j p) n -> p (a j) n", p=P))

        def slot_view(s):
            return slot_of(s).rearrange("p (j n) -> p j n", j=2) if s % 3 == 2 else slot_of(s)

        def mm_pick(dst, hot, vals):
            for t, (_, n) in enumerate(TILES):
                mm = nc.tensor.matmul(dst[:, 0:2], hot[0:n, t, :], vals[0:n, t, :], start=(t == 0),
                                      stop=(t == NT - 1))
            return mm

        def mm_x(dst, hot):
            for t, (_, n) in enumerate(TILES):
                hv = h[0:n, t, :].rearrange("p (m k) -> p k m", k=KC)
                for half in range(2):
                    mm = nc.tensor.matmul(dst[SLOTS * half:SLOTS * half + SLOTS, :], hot[0:n, t, 0:SLOTS],
                                          hv[:, 4 * half:4 * half + 4, :], start=(t == 0), stop=(t == NT - 1))
            return mm

        def mm_turn_x(dst):
            for j in range(4):
                mm = nc.tensor.transpose(dst[:, P * j:P * j + P], xs[:, P * j:P * j + P], ident[:, :])
            return mm

        def copy_xt():
            return nc.vector.tensor_copy(xgT.rearrange("p (r j) m -> p j r m", r=2),
                                         ps[:, bU, :].rearrange("p (j r m) -> p j r m", j=4, r=2))

        def mm_gate_up(dst, s):
            for k in range(KC):
                for j in range(2):
                    mm = nc.tensor.matmul(dst[SLOTS * j:SLOTS * j + SLOTS, 0:FF], xgT[:, k, :],
                                          slot_of(s + j)[:, FF * k:FF * k + FF], start=(k == 0), stop=(k == KC - 1))
            return mm

        def mm_turn(dst):
            for j in range(2):
                mm = nc.tensor.transpose(dst[:, P * j:P * j + P], guc[:, P * j:P * j + P], ident[:, :])
            return mm

        def turned_part(which):
            return ps[:, bR, 0:2 * P].rearrange("p (j m) -> p j m", j=2)[:, :, SLOTS * which:SLOTS * which + SLOTS]

        def mm_down(dst, s, hid):
            for j in range(2):
                for half in range(2):
                    mm = nc.tensor.matmul(dst[SLOTS * half:SLOTS * half + SLOTS, :], hid[:, j, :],
                                          slot_of(s)[:, D * j + 512 * half:D * j + 512 * half + 512],
                                          start=(j == 0), stop=(j == 1))
            return mm

        def mark_slots(hot, pos, first_slot):
            return nc.vector.scalar_tensor_tensor(
                out=hot, in0=iota_s.unsqueeze(1).to_broadcast([P, NT, 2 * SLOTS]), scalar=float(first_slot),
                in1=pos.to_broadcast([P, NT, 2 * SLOTS]), op0=ALU.add, op1=ALU.is_equal)

        def take_index(picked, s, gate_of):
            nc.vector.tensor_scalar(s, picked[0:SLOTS, 0:1], OUT_OF_RANGE, None, ALU.add)
            return nc.vector.tensor_copy(gate_of, picked[:, 1:2])

        def scatter(l, src, index):
            return nc.gpsimd.indirect_dma_start(
                out=routed[l], out_offset=bass.IndirectOffsetOnAxis(ap=index, axis=0), in_=src, in_offset=None,
                bounds_check=T * TOPK - 1, oob_is_err=False)

        def sp_expert(sp, L, l, e):
            slots = e_slots(e)
            first = isinstance(e[0], int) and e[1] < SETS
            for j, (s, src) in enumerate(zip(slots, expert_weights(l, num(e)))):
                if first:
                    if L.entry_free[s]:
                        sp.wait_ge(*L.entry_free[s])
                elif j == 0:
                    sp.wait_ge(L.gu, num(plus(e, -SETS), 1, L.base + 1))
                elif j == 2:
                    sp.wait_ge(L.down, num(plus(e, -SETS), 1, L.base + 1))
                sp.dma_start(slot_view(s), src).then_inc(slot_loaded[s], 16)

        def pe_x(pe, L, e):
            pe.wait_ge(L.onehot, num(e, 1, L.base + 1))
            wait(pe, L.x_copied, num(e, 1, L.base))
            wait(pe, L.index, num(e, 1, L.base))
            mm_x(ps[:, bX, :], hot[e[1] % 2]).then_inc(L.x, 1)
            mm_pick(ps[:, bV, :], hot[e[1] % 2], column(values, e, 2)).then_inc(L.values, 1)

        def pe_turn_x(pe, L, l, e):
            copied = num(e, 1, L.base + 1)
            if not isinstance(copied, int):
                pe.reg_add(x_copied_count, x_copied_count, 1)
                copied = x_copied_count
            pe.wait_ge(*moe_dve[l].at("zero"))
            pe.wait_ge(L.x_copied, copied)
            mm_turn_x(ps[:, bU, :]).then_inc(L.xt, 1)

        def pe_expert(pe, L, l, e, this=True):
            after, two_after, prev = ahead(e, 1), ahead(e, 2), e_before(e)
            if this:
                s0, s1, _ = e_slots(e)
                pe.wait_ge(L.xt_copied, num(e, 1, L.base + 1))
                pe.wait_ge(slot_loaded[s0], num(e, 16, L.slot_base[s0] + 16, per=SETS))
                pe.wait_ge(slot_loaded[s1], num(e, 16, L.slot_base[s1] + 16, per=SETS))
                wait(pe, L.gu_copied, num(e, 1, L.base))
                mm_gate_up(ps[:, bG, :], s0).then_inc(L.gu, 1)
            if this and after:
                pe_turn_x(pe, L, l, plus(e, 1))
            if this and two_after:
                pe_x(pe, L, plus(e, 2))
            if this:
                copied, hidden = num(e, 1, L.base + 1), num(e, 1, L.base)
                if not isinstance(copied, int):
                    pe.reg_add(copied_count, copied_count, 1)
                    pe.reg_add(hidden_count, hidden_count, 1)
                    copied, hidden = copied_count, hidden_count
                pe.wait_ge(*moe_dve[l].at("zero"))
                pe.wait_ge(L.gu_copied, copied)
                wait(pe, L.hid, hidden)
                mm_turn(ps[:, bR, :]).then_inc(L.turned, 1)
            if prev:
                q = plus(e, -1)
                s2 = e_slots(q)[2]
                pe.wait_ge(L.hid, num(q, 1, L.base + 1))
                pe.wait_ge(slot_loaded[s2], num(q, 16, L.slot_base[s2] + 16, per=SETS))
                wait(pe, L.y_a, num(q, 1, L.base - 1))
                wait(pe, L.y_v, num(q, 1, L.base - 1))
                mm_down(ps[:, bY[q[1] % 2], :], s2, hidT[q[1] % 2]).then_inc(L.down, 1)

        def act_copy_x(act, L, e):
            act.wait_ge(L.x, num(e, 1, L.base + 1))
            wait(act, L.xt, num(e, 1, L.base))
            nc.scalar.copy(xs, ps[:, bX, :]).then_inc(L.x_copied, 1)

        def act_expert(act, L, e, this=True):
            two_after, prev = ahead(e, 2), e_before(e)
            if this:
                act.wait_ge(L.gu, num(e, 1, L.base + 1))
                wait(act, L.turned, num(e, 1, L.base))
                nc.scalar.copy(guc, ps[:, bG, 0:FF]).then_inc(L.gu_copied, 1)
            if this and two_after:
                act_copy_x(act, L, plus(e, 2))
            if this:
                act.wait_ge(L.turned, num(e, 1, L.base + 1))
                wait(act, L.hid, num(e, 1, L.base))
                nc.scalar.activation(silu, turned_part(0), ACT.Silu).then_inc(L.silu, 1)
            if prev:
                q = plus(e, -1)
                act.wait_ge(L.down, num(q, 1, L.base + 1))
                act.wait_ge(L.index, num(q, 1, L.base + 1))
                wait(act, L.scattered[q[1] % 4], num(q, 16, 4 * L.base, per=4))
                nc.scalar.activation(ysc[q[1] % 4][:, 512:1024], ps[SLOTS:P, bY[q[1] % 2], :], ACT.Copy,
                                     scale=gate_s[q[1] % 8][SLOTS:P]).then_inc(L.y_a, 1)

        def dve_mark(dve, L, e):
            wait(dve, L.values, num(e, 1, L.base - 1))
            mark_slots(hot[e[1] % 2], column(posm, e), 0).then_inc(L.onehot, 1)

        def dve_index(dve, L, e):
            k = e[1] % 8
            dve.wait_ge(L.values, num(e, 1, L.base + 1))
            wait(dve, L.scattered[e[1] % 4], num(e, 16, 4 * L.base - 16, per=4))
            take_index(ps[:, bV, :], sidx[k], gate_s[k]).then_inc(L.index, 1)

        def dve_copy_xt(dve, L, e):
            dve.wait_ge(L.xt, num(e, 1, L.base + 1))
            wait(dve, L.gu, num(e, 1, L.base))
            copy_xt().then_inc(L.xt_copied, 1)

        def dve_expert(dve, L, e, this=True):
            if this and ahead(e, 3):
                dve_mark(dve, L, plus(e, 3))
            if this and ahead(e, 1):
                dve_copy_xt(dve, L, plus(e, 1))
            if this and ahead(e, 2):
                dve_index(dve, L, plus(e, 2))
            prev = e_before(e)
            if this:
                dve.wait_ge(L.silu, num(e, 1, L.base + 1))
                wait(dve, L.down, num(e, 1, L.base - 1))
                nc.vector.tensor_tensor(hidT[e[1] % 2], silu, turned_part(1), ALU.mult).then_inc(L.hid, 1)
            if prev:
                q = plus(e, -1)
                dve.wait_ge(L.down, num(q, 1, L.base + 1))
                dve.wait_ge(L.index, num(q, 1, L.base + 1))
                wait(dve, L.scattered[q[1] % 4], num(q, 16, 4 * L.base, per=4))
                nc.vector.tensor_scalar(ysc[q[1] % 4][:, 0:512], ps[0:SLOTS, bY[q[1] % 2], :],
                                        gate_s[q[1] % 8][0:SLOTS], None, ALU.mult).then_inc(L.y_v, 1)

        def pool_scatter(pool, L, l, e):
            scaled = num(e, 1, L.base + 1)
            if not isinstance(scaled, int):
                pool.reg_add(scaled_count, scaled_count, 1)
                scaled = scaled_count
            pool.wait_ge(*moe_dve[l].at("zero"))
            pool.wait_ge(L.y_a, scaled)
            pool.wait_ge(L.y_v, scaled)
            scatter(l, ysc[e[1] % 4], sidx[e[1] % 8]).then_inc(L.scattered[e[1] % 4], 16)

        def over_experts(eng, body):
            for k in range(HEAD):
                body((0, k))
            with eng.Fori(0, (E - HEAD - TAIL) // UNROLL) as i:
                for j in range(UNROLL):
                    body((i, HEAD + j))
            for k in range(E - TAIL, E):
                body((0, k))

        def ahead(e, k):
            return not isinstance(e[0], int) or e[1] + k < E

        def e_before(e):
            return not isinstance(e[0], int) or e[1] >= 1

        def sp_experts(sp, L, l):
            over_experts(sp, lambda e: sp_expert(sp, L, l, e))

        def pe_experts(pe, L, l):
            pe.reg_mov(copied_count, num((0, HEAD - 1), 1, L.base + 1))
            pe.reg_mov(hidden_count, num((0, HEAD - 1), 1, L.base))
            pe.reg_mov(x_copied_count, num((0, HEAD), 1, L.base + 1))
            pe_x(pe, L, (0, 0))
            pe_turn_x(pe, L, l, (0, 0))
            pe_x(pe, L, (0, 1))
            over_experts(pe, lambda e: pe_expert(pe, L, l, e))
            pe_expert(pe, L, l, (0, E), this=False)

        def act_experts(act, L):
            act_copy_x(act, L, (0, 0))
            act_copy_x(act, L, (0, 1))
            over_experts(act, lambda e: act_expert(act, L, e))
            act_expert(act, L, (0, E), this=False)

        def dve_experts(dve, L):
            dve_mark(dve, L, (0, 0))
            dve_mark(dve, L, (0, 1))
            dve_index(dve, L, (0, 0))
            dve_copy_xt(dve, L, (0, 0))
            dve_mark(dve, L, (0, 2))
            dve_index(dve, L, (0, 1))
            over_experts(dve, lambda e: dve_expert(dve, L, e))
            dve_expert(dve, L, (0, E), this=False)

        def pool_experts(pool, L, l):
            pool.reg_mov(scaled_count, num((0, HEAD - 2), 1, L.base + 1))
            over_experts(pool, lambda e: pool_scatter(pool, L, l, plus(e, -1)) if e_before(e) else None)
            pool_scatter(pool, L, l, (0, E - 1))

        def all_scattered(eng, l):
            for s in main.scattered:
                eng.wait_ge(s, 4 * E * (l + 1))

        SPILLS = range(SLOTS, T, SLOTS)

        def run_spill(eng, l, body, counted=None):
            X = spill[l]
            eng.wait_ge(*moe_dve[l].at("maxi"))
            count = eng.value_load(mosti_of[l][0:1, 0:1], min_val=0, max_val=T)
            for p, first_slot in enumerate(SPILLS):
                with eng.If(count > first_slot):
                    with eng.Fori(0, E) as e:
                        n = e + p * E
                        body(X, e, n, first_slot)
                        if counted is not None:
                            eng.reg_add(counted, counted, 16)
                            eng.wait_ge(*moe_dve[l].at("zero"))
                        eng.wait_ge(X.scattered, n * 16 + 16 if counted is None else counted)

        def sp_spill(sp, l):
            sp.wait_ge(main.down, E * (l + 1))

            def body(X, e, n, first_slot):
                for s, src in zip(range(3), expert_weights(l, e)):
                    sp.dma_start(slot_view(s), src).then_inc(X.weights[s], 16)
            sp.reg_mov(scattered_count, 0)
            run_spill(sp, l, body, scattered_count)

        def pe_spill(pe, l):
            def body(X, e, n, first_slot):
                pe.wait_ge(X.onehot, n + 1)
                mm_x(ps[:, bX, :], hot[0]).then_inc(X.x, 1)
                mm_pick(ps[:, bV, :], hot[0], values[:, :, bass.ds(e * 2, 2)]).then_inc(X.values, 1)
                pe.reg_add(copied_count, copied_count, 1)
                pe.wait_ge(*moe_dve[l].at("zero"))
                pe.wait_ge(X.x_copied, copied_count)
                mm_turn_x(ps[:, bU, :]).then_inc(X.xt, 1)
                pe.wait_ge(X.xt_copied, n + 1)
                pe.wait_ge(X.weights[0], n * 16 + 16)
                pe.wait_ge(X.weights[1], n * 16 + 16)
                mm_gate_up(ps[:, bG, :], 0).then_inc(X.gu, 1)
                pe.wait_ge(*moe_dve[l].at("zero"))
                pe.wait_ge(X.gu_copied, copied_count)
                mm_turn(ps[:, bR, :]).then_inc(X.turned, 1)
                pe.wait_ge(X.hid, n + 1)
                pe.wait_ge(X.weights[2], n * 16 + 16)
                mm_down(ps[:, bY[0], :], 2, hidT[0]).then_inc(X.down, 1)
            pe.reg_mov(copied_count, 0)
            run_spill(pe, l, body)

        def act_spill(act, l):
            def body(X, e, n, first_slot):
                act.wait_ge(X.x, n + 1)
                nc.scalar.copy(xs, ps[:, bX, :]).then_inc(X.x_copied, 1)
                act.wait_ge(X.gu, n + 1)
                nc.scalar.copy(guc, ps[:, bG, 0:FF]).then_inc(X.gu_copied, 1)
                act.wait_ge(X.turned, n + 1)
                nc.scalar.activation(silu, turned_part(0), ACT.Silu).then_inc(X.silu, 1)
                act.wait_ge(X.down, n + 1)
                act.wait_ge(X.index, n + 1)
                nc.scalar.activation(ysc[0][:, 512:1024], ps[SLOTS:P, bY[0], :], ACT.Copy, scale=gate_s[0][SLOTS:P])\
                    .then_inc(X.y_a, 1)
            run_spill(act, l, body)

        def dve_spill(dve, l):
            def body(X, e, n, first_slot):
                mark_slots(hot[0], posm[:, :, bass.ds(e, 1)], first_slot).then_inc(X.onehot, 1)
                dve.wait_ge(X.values, n + 1)
                take_index(ps[:, bV, :], sidx[0], gate_s[0]).then_inc(X.index, 1)
                dve.wait_ge(X.xt, n + 1)
                copy_xt().then_inc(X.xt_copied, 1)
                dve.wait_ge(X.silu, n + 1)
                nc.vector.tensor_tensor(hidT[0], silu, turned_part(1), ALU.mult).then_inc(X.hid, 1)
                dve.wait_ge(X.down, n + 1)
                dve.wait_ge(X.index, n + 1)
                nc.vector.tensor_scalar(ysc[0][:, 0:512], ps[0:SLOTS, bY[0], :], gate_s[0][0:SLOTS], None, ALU.mult)\
                    .then_inc(X.y_v, 1)
            all_scattered(dve, l)
            run_spill(dve, l, body)

        def pool_spill(pool, l):
            def body(X, e, n, first_slot):
                pool.reg_add(scaled_count, scaled_count, 1)
                pool.wait_ge(*moe_dve[l].at("zero"))
                pool.wait_ge(X.y_a, scaled_count)
                pool.wait_ge(X.y_v, scaled_count)
                scatter(l, ysc[0], sidx[0]).then_inc(X.scattered, 16)
            pool.reg_mov(scaled_count, 0)
            run_spill(pool, l, body)

        def set_main(l):
            main.base = l * E
            main.slot_base, main.entry_free = main_slots[l]

        def row(src):
            return src.rearrange("(a n) -> a n", a=1).to_broadcast([P, src.shape[0]])

        @block.sync
        def _(sp):
            def static(group):
                for slot, pieces, free in fills[group]:
                    if free:
                        sp.wait_ge(*free)
                    for dst, src in pieces:
                        sp.dma_start(dst, src).then_inc(slot_loaded[slot], 16)

            sp.dma_start(x0[0:META, 0, :], I["meta"]).then_inc(x_loaded, 16)
            sp.dma_start(x0[META:P, 0, :], I["x"][0, 0:P - META, :]).then_inc(x_loaded, 16)
            sp.dma_start(x0[:, 1, :], I["x"][0, P - META:2 * P - META, :]).then_inc(x_loaded, 16)
            sp.dma_start(x0[0:16, 2, :], I["x"][0, 2 * P - META:SEQ, :]).then_inc(x_loaded, 16)
            sp.wait_ge(params_loaded, 16 * 14)
            static("rwkv")
            for l in range(2):
                static(f"moe{l}")
                set_main(l)
                sp_experts(sp, main, l)
                sp_spill(sp, l)
                if l == 0:
                    sp.wait_ge(routed_loaded[NT - 2][TOPK // 2 - 1], 16)
                    static("attn")

        @block.gpsimd
        def _(pool):
            nc.gpsimd.memset(ident[:, :], 0.0).then_inc(*consts.step("ones", 0))
            for m in (up16, up32, up32d, low16, lowoff, before, allones, headones):
                last = nc.gpsimd.memset(m[:, :], 1.0)
            last.then_inc(*consts.step("ones", 1))
            nc.gpsimd.memset(anti[:, :], 0.0)
            nc.gpsimd.memset(notfirst[:, :], 1.0)
            nc.gpsimd.memset(eps[:, 0:1], LN_EPS)
            nc.gpsimd.memset(eps[:, 1:2], GN_EPS).then_inc(*consts.step("ones", 2))
            nc.gpsimd.memset(few_sum, 1.0).then_inc(*consts.step("ones", 3))
            pool.wait_ge(*consts.at("ones"))
            made = sem("mask_step")
            count = [0]

            def select(m, blk, op, base, cm, pattern, fill=0.0):
                v = m if blk is None else m.rearrange("p (b n) -> p b n", n=blk)
                nc.gpsimd.affine_select(out=v, in_=v, compare_op=op, fill=fill, base=base, pattern=pattern,
                                        channel_multiplier=cm).then_inc(made, 1)
                count[0] += 1
                pool.wait_ge(made, count[0])

            def same_block(m, blk):
                nb = P // blk
                select(m[:, :], blk, ALU.is_ge, 0, 1, [[-blk, nb], [0, blk]])
                select(m[:, :], blk, ALU.is_ge, blk - 1, -1, [[blk, nb], [0, blk]])

            select(ident[:, :], None, ALU.not_equal, 0, 1, [[-1, P]], 1.0)
            pool.nop().then_inc(*consts.step("ident"))
            select(anti[:, :], None, ALU.not_equal, -(P - 1), 1, [[1, P]], 1.0)
            same_block(headones, HD)
            for m, op, blk in ((up16, ALU.is_gt, HALF), (up32, ALU.is_gt, CHUNK), (up32d, ALU.is_ge, CHUNK)):
                select(m[:, :], None, op, 0, -1, [[1, P]])
                same_block(m, blk)
            select(before[:, :], None, ALU.is_gt, 0, -1, [[1, P]])
            select(low16[:, :], None, ALU.is_gt, 0, 1, [[-1, P]])
            same_block(low16, HALF)
            same_block(lowoff, CHUNK)
            select(lowoff[:, :], HALF, ALU.is_ge, -HALF, 1, [[-HALF, P // HALF], [0, HALF]])
            select(notfirst[:, 0:256], CHUNK, ALU.is_gt, 0, 0, [[0, 256 // CHUNK], [1, CHUNK]])
            select(notfirst[:, 256:T], None, ALU.is_gt, 0, 0, [[1, T - 256]])
            select(few_sum, None, ALU.is_ge, 0, 1, [[-TOPK, META]])
            select(few_sum, None, ALU.is_ge, TOPK - 1, -1, [[TOPK, META]])
            pool.nop().then_inc(*consts.step("made"))

            def load_ln(g, b):
                pool.dma_start(lnrow[:, 0, :], row(g)).then_inc(ln_loaded, 16)
                pool.dma_start(lnrow[:, 1, :], row(b)).then_inc(ln_loaded, 16)

            load_ln(I["ln_mix_g"][0], I["ln_mix_b"][0])
            pool.wait_ge(*rv.at("bias"))
            pool.dma_start(biasd, brow).then_inc(bias_stored, 16)
            for c in range(KC):
                pool.wait_ge(*ra.at("pi", c))
                pool.wait_ge(*rv.at("rk", c))
                nc.gpsimd.tensor_tensor(kT[:, c, :], kT[:, c, :], PIN[:, c, :], ALU.mult).then_inc(kh_made, 1)
            for c in range(KC):
                pool.wait_ge(*rv.at("bonus", c))
                nc.gpsimd.tensor_scalar(bonus[:, c, :], bonus[:, c, :], param(PLB, c), None, ALU.add)\
                    .then_inc(bonus_shifted, 1)
            pool.wait_ge(*rv.at(f"y_{NCH - 1}_{NT - 1}"))
            pool.wait_ge(*rp.at(f"q2_{UNITS - 1}_{NT - 1}"))
            pool.dma_start(h[0:META, 0, :], I["meta"]).then_inc(h_loaded, 16)
            pool.dma_start(h[META:P, 0, :], I["x"][0, 0:P - META, :]).then_inc(h_loaded, 16)
            pool.dma_start(h[:, 1, :], I["x"][0, P - META:2 * P - META, :]).then_inc(h_loaded, 16)
            pool.dma_start(h[0:16, 2, :], I["x"][0, 2 * P - META:SEQ, :]).then_inc(h_loaded, 16)

            for l in range(2):
                before_dve = rv if l == 0 else av
                pool.wait_ge(*before_dve.end())
                load_ln(I["ln_ffn_g"][l], I["ln_ffn_b"][l])
                nc.gpsimd.iota(tie2i[:, 0:2 * SLOTS], [[0, 2], [1, SLOTS]], base=0, channel_multiplier=0)\
                    .then_inc(made, 1)
                nc.gpsimd.iota(tie2i[:, 2 * SLOTS:2 * SLOTS + NT], [[P, NT]], base=0, channel_multiplier=1).then_inc(made, 1)
                count[0] += 2
                pool.wait_ge(made, count[0])
                nc.gpsimd.tensor_copy(iota_s, tie2i[:, 0:2 * SLOTS]).then_inc(made, 1)
                nc.gpsimd.tensor_copy(tokid, tie2i[:, 2 * SLOTS:2 * SLOTS + NT]).then_inc(made, 1)
                nc.gpsimd.memset(rowok, 1.0).then_inc(made, 1)
                nc.gpsimd.memset(tie, 1.0).then_inc(made, 1)
                count[0] += 4
                pool.wait_ge(made, count[0])
                select(rowok[:, 2:3], None, ALU.is_gt, 16, -1, [[0, 1]])
                nc.gpsimd.affine_select(out=tie, in_=tie, compare_op=ALU.is_gt, fill=0.0, base=0,
                                        pattern=[[1, GROUPS], [-1, GROUPS]], channel_multiplier=0)\
                    .then_inc(route_consts, 1)
                set_main(l)
                pool_experts(pool, main, l)
                pool_spill(pool, l)
                all_scattered(pool, l)
                if l == 0:
                    pool.dma_start(bqkv[:, 0:8], I["attn_b_qkv"][0, 0:HEADS * HD].rearrange("(c p) -> p c", p=P),
                                   allow_slow_non_contiguous=True).then_inc(attn_loaded, 16)
                    bk = I["attn_b_qkv"][0, HEADS * HD:(HEADS + KV) * HD].rearrange("(g p) -> p g", p=HD)
                    for r in range(2):
                        pool.dma_start(bqkv[HD * r:HD * r + HD, 8:12], bk,
                                       allow_slow_non_contiguous=True).then_inc(attn_loaded, 16)
                    pool.dma_start(bqkv[:, 12:14], I["attn_b_qkv"][0, (HEADS + KV) * HD:QKV]
                                   .rearrange("(c p) -> p c", p=P), allow_slow_non_contiguous=True)\
                        .then_inc(attn_loaded, 16)
                    pool.dma_start(sinks, row(I["attn_sinks"][0])).then_inc(attn_loaded, 16)
                    pool.dma_start(borow, row(I["attn_b_o"][0])).then_inc(attn_loaded, 16)
                pool.dma_start(few, routed[l][(T - META) * TOPK:, :]).then_inc(few_loaded, 16)
                rv3 = routed[l].rearrange("(t k) d -> t k d", k=TOPK)
                for t in range(NT - 1):
                    for j in range(TOPK // 2):
                        pool.dma_start(rt[t][:, 2 * j:2 * j + 2, :], rv3[P * t:P * t + P, 2 * j:2 * j + 2, :])\
                            .then_inc(routed_loaded[t][j], 16)
                if l == 0:
                    pool.wait_ge(*end_dve[0].end())
                    load_ln(I["ln_mix_g"][1], I["ln_mix_b"][1])
            pool.wait_ge(*end_dve[1].end())
            o = out[0]
            pool.dma_start(o[0:P - META, :], h[META:P, 0, :]).then_inc(out_stored, 16)
            pool.dma_start(o[P - META:2 * P - META, :], h[:, 1, :]).then_inc(out_stored, 16)
            pool.dma_start(o[2 * P - META:SEQ, :], h[0:16, 2, :]).then_inc(out_stored, 16)
            pool.wait_ge(out_stored, 48)

        @block.tensor
        def _(pe):
            mm_ = nc.tensor.matmul

            def need(name):
                s, v, slot = landed[name]
                pe.wait_ge(s, v)
                return slot

            def start(steps, evac, name, u=0):
                bank_free(pe, steps, evac, name, u)
                return psum_of(steps, name, u)

            def R(name, u=0):
                return start(rp, r_evac, name, u)

            pe.wait_ge(*consts.at("ident"))
            pe.wait_ge(params_loaded, 16 * 14)
            b = R("par")
            nc.tensor.transpose(b[:, 0:56], prow[0:56, :], ident[0:56, 0:56]).then_inc(*rp.step("par"))
            pe.wait_ge(x_loaded, 64)
            for k in range(KC):
                b = R("xT", k)
                for t, (r0, n) in enumerate(TILES):
                    xv = x0[0:n, t, :].rearrange("p (m k) -> p k m", k=KC)
                    m = nc.tensor.transpose(b[:, r0:r0 + n], xv[:, k, :], ident[0:n, 0:n])
                m.then_inc(*rp.step("xT", k))
            pe.wait_ge(hidden_row, 1)
            for j in range(4):
                b = R("bias", j)
                mm_(b[0:HEADS, 0:T], relt[:, :], onehot[:, j // 2, T * (j % 2):T * (j % 2) + T], start=True,
                    stop=True).then_inc(*rp.step("bias", j))

            def proj(name, mix):
                pe.wait_ge(*rv.at(f"mix{mix}"))
                for c in range(C8):
                    s = need(f"{name}{c // 2}")
                    b = R(name, c)
                    for k in range(KC):
                        m = mm_(b[:, 0:T], slot3(s)[:, k, P * (c % 2):P * (c % 2) + P], xm[MIXBUF[mix]][:, k, :],
                                start=(k == 0), stop=(k == KC - 1))
                    m.then_inc(*rp.step(name, c))

            pe.wait_ge(*consts.at("made"))
            proj("r", 0)
            proj("k", 2)
            proj("v", 3)
            for nm, mix, wn, dst in (("w", 1, LORA, thid), ("a", 4, LORA, ahid)):
                pe.wait_ge(*rv.at(f"mix{mix}"))
                s = need(nm)
                b = R(nm + "h")
                for k in range(KC):
                    m = mm_(b[0:LORA, 0:T], ring[:, s, LORA * k:LORA * k + LORA], xm[MIXBUF[mix]][:, k, :],
                            start=(k == 0), stop=(k == KC - 1))
                m.then_inc(*rp.step(nm + "h"))
                pe.wait_ge(*ra.at(nm + "h"))
                for c in range(C8):
                    b = R(nm, c)
                    mm_(b[:, 0:T], ring[0:LORA, s, 512 + P * c:512 + P * c + P], dst, start=True,
                        stop=True).then_inc(*rp.step(nm, c))
            pe.wait_ge(*rv.at("mix5"))
            s = need("g1")
            for j, (m0, mn) in enumerate(((0, P), (P, GLORA - P))):
                b = R("gh", j)
                for k in range(KC):
                    m = mm_(b[0:mn, 0:T], ring[:, s, GLORA * k + m0:GLORA * k + m0 + mn], xm[MIXBUF[5]][:, k, :],
                            start=(k == 0), stop=(k == KC - 1))
                m.then_inc(*rp.step("gh", j))
            pe.wait_ge(*ra.at("gh"))
            s = need("g2")
            for c in range(C8):
                b = R("g", c)
                mm_(b[:, 0:T], ring[:, s, P * c:P * c + P], ghid[:, 0, :], start=True, stop=False)
                mm_(b[:, 0:T], ring[0:GLORA - P, s, D + P * c:D + P * c + P], ghid[0:GLORA - P, 1, :],
                    start=False, stop=True).then_inc(*rp.step("g", c))
            for c in range(C8):
                pe.wait_ge(*ra.at("sq", c))
                b = R("n2", c)
                mm_(b[:, 0:T], headones[:, :], tmpN(c), start=True, stop=True).then_inc(*rp.step("n2", c))
            for c in range(C8):
                pe.wait_ge(*rv.at("rk", c))
                b = R("bon", c)
                mm_(b[:, 0:T], headones[:, :], A[0][:, c, :], start=True, stop=True).then_inc(*rp.step("bon", c))

            for t, (r0, n) in enumerate(TILES):
                cols = slice(r0, r0 + n)
                for j, (src, w) in enumerate(((btile, "bt"), (ktile, "kt"), (vT, None), (zT, None))):
                    if w:
                        pe.wait_ge(*rv.at(f"{w}{t}"))
                    for half in range(2):
                        u = 2 * j + half
                        b = R(f"tr{t}", u)
                        for i in range(4):
                            c = 4 * half + i
                            a_in = src[:, c, 0:n] if w else src[:, c, cols]
                            m = nc.tensor.transpose(b[0:n, P * i:P * i + P], a_in, ident[:, :])
                        m.then_inc(*rp.step(f"tr{t}", u))
                for pair in range(UNITS // 2):
                    both = (2 * pair, 2 * pair + 1)

                    def N(x, g):
                        return f"{x}_{g}_{t}"

                    def four(name, f, ready=(), after=(), in_turns=False):
                        for w in after:
                            pe.wait_ge(*w)
                        for units in (both,) if in_turns else ((g,) for g in both):
                            banks = []
                            for g in units:
                                for steps, nm in ready:
                                    pe.wait_ge(*steps.at(N(nm, g)))
                                banks.append(R(N(name, g)))
                            for i in range(4):
                                for g, b in zip(units, banks):
                                    m = f(g, i, unit_heads(g)[i], b)
                                    if i == 3:
                                        m.then_inc(*rp.step(N(name, g)))

                    def ch(arr, hd):
                        return arr[hrows(hd), hd // 2, cols]

                    def cross(lhs, rhs):
                        return lambda g, i, hd, b: mm_(b[0:n, P * i:P * i + n], ch(lhs, hd), ch(rhs, hd),
                                                       start=True, stop=True)

                    four("ab", cross(bT, zT), after=[rv.at("s0")], in_turns=True)
                    four("ba", cross(zT, bT), in_turns=True)
                    four("ak", cross(kT, zT), in_turns=True)
                    four("bb", cross(bT, rT), in_turns=True)
                    four("bk", cross(kT, rT), in_turns=True)

                    def sq(lhs, rhs):
                        return lambda g, i, hd, b: mm_(b[0:n, P * i:P * i + n], lhs[g % 2][0:n, i, 0:n],
                                                       rhs[g % 2][0:n, i, 0:n], start=True, stop=True)

                    four("x2", sq(XT, X), [(rv, "ba")])
                    four("x2t", sq(X, XT))
                    four("tt2", sq(X2, TT), [(ra, "x2"), (rv, "tt1")])
                    four("x4", sq(X2T, X2), [(ra, "x2t")])
                    four("x4t", sq(X2, X2T))
                    four("tt3", sq(X, TT), [(ra, "x4"), (rv, "tt2")])
                    four("x8", sq(XT, X), [(ra, "x4t")])
                    four("tt4", sq(X2, TT), [(ra, "x8"), (rv, "tt3")])
                    if not one_block(t):
                        four("td", lambda g, i, hd, b: nc.tensor.transpose(b[0:n, P * i:P * i + n],
                                                                           TT[g % 2][0:n, i, 0:n], ident[0:n, 0:n]),
                             [(rv, "tt4")])
                        four("f", sq(OFF, TT), [(rv, "off")])
                        four("tt5", sq(X, X2T), [(ra, "td"), (ra, "f")])
                    four("g1", lambda g, i, hd, b: mm_(b[0:n, HD * i:HD * i + HD], AK[g % 2][0:n, i, 0:n],
                                                       tokV[0:n, hd // 2, hrows(hd)], start=True, stop=True),
                         [(rv, "ak")], [ra.at(f"tr{t}")])

                    def w12(g, i, hd, b):
                        mm_(b[0:n, P * i:P * i + HD], TT[g % 2][0:n, i, 0:n], tokZ[0:n, hd // 2, hrows(hd)],
                            start=True, stop=True)
                        return mm_(b[0:n, P * i + HD:P * i + P], TT[g % 2][0:n, i, 0:n], GZ[g % 2][0:n, i, :],
                                   start=True, stop=True)
                    four("w12", w12, [(ra, "g1"), (rv, "tt4" if one_block(t) else "tt5")])
                    four("q1", lambda g, i, hd, b: mm_(b[hrows(hd), P * i:P * i + n], W12[0:n, hd, 0:HD],
                                                       BB[g % 2][0:n, i, 0:n], start=True, stop=True),
                         [(ra, "w12"), (rv, "bk")], in_turns=True)

                    def q2(g, i, hd, b):
                        o = b[hrows(hd), P * i:P * i + n]
                        mm_(o, W12[0:n, hd, HD:P], BB[g % 2][0:n, i, 0:n], start=True, stop=False)
                        return mm_(o, tokV[0:n, hd // 2, hrows(hd)], BK[g % 2][0:n, i, 0:n], start=False, stop=True)
                    four("q2", q2, in_turns=True)
                live = carried(t)
                for name, parts in (("m", 1), ("kv", 2)):
                    banks = [R(f"{name}_{t}", j) for j in range(len(live))]
                    for pr in range(PAIRS):
                        for part in range(parts):
                            for j, b in enumerate(banks):
                                rows = slice(CHUNK * j, CHUNK * j + CHUNK)
                                for hd in (2 * pr, 2 * pr + 1):
                                    hr = hrows(hd)
                                    if name == "m":
                                        lhs, rhs = W12[rows, hd, 0:HD], tokB[rows, pr, hr]
                                    elif part == 0:
                                        lhs, rhs = tokB[rows, pr, hr], W12[rows, hd, HD:P]
                                    else:
                                        lhs, rhs = tokK[rows, pr, hr], tokV[rows, pr, hr]
                                    m = mm_(b[hr, HD * pr:HD * pr + HD], lhs, rhs, start=(part == 0),
                                            stop=(part == parts - 1), tile_position=tpos(CHUNK * j, hr))
                                if pr == PAIRS - 1 and part == parts - 1:
                                    m.then_inc(*rp.step(f"{name}_{t}", j))
                for c in chunk_ids(t):
                    qn = min(CHUNK, T - CHUNK * c)
                    if c > 0:
                        pe.wait_ge(*rv.at(f"s_{c - 1}_{(c - 1) // 4}"))
                    pe.wait_ge(*rv.at(f"q1_{UNITS - 1}_{t}"))
                    b = R(f"y_{c}_{t}")
                    for hd in range(HEADS):
                        pr, hr = hd // 2, hrows(hd)
                        m = mm_(b[hr, CHUNK * pr:CHUNK * pr + qn], S[hr, pr, :], rT[hr, pr, CHUNK * c:CHUNK * c + qn],
                                start=True, stop=True)
                    m.then_inc(*rp.step(f"y_{c}_{t}"))
                    if c in live:
                        pe.wait_ge(*ra.at(f"m_{t}", c % 4))
                        b = R(f"s_{c}_{t}")
                        for hd in range(HEADS):
                            pr, hr = hd // 2, hrows(hd)
                            m = mm_(b[hr, HD * pr:HD * pr + HD], M[c % 4][hr, pr, :], S[hr, pr, :], start=True,
                                    stop=True)
                        m.then_inc(*rp.step(f"s_{c}_{t}"))
            for c in range(C8):
                pe.wait_ge(*rv.at(f"y_{NCH - 1}_{NT - 1}"))
                b = R("mean", c)
                mm_(b[:, 0:T], headones[:, :], yT[:, c, :], start=True, stop=True).then_inc(*rp.step("mean", c))
            for c in range(C8):
                pe.wait_ge(*ra.at("ysq", c))
                b = R("var", c)
                mm_(b[:, 0:T], headones[:, :], A[0][:, c, :], start=True, stop=True).then_inc(*rp.step("var", c))
            pe.wait_ge(*rv.at("yo"))
            for q in range(4):
                s = need(f"o{q}")
                for t, (r0, n) in enumerate(TILES):
                    b = R("o", 3 * q + t)
                    for c in range(C8):
                        m = mm_(b[0:n, 0:256], yT[:, c, r0:r0 + n], slot3(s)[:, c, :], start=(c == 0),
                                stop=(c == C8 - 1))
                    m.then_inc(*rp.step("o", 3 * q + t))

            def moe(l, prev_dve):
                st, ev = moe_pe[l], m_evac(l)
                pe.wait_ge(*prev_dve.end())
                for k in range(KC):
                    b = start(st, ev, "hT", k)
                    for t, (r0, n) in enumerate(TILES):
                        hv = h[0:n, t, :].rearrange("p (m k) -> p k m", k=KC)
                        m = nc.tensor.transpose(b[:, r0:r0 + n], hv[:, k, :], ident[0:n, 0:n])
                    m.then_inc(*st.step("hT", k))
                pe.wait_ge(*moe_dve[l].at("hT"))
                for t, (r0, n) in enumerate(TILES):
                    b = start(st, ev, "lg", t)
                    for k in range(KC):
                        m = mm_(b[0:n, 0:E], mhT[:, k, r0:r0 + n], router[:, l, k, :], start=(k == 0),
                                stop=(k == KC - 1))
                    m.then_inc(*st.step("lg", t))
                for u in range(4):
                    s = need(f"sh{u // 2}_{l}")
                    b = start(st, ev, "sg", u)
                    for k in range(KC):
                        w = ring[:, s, FF * k:FF * k + FF].rearrange("p (m j) -> p j m", j=2)
                        m = mm_(b[:, 0:T], w[:, u % 2, :], mhT[:, k, :], start=(k == 0), stop=(k == KC - 1))
                    m.then_inc(*st.step("sg", u))
                pe.wait_ge(*moe_dve[l].at("sel"))
                for t in range(NT + 1):
                    b = start(st, ev, "pos", t)
                    for t2 in range(min(t + 1, NT)):
                        m = mm_(b[:, 0:E], (before if t2 == t else allones)[:, :], sel[:, t2, :],
                                start=(t2 == 0), stop=(t2 == min(t, NT - 1)))
                    m.then_inc(*st.step("pos", t))
                s = need(f"sh2_{l}")
                pe.wait_ge(*moe_dve[l].at("sm"))
                for u in range(6):
                    r0, n = TILES[u // 2]
                    b = start(st, ev, "sd", u)
                    for j in range(2):
                        m = mm_(b[0:n, :], shm[:, j, r0:r0 + n], ring[:, s, D * j + 512 * (u % 2):][:, 0:512],
                                start=(j == 0), stop=(j == 1))
                    m.then_inc(*st.step("sd", u))
                pe.wait_ge(*moe_dve[l].end())
                pe.wait_ge(*moe_act[l].end())
                set_main(l)
                pe_experts(pe, main, l)
                pe_spill(pe, l)
                pe.wait_ge(few_loaded, 16 * (l + 1))
                for half in range(2):
                    mm_(ps[0:META, 6 + half, :], few_sum, few[:, 512 * half:512 * half + 512], start=True,
                        stop=True).then_inc(*end_pe[l].step("few", half))

            moe(0, rv)

            pe.wait_ge(*end_dve[0].end())

            def G(name, u=0):
                return start(ap, a_evac, name, u)

            for k in range(KC):
                b = G("hT", k)
                for t, (r0, n) in enumerate(TILES):
                    hv = h[0:n, t, :].rearrange("p (m k) -> p k m", k=KC)
                    m = nc.tensor.transpose(b[:, r0:r0 + n], hv[:, k, :], ident[0:n, 0:n])
                m.then_inc(*ap.step("hT", k))
            pe.wait_ge(*av.at("hT"))
            for c in range(8):
                s = need(f"qkv{c // 2}")
                b = G("q", c)
                for k in range(KC):
                    m = mm_(b[:, 0:T], slot3(s)[:, k, P * (c % 2):P * (c % 2) + P], ahT[:, k, :], start=(k == 0),
                            stop=(k == KC - 1))
                m.then_inc(*ap.step("q", c))
            for g in range(KV):
                s = need("qkv4")
                b = G("k", g)
                for r in range(2):
                    for k in range(KC):
                        m = mm_(b[HD * r:HD * r + HD, 0:T], slot3(s)[:, k, HD * g:HD * g + HD], ahT[:, k, :],
                                start=(k == 0), stop=(k == KC - 1))
                m.then_inc(*ap.step("k", g))
            for c in range(2):
                s = need("qkv5")
                b = G("v", c)
                for k in range(KC):
                    m = mm_(b[:, 0:T], slot3(s)[:, k, P * c:P * c + P], ahT[:, k, :], start=(k == 0),
                            stop=(k == KC - 1))
                m.then_inc(*ap.step("v", c))
            pe.wait_ge(*aa.at("v"))
            for t, (r0, n) in enumerate(TILES):
                b = G("vt", t)
                for c in range(2):
                    m = nc.tensor.transpose(b[0:n, P * c:P * c + P], vcT[:, c, r0:r0 + n], ident[:, :])
                m.then_inc(*ap.step("vt", t))
            pe.wait_ge(bias_loaded, 16 * 6)
            pe.wait_ge(*av.at("vt"))
            def scores(t, g):
                r0, n = TILES[t]
                nk = NK[t]
                for i, hd in enumerate(heads_of(g)):
                    b = G(f"sc{t}_{g}", i)
                    mm_(b[0:n, 0:nk], qT[hrows(hd), hd // 2, r0:r0 + n], kdT[hrows(hd), g, 0:nk], start=True,
                        stop=False)
                    mm_(b[0:n, 0:nk], anti[0:n, P - n:P], hank[t][0:n, hd, 0:nk], start=False,
                        stop=True).then_inc(*ap.step(f"sc{t}_{g}", i))

            scores(*BATCHES[0])
            for k, (t, g) in enumerate(BATCHES):
                r0, n = TILES[t]
                if k + 1 < len(BATCHES):
                    scores(*BATCHES[k + 1])
                pe.wait_ge(*aa.at(f"ex{t}_{g}", 3))
                for j in range(t + 1):
                    kj = TILES[j][1]
                    b = G(f"pt{t}_{g}", j)
                    for i in range(4):
                        m = nc.tensor.transpose(b[0:kj, n * i:n * i + n], prob[k % 2][0:n, i, P * j:P * j + kj],
                                                ident[0:n, 0:n])
                    m.then_inc(*ap.step(f"pt{t}_{g}", j))
                pe.wait_ge(*av.at(f"pt{t}_{g}"))
                b = G(f"pv{t}_{g}")
                for i in range(4):
                    for j in range(t + 1):
                        kj = TILES[j][1]
                        m = mm_(b[0:n, HD * i:HD * i + HD], probT[0:kj, j, i, 0:n],
                                vtok[0:kj, j, HD * g:HD * g + HD], start=(j == 0), stop=(j == t))
                m.then_inc(*ap.step(f"pv{t}_{g}"))
            pe.wait_ge(*av.at(f"pv{NT - 1}_{KV - 1}"))
            for c in range(8):
                b = G("oT", c)
                for t, (r0, n) in enumerate(TILES):
                    m = nc.tensor.transpose(b[:, r0:r0 + n], otok[0:n, t, P * c:P * c + P], ident[0:n, 0:n])
                m.then_inc(*ap.step("oT", c))
            pe.wait_ge(*aa.at("oT"))
            for q in range(4):
                s = need(f"ao{q}")
                for t, (r0, n) in enumerate(TILES):
                    b = G("o", 3 * q + t)
                    for c in range(C8):
                        m = mm_(b[0:n, 0:256], oT[:, c, r0:r0 + n], slot3(s)[:, c, :], start=(c == 0),
                                stop=(c == C8 - 1))
                    m.then_inc(*ap.step("o", 3 * q + t))
            moe(1, av)

        @block.scalar
        def _(act):
            A_ = nc.scalar.activation

            def got(name, u=0, st=rp):
                act.wait_ge(*st.at(name, u))
                return psum_of(st, name, u)

            vecs = (I["rwkv_w0"][0], I["rwkv_a0"][0], I["rwkv_k_k"][0], I["rwkv_k_a"][0],
                    I["rwkv_r_k"][0].rearrange("h n -> (h n)"), I["rwkv_lnx_g"][0], I["rwkv_lnx_b"][0])
            for i, v in enumerate(vecs):
                act.dma_start(prow[8 * i:8 * i + 8, :], v.rearrange("(c p) -> c p", p=P)).then_inc(params_loaded, 16)
            act.dma_start(mu, I["rwkv_mu"][0].rearrange("m (p k) -> p m k", k=KC)).then_inc(params_loaded, 16)
            act.dma_start(onehot, I["t5"]).then_inc(params_loaded, 16)
            act.dma_start(relt[0:BUCKETS, :], I["rel_bias"]).then_inc(params_loaded, 16)
            for l in range(2):
                act.dma_start(router[:, l], I["moe_router"][l].rearrange("(p k) n -> p k n", k=KC))\
                    .then_inc(params_loaded, 16)
                act.dma_start(rbias[:, l, :], row(I["moe_bias"][l])).then_inc(params_loaded, 16)
            act.wait_ge(*rv.at("omk"))
            act.wait_ge(*consts.at("ones"))
            for nm, dst in (("r", rT), ("k", kT), ("v", vT)):
                for c in range(C8):
                    nc.scalar.copy(dst[:, c, :], got(nm, c)[:, 0:T]).then_inc(*ra.step(nm, c))
            act.wait_ge(*rp.at("bias"))
            A_(thid, got("wh")[0:LORA, 0:T], ACT.Tanh).then_inc(*ra.step("wh"))
            for c in range(C8):
                A_(wT[:, c, :], got("w", c)[:, 0:T], ACT.Sigmoid, bias=param(PW0, c)).then_inc(*ra.step("w", c))
            nc.scalar.copy(ahid, got("ah")[0:LORA, 0:T]).then_inc(*ra.step("ah"))
            for c in range(C8):
                A_(aT[:, c, :], got("a", c)[:, 0:T], ACT.Sigmoid, bias=param(PA0, c)).then_inc(*ra.step("a", c))
            A_(ghid[:, 0, :], got("gh", 0)[:, 0:T], ACT.Sigmoid).then_inc(*ra.step("gh", 0))
            A_(ghid[0:GLORA - P, 1, :], got("gh", 1)[0:GLORA - P, 0:T], ACT.Sigmoid).then_inc(*ra.step("gh", 1))
            act.wait_ge(*rv.at("mix5"))
            act.wait_ge(*ra.at("k"))
            for c in range(C8):
                nc.scalar.activation(kkn[:, c, :], kT[:, c, :], ACT.Copy, scale=param(PKK, c))\
                    .then_inc(*ra.step("kk0", c))
            for c in range(C8):
                act.wait_ge(*ra.at("kk0", c))
                A_(tmpN(c), kkn[:, c, :], ACT.Square).then_inc(*ra.step("sq", c))
            for c in range(C8):
                nc.scalar.copy(gT[:, c, :], got("g", c)[:, 0:T]).then_inc(*ra.step("g", c))
            for c in range(C8):
                A_(tmpN(c), got("n2", c)[:, 0:T], ACT.Sqrt).then_inc(*ra.step("n2", c))
            for c in range(C8):
                act.wait_ge(*rv.at("cumx", c))
                A_(PMX[:, c, :], PMX[:, c, :], ACT.Exp, scale=-EXP_HALF).then_inc(*ra.step("pm", c))
            for c in range(C8):
                A_(PIN[:, c, :], cum[:, c, :], ACT.Exp, scale=EXP_HALF).then_inc(*ra.step("pi", c))
            act.wait_ge(*rv.at("kk"))
            for c in range(C8):
                A_(PEX[:, c, :], cum[:, c, :], ACT.Exp, scale=-EXP_HALF).then_inc(*ra.step("pp", c))
            act.wait_ge(*ra.at("pp"))
            for c in range(C8):
                A_(A[0][:, c, :], aT[:, c, :], ACT.Identity, scale=param(PKA, c), bias=omk[:, c:c + 1])\
                    .then_inc(*ra.step("k2t", c))
            for t, (r0, n) in enumerate(TILES):
                cols = slice(r0, r0 + n)
                if t == 0:
                    act.wait_ge(*rv.at("s0"))
                for j, dst in enumerate((tokB, tokK, tokV, tokZ)):
                    for half in range(2):
                        u = 2 * j + half
                        b = got(f"tr{t}", u)
                        nc.scalar.copy(dst[0:n, 4 * half:4 * half + 4, :],
                                       b[0:n, :].rearrange("p (i m) -> p i m", i=4)).then_inc(*ra.step(f"tr{t}", u))
                for pair in range(UNITS // 2):
                    both = (2 * pair, 2 * pair + 1)

                    def cp(name, dst, after=None):
                        for g in both:
                            nm = f"{name}_{g}_{t}"
                            b = got(nm)
                            if after:
                                act.wait_ge(*rp.at(f"{after}_{g}_{t}"))
                            nc.scalar.copy(dst[g % 2][0:n, :, 0:n],
                                           b[0:n, :].rearrange("p (i m) -> p i m", i=4)[:, :, 0:n])\
                                .then_inc(*ra.step(nm))
                    cp("x2", X2)
                    cp("x2t", X2T)
                    cp("x4", X, "x2t")
                    cp("x4t", XT)
                    cp("x8", X2, "x4t")
                    if not one_block(t):
                        cp("td", X, "x8")
                        cp("f", X2T)
                    for g in both:
                        nm = f"g1_{g}_{t}"
                        b = got(nm)
                        nc.scalar.copy(GZ[g % 2][0:n], b[0:n, 0:4 * HD].rearrange("p (i m) -> p i m", i=4))\
                            .then_inc(*ra.step(nm))
                    for g in both:
                        nm = f"w12_{g}_{t}"
                        b = got(nm)
                        nc.scalar.copy(unit(W12, g, slice(0, n)), b[0:n, :].rearrange("p (i m) -> p i m", i=4))\
                            .then_inc(*ra.step(nm))
                    for g in both:
                        nm = f"q2_{g}_{t}"
                        b = got(nm)
                        hr, prs = hrows(g), slice(4 * (g // 2), 4 * (g // 2) + 4)
                        nc.scalar.copy(bT[hr, prs, cols], b[hr, :].rearrange("p (i m) -> p i m", i=4)[:, :, 0:n])\
                            .then_inc(*ra.step(nm))
                for j in range(len(carried(t))):
                    nc.scalar.copy(M[j], got(f"m_{t}", j).rearrange("p (c m) -> p c m", c=PAIRS))\
                        .then_inc(*ra.step(f"m_{t}", j))
            for c in range(C8):
                act.wait_ge(*rv.at("ym", c))
                A_(A[0][:, c, :], yT[:, c, :], ACT.Square, scale=HD ** -0.5).then_inc(*ra.step("ysq", c))
            for c in range(C8):
                A_(A[0][:, c, :], got("var", c)[:, 0:T], ACT.Sqrt, bias=eps[:, 1:2]).then_inc(*ra.step("std", c))

            def ln(sa, sv):
                act.wait_ge(*sv.at("ln", 2))
                A_(std, mv[:, :, 1], ACT.Sqrt, bias=eps[:, 0:1]).then_inc(*sa.step("ln"))

            ln(ra, rv)

            def moe(l, prev_dve):
                sa = moe_act[l]
                act.wait_ge(*prev_dve.end())
                act.wait_ge(*moe_dve[l].at("zero"))
                for t, (r0, n) in enumerate(TILES):
                    b = got("lg", t, moe_pe[l])
                    A_(score[0:n, t, :], b[0:n, 0:E], ACT.Sigmoid).then_inc(*sa.step("sc", t))
                for j in range(2):
                    b = got("sg", j, moe_pe[l])
                    A_(shid[:, j, :], b[:, 0:T], ACT.Silu).then_inc(*sa.step("sg", j))
                act.wait_ge(*moe_dve[l].end())
                set_main(l)
                act_experts(act, main)
                act_spill(act, l)
                ln(end_act[l], end_dve[l])

            moe(0, rv)
            act.wait_ge(*end_dve[0].end())
            act.wait_ge(bias_stored, 16)
            for t, (r0, n) in enumerate(TILES):
                off = T - (r0 + n)
                nk = NK[t]
                act.dma_start(hank[t][0:n, :, META:nk],
                              bass.AP(biasd.tensor, off + META, [[1, n], [2 * BIASLEN, HEADS], [1, nk - META]]))\
                    .then_inc(bias_loaded, 16)
                act.dma_start(hank[t][0:n, :, 0:META],
                              bass.AP(biasd.tensor, BIASLEN + off, [[1, n], [2 * BIASLEN, HEADS], [1, META]]))\
                    .then_inc(bias_loaded, 16)
            act.wait_ge(attn_loaded, 16 * 6)
            act.wait_ge(*av.at("sink"))
            for c in range(8):
                A_(qT[:, c, :], got("q", c, ap)[:, 0:T], ACT.Identity, bias=bq8[:, c:c + 1], scale=0.125)\
                    .then_inc(*aa.step("q", c))
            for g in range(KV):
                A_(kdT[:, g, :], got("k", g, ap)[:, 0:T], ACT.Identity, bias=bqkv[:, 8 + g:9 + g])\
                    .then_inc(*aa.step("k", g))
            for c in range(2):
                A_(vcT[:, c, :], got("v", c, ap)[:, 0:T], ACT.Identity, bias=bqkv[:, 12 + c:13 + c])\
                    .then_inc(*aa.step("v", c))
            for k, (t, g) in enumerate(BATCHES):
                r0, n = TILES[t]
                nk = NK[t]
                act.wait_ge(*av.at(f"mx{t}_{g}", 3))
                if k >= 2:
                    pt, pg = BATCHES[k - 2]
                    act.wait_ge(*ap.at(f"pt{pt}_{pg}"))
                for i in range(4):
                    A_(prob[k % 2][0:n, i, 0:nk], psum_of(ap, f"sc{t}_{g}", i)[0:n, 0:nk], ACT.Exp,
                       bias=negm[k % 2][0:n, i:i + 1], accum_out=dens[k % 2][0:n, i:i + 1]).then_inc(*aa.step(f"ex{t}_{g}", i))
                A_(esink[k % 2][0:n, :], esin[k % 2][0:n, :], ACT.Exp).then_inc(*aa.step(f"ex{t}_{g}", 4))
            for c in range(8):
                nc.scalar.copy(oT[:, c, :], got("oT", c, ap)[:, 0:T]).then_inc(*aa.step("oT", c))
            ln(aa, av)
            moe(1, av)

        @block.vector
        def _(dve):
            V = nc.vector

            def got(name, u=0, st=rp):
                dve.wait_ge(*st.at(name, u))
                return psum_of(st, name, u)

            V.memset(relt_hidden, HIDDEN).then_inc(hidden_row, 1)
            V.tensor_copy(par, got("par")[:, 0:56]).then_inc(*rv.step("par"))
            dve.wait_ge(*rv.at("par"))
            V.tensor_scalar(omk, par[:, 8 * PKA:8 * PKA + 8], -1.0, 1.0, ALU.mult, ALU.add).then_inc(*rv.step("omk"))
            for k in range(KC):
                V.tensor_copy(hT[:, k, :], got("xT", k)[:, 0:T]).then_inc(*rv.step("xT", k))
            for j in range(4):
                V.tensor_copy(brow[:, j // 2, T * (j % 2):T * (j % 2) + T], got("bias", j)[0:HEADS, 0:T])\
                    .then_inc(*rv.step("bias", j))
            dve.wait_ge(*rv.at("xT"))
            V.tensor_tensor(xx[:, :, 1:T], hT[:, :, 0:T - 1], hT[:, :, 1:T], ALU.subtract).then_inc(*rv.step("xx", 0))
            V.tensor_scalar(xx[:, :, 0:1], hT[:, :, 0:1], -1.0, None, ALU.mult).then_inc(*rv.step("xx", 1))
            dve.wait_ge(*rv.at("xx"))
            prior = {3: "r", 1: "k", 4: "v", 5: "wh"}
            for m in (0, 2, 3, 1, 4, 5):
                if m in prior:
                    dve.wait_ge(*rp.at(prior[m]))
                for k in range(KC):
                    V.scalar_tensor_tensor(out=xm[MIXBUF[m]][:, k, :], in0=xx[:, k, :], scalar=mu[:, m, k:k + 1],
                                           in1=hT[:, k, :], op0=ALU.mult, op1=ALU.add).then_inc(*rv.step(f"mix{m}", k))
            dve.wait_ge(*rv.at("mix5"))
            for c in range(C8):
                dve.wait_ge(*ra.at("w", c))
                V.tensor_tensor_scan(cum[:, c, :], notfirst[:, :], wT[:, c, :], 0.0, ALU.mult, ALU.add)\
                    .then_inc(*rv.step("cum", c))
            dve.wait_ge(*rp.at("gh"))
            for c in range(C8):
                dve.wait_ge(*rv.at("cum", c))
                V.tensor_tensor(PMX[:, c, :], cum[:, c, :], wT[:, c, :], ALU.subtract).then_inc(*rv.step("cumx", c))
            for c in range(C8):
                dve.wait_ge(*ra.at("n2", c))
                V.tensor_scalar(tmpN(c), tmpN(c), 1e-12, None, ALU.max).then_inc(rn_step, 1)
                dve.wait_ge(rn_step, c + 1)
                V.reciprocal(tmpN(c), tmpN(c)).then_inc(*rv.step("rn", c))
            for c in range(C8):
                dve.wait_ge(*rv.at("rn", c))
                V.tensor_tensor(kkn[:, c, :], kkn[:, c, :], tmpN(c), ALU.mult).then_inc(*rv.step("kk", c))
            for c in range(C8):
                dve.wait_ge(*ra.at("k2t", c))
                V.tensor_tensor(kT[:, c, :], kT[:, c, :], A[0][:, c, :], ALU.mult).then_inc(*rv.step("k2", c))
            for c in range(C8):
                V.tensor_tensor(bT[:, c, :], kkn[:, c, :], aT[:, c, :], ALU.mult).then_inc(*rv.step("b", c))
            for c in range(C8):
                dve.wait_ge(*rv.at("k2", c))
                V.scalar_tensor_tensor(out=A[0][:, c, :], in0=rT[:, c, :], scalar=param(PRK, c), in1=kT[:, c, :],
                                       op0=ALU.mult, op1=ALU.mult).then_inc(*rv.step("rk", c))
            for c in range(C8):
                dve.wait_ge(*rv.at("b", c))
                V.scalar_tensor_tensor(out=zT[:, c, :], in0=kkn[:, c, :], scalar=-1.0, in1=PMX[:, c, :],
                                       op0=ALU.mult, op1=ALU.mult).then_inc(*rv.step("z", c))
            for c in range(C8):
                dve.wait_ge(*rv.at("z", c))
                V.tensor_tensor(bonus[:, c, :], got("bon", c)[:, 0:T], vT[:, c, :], ALU.mult)\
                    .then_inc(*rv.step("bonus", c))
            V.tensor_copy(pc[:, :, 0:NCH - 1],
                          PEX[:, :, 0:256].rearrange("p c (n s) -> p c n s", s=CHUNK)[:, :, :, CHUNK - 1])\
                .then_inc(*rv.step("pc", 0))
            V.tensor_copy(pc[:, :, NCH - 1:NCH], PEX[:, :, T - 1:T]).then_inc(*rv.step("pc", 1))
            for c in range(C8):
                V.tensor_tensor(bT[:, c, :], bT[:, c, :], PIN[:, c, :], ALU.mult).then_inc(*rv.step("bh", c))
            dve.wait_ge(*rv.at("rk"))
            for c in range(C8):
                V.tensor_tensor(rT[:, c, :], rT[:, c, :], PEX[:, c, :], ALU.mult).then_inc(*rv.step("rh", c))
            dve.wait_ge(*rv.at("rh"))
            dve.wait_ge(kh_made, KC)
            dve.wait_ge(bias_stored, 16)
            V.memset(S, 0.0).then_inc(*rv.step("s0"))
            dve.wait_ge(*rv.at("s0"))
            for t, (r0, n) in enumerate(TILES):
                cols = slice(r0, r0 + n)
                nch = -(-n // CHUNK)
                cs = min(CHUNK, n)
                if t:
                    dve.wait_ge(*rp.at(f"tr{t - 1}", 3))
                for nm, src, dst in (("bt", bT, btile), ("kt", kT, ktile)):
                    for c in range(C8):
                        m = V.tensor_tensor(dst[:, c, 0:n].rearrange("p (a s) -> p a s", s=cs),
                                            src[:, c, cols].rearrange("p (a s) -> p a s", s=cs),
                                            pc[:, c, 4 * t:4 * t + nch].unsqueeze(2).to_broadcast([P, nch, cs]),
                                            ALU.mult)
                    m.then_inc(*rv.step(f"{nm}{t}"))
                for pair in range(UNITS // 2):
                    both = (2 * pair, 2 * pair + 1)

                    def N(x, g):
                        return f"{x}_{g}_{t}"

                    def b4(name, g):
                        return got(N(name, g))[0:n, :].rearrange("p (i m) -> p i m", i=4)[:, :, 0:n]

                    def bc(mask):
                        return mask[0:n, 0:n].unsqueeze(1).to_broadcast([n, 4, n])

                    def masked_copy(name, step, dst, mask):
                        for g in both:
                            V.tensor_tensor(dst[g % 2][0:n, :, 0:n], b4(name, g), bc(mask), ALU.mult)\
                                .then_inc(*rv.step(N(step, g)))

                    if pair or t:
                        pt = t if pair else t - 1
                        dve.wait_ge(*rp.at(f"q2_{(2 * pair - 1) % UNITS}_{pt}"))
                        if not pair:
                            dve.wait_ge(*rp.at(f"s_{carried(pt)[-1]}_{pt}"))
                    masked_copy("ab", "ab", XT, up16)
                    for g in both:
                        dve.wait_ge(*rv.at(N("ab", g)))
                        V.tensor_tensor(TT[g % 2][0:n, :, 0:n], XT[g % 2][0:n, :, 0:n], bc(ident), ALU.add)\
                            .then_inc(*rv.step(N("tt1", g)))
                    masked_copy("ba", "ba", X, low16)
                    if not one_block(t):
                        masked_copy("ba", "off", OFF, lowoff)
                    masked_copy("ak", "ak", AK, up32)
                    masked_copy("bb", "bb", BB, up32d)
                    masked_copy("bk", "bk", BK, up32d)
                    for j in range(2, 5 if one_block(t) else 6):
                        for g in both:
                            nm = N(f"tt{j}", g)
                            V.tensor_tensor(TT[g % 2][0:n, :, 0:n], TT[g % 2][0:n, :, 0:n], b4(f"tt{j}", g), ALU.add)\
                                .then_inc(*rv.step(nm))
                    for g in both:
                        b = got(N("q1", g))
                        hr, prs = hrows(g), slice(4 * (g // 2), 4 * (g // 2) + 4)
                        V.tensor_tensor(rT[hr, prs, cols], rT[hr, prs, cols],
                                        b[hr, :].rearrange("p (i m) -> p i m", i=4)[:, :, 0:n], ALU.add)\
                            .then_inc(*rv.step(N("q1", g)))
                live = carried(t)
                for j in range(len(live)):
                    V.tensor_copy(KVS[j], got(f"kv_{t}", j).rearrange("p (c m) -> p c m", c=PAIRS))\
                        .then_inc(*rv.step(f"kv_{t}", j))
                for c in chunk_ids(t):
                    qn = min(CHUNK, T - CHUNK * c)
                    cc = slice(CHUNK * c, CHUNK * c + qn)
                    if c in live:
                        if c:
                            dve.wait_ge(*rv.at(f"s_{c - 1}_{(c - 1) // 4}"))
                        V.tensor_tensor(SP, S, pc[:, :, c:c + 1].to_broadcast([P, KC, HD]), ALU.mult)\
                            .then_inc(*rv.step(f"sp_{c}_{t}", 0))
                        dve.wait_ge(*rv.at(f"sp_{c}_{t}", 0))
                        V.tensor_tensor(SP, SP, KVS[c % 4], ALU.add).then_inc(*rv.step(f"sp_{c}_{t}", 1))
                    b = got(f"y_{c}_{t}")
                    dve.wait_ge(*ra.at(f"q2_{UNITS - 1}_{t}"))
                    V.tensor_tensor(yT[:, :, cc], bT[:, :, cc],
                                    b[:, 0:CHUNK * PAIRS].rearrange("p (c s) -> p c s", c=PAIRS)[:, :, 0:qn],
                                    ALU.add).then_inc(*rv.step(f"y_{c}_{t}"))
                    if c in live:
                        b = got(f"s_{c}_{t}")
                        dve.wait_ge(*rv.at(f"sp_{c}_{t}"))
                        V.tensor_tensor(S, SP, b.rearrange("p (c m) -> p c m", c=PAIRS), ALU.add)\
                            .then_inc(*rv.step(f"s_{c}_{t}"))
            dve.wait_ge(*rv.at(f"y_{NCH - 1}_{NT - 1}"))
            dve.wait_ge(*rp.at("mean"))
            for c in range(C8):
                V.scalar_tensor_tensor(out=yT[:, c, :], in0=got("mean", c)[:, 0:T], scalar=-1.0 / HD,
                                       in1=yT[:, c, :], op0=ALU.mult, op1=ALU.add).then_inc(*rv.step("ym", c))
            for c in range(C8):
                dve.wait_ge(*ra.at("std", c))
                V.reciprocal(A[0][:, c, :], A[0][:, c, :]).then_inc(*rv.step("yr", c))
            for c in range(C8):
                dve.wait_ge(*rv.at("yr", c))
                V.tensor_tensor(yT[:, c, :], yT[:, c, :], A[0][:, c, :], ALU.mult).then_inc(*rv.step("yn", c))
            dve.wait_ge(bonus_shifted, KC)
            for c in range(C8):
                dve.wait_ge(*rv.at("yn", c))
                V.scalar_tensor_tensor(out=yT[:, c, :], in0=yT[:, c, :], scalar=param(PLG, c), in1=bonus[:, c, :],
                                       op0=ALU.mult, op1=ALU.add).then_inc(*rv.step("yb", c))
            for c in range(C8):
                dve.wait_ge(*rv.at("yb", c))
                V.tensor_tensor(yT[:, c, :], yT[:, c, :], gT[:, c, :], ALU.mult).then_inc(*rv.step("yo", c))
            dve.wait_ge(*rv.at("yo"))
            dve.wait_ge(h_loaded, 64)

            def residual(steps, st, acc):
                for q in range(4):
                    for t, (r0, n) in enumerate(TILES):
                        b = got("o", 3 * q + t, st)
                        V.scalar_tensor_tensor(out=acc[0:n, t, 256 * q:256 * q + 256],
                                               in0=h[0:n, t, 256 * q:256 * q + 256], scalar=ALPHA,
                                               in1=b[0:n, 0:256], op0=ALU.mult, op1=ALU.add)\
                            .then_inc(*steps.step("res", 3 * q + t))

            def ln(steps, sa, acc, which):
                for t, (r0, n) in enumerate(TILES):
                    for j in range(2):
                        m = V.bn_stats(stat[0:n, t, 6 * j:6 * j + 6], acc[0:n, t, 512 * j:512 * j + 512])
                m.then_inc(*steps.step("ln", 0))
                dve.wait_ge(*steps.at("ln", 0))
                V.memset(mv, 1.0).then_inc(*steps.step("ln", 1))
                dve.wait_ge(*steps.at("ln", 1))
                for t, (r0, n) in enumerate(TILES):
                    m = V.bn_aggr(mv[0:n, t, :], stat[0:n, t, :])
                m.then_inc(*steps.step("ln", 2))
                dve.wait_ge(*steps.at("ln", 2))
                dve.wait_ge(ln_loaded, 32 * which)
                for t, (r0, n) in enumerate(TILES):
                    m = V.scalar_tensor_tensor(out=acc[0:n, t, :], in0=acc[0:n, t, :], scalar=mv[0:n, t, 0:1],
                                               in1=lnrow[0:n, 0, :], op0=ALU.subtract, op1=ALU.mult)
                m.then_inc(*steps.step("ln", 3))
                dve.wait_ge(*sa.at("ln"))
                V.reciprocal(rstd, std).then_inc(*steps.step("ln", 4))
                dve.wait_ge(*steps.at("ln", 4))
                for t, (r0, n) in enumerate(TILES):
                    V.scalar_tensor_tensor(out=h[0:n, t, :], in0=acc[0:n, t, :], scalar=rstd[0:n, t:t + 1],
                                           in1=lnrow[0:n, 1, :], op0=ALU.mult, op1=ALU.add)\
                        .then_inc(*steps.step("ln", 5 + t))
                dve.wait_ge(*steps.at("ln"))

            residual(rv, rp, facc)
            dve.wait_ge(*rv.at("res"))
            ln(rv, ra, facc, 1)

            def moe(l):
                st = moe_dve[l]
                sp_ = moe_pe[l]

                def fin(ins, name, u=0):
                    ins.then_inc(*st.step(name, u))
                    dve.wait_ge(*st.at(name, u))

                V.memset(score, 0.0).then_inc(*st.step("zero", 0))
                V.memset(values, 0.0).then_inc(*st.step("zero", 1))
                for k in range(KC):
                    V.tensor_copy(mhT[:, k, :], got("hT", k, sp_)[:, 0:T]).then_inc(*st.step("hT", k))
                dve.wait_ge(route_consts, l + 1)
                dve.wait_ge(*moe_act[l].at("sc"))
                fin(V.tensor_tensor(choice, score, rbias[:, l, :].unsqueeze(1).to_broadcast([P, NT, E]), ALU.add),
                    "choice")
                for t in range(NT):
                    for g in range(GROUPS):
                        V.max(top2[:, t, 8 * g:8 * g + 8], choice[:, t, GE * g:GE * g + GE])\
                            .then_inc(*st.step("top2", GROUPS * t + g))
                dve.wait_ge(*st.at("top2"))
                t2 = top2.rearrange("p t (g k) -> p t g k", k=8)
                fin(V.tensor_tensor(gsc, t2[:, :, :, 0], t2[:, :, :, 1], ALU.add), "gs")
                for t in range(NT):
                    a = gsc[:, t, :].unsqueeze(1).to_broadcast([P, GROUPS, GROUPS])
                    c = gsc[:, t, :].unsqueeze(2).to_broadcast([P, GROUPS, GROUPS])
                    fin(V.tensor_tensor(cmp1, a, c, ALU.is_gt), "rank", 5 * t)
                    fin(V.tensor_tensor(cmp2, a, c, ALU.is_equal), "rank", 5 * t + 1)
                    fin(V.tensor_tensor(cmp2, cmp2, tie, ALU.mult), "rank", 5 * t + 2)
                    fin(V.tensor_tensor(cmp1, cmp1, cmp2, ALU.add), "rank", 5 * t + 3)
                    fin(V.tensor_reduce(grank[:, t, :], cmp1, AX.X, ALU.add), "rank", 5 * t + 4)
                fin(V.tensor_scalar(keep, grank, TOP_GROUPS - 0.5, None, ALU.is_lt), "keep")
                fin(V.tensor_scalar(grank, keep, -HIDDEN, HIDDEN, ALU.mult, ALU.add), "hide")
                kb = keep.rearrange("p t g -> p (t g)").unsqueeze(2).to_broadcast([P, NT * GROUPS, GE])
                hb = grank.rearrange("p t g -> p (t g)").unsqueeze(2).to_broadcast([P, NT * GROUPS, GE])
                mk = masked.rearrange("p t (g e) -> p (t g) e", e=GE)
                fin(V.tensor_tensor(mk, choice.rearrange("p t (g e) -> p (t g) e", e=GE), kb, ALU.mult), "mask", 0)
                fin(V.tensor_tensor(mk, mk, hb, ALU.add), "mask", 1)
                for t in range(NT):
                    fin(V.max(top8[:, t, :], masked[:, t, :]), "top8", 2 * t)
                    fin(V.match_replace(taken[:, t, :], top8[:, t, :], masked[:, t, :], 2 * HIDDEN), "top8", 2 * t + 1)
                fin(V.tensor_tensor(sel, taken, masked, ALU.not_equal), "sel", 0)
                fin(V.tensor_tensor(sel, sel, rowok.unsqueeze(2).to_broadcast([P, NT, E]), ALU.mult), "sel", 1)
                dve.wait_ge(*moe_act[l].at("sg"))
                for j in range(2):
                    V.tensor_tensor(shm[:, j, :], shid[:, j, :], got("sg", 2 + j, sp_)[:, 0:T], ALU.mult)\
                        .then_inc(*st.step("sm", j))
                fin(V.tensor_tensor(gate, score, sel, ALU.mult), "g0")
                fin(V.tensor_reduce(gsum, gate, AX.X, ALU.add), "gsum")
                fin(V.tensor_scalar(rowbad, rowok, -1.0, 1.0, ALU.mult, ALU.add), "grec", 0)
                fin(V.tensor_tensor(gsum, gsum, rowbad, ALU.add), "grec", 1)
                fin(V.reciprocal(grec, gsum), "g1")
                v3 = values.rearrange("p t (e c) -> p t e c", c=2)
                fin(V.scalar_tensor_tensor(out=v3[:, :, :, 1], in0=gate, scalar=SCALE,
                                           in1=grec.unsqueeze(2).to_broadcast([P, NT, E]), op0=ALU.mult,
                                           op1=ALU.mult), "g2")
                for t in range(NT):
                    fin(V.tensor_tensor_scan(krank[:, t, :], allones[:, 0:E], sel[:, t, :], 0.0, ALU.mult, ALU.add),
                        "kr", t)
                fin(V.tensor_tensor(krank, krank, sel, ALU.subtract), "kr2")
                for t in range(NT):
                    fin(V.tensor_scalar(dest8[:, t:t + 1], tokid[:, t:t + 1], float(TOPK), -OUT_OF_RANGE,
                                        ALU.mult, ALU.add), "dest", t)
                for t in range(NT):
                    V.tensor_scalar(v3[:, t, :, 0], krank[:, t, :], dest8[:, t:t + 1], None, ALU.add)\
                        .then_inc(*st.step("tok", t))
                dve.wait_ge(*st.at("tok"))
                for t in range(NT):
                    b = got("pos", t, sp_)
                    V.scalar_tensor_tensor(out=posm[:, t, :], in0=b[:, 0:E], scalar=1.0, in1=sel[:, t, :],
                                           op0=ALU.add, op1=ALU.mult).then_inc(*st.step("pos", t))
                dve.wait_ge(*st.at("pos"))
                fin(V.tensor_scalar(posm, posm, -1.0, None, ALU.add), "pos2")
                fin(V.tensor_reduce(most, got("pos", 3, sp_)[:, 0:E], AX.X, ALU.max), "max")
                fin(V.tensor_copy(mosti_of[l], most), "maxi")
                for u in range(6):
                    r0, n = TILES[u // 2]
                    cs = slice(512 * (u % 2), 512 * (u % 2) + 512)
                    V.scalar_tensor_tensor(out=macc[0:n, u // 2, cs], in0=h[0:n, u // 2, cs], scalar=ALPHA,
                                           in1=got("sd", u, sp_)[0:n, :], op0=ALU.mult, op1=ALU.add)\
                        .then_inc(*st.step("sd", u))
                dve.wait_ge(*st.at("sd"))
                set_main(l)
                dve_experts(dve, main)
                dve_spill(dve, l)
                es = end_dve[l]
                for half in range(2):
                    dve.wait_ge(*end_pe[l].at("few", half))
                    cs = slice(512 * half, 512 * half + 512)
                    V.tensor_tensor(macc[0:META, NT - 1, cs], macc[0:META, NT - 1, cs], ps[0:META, 6 + half, :],
                                    ALU.add).then_inc(*es.step("few", half))
                dve.wait_ge(*es.at("few"))
                for t in range(NT - 1):
                    for k in range(TOPK):
                        dve.wait_ge(routed_loaded[t][k // 2], 16 * (l + 1))
                        V.tensor_tensor(macc[:, t, :], macc[:, t, :], rt[t][:, k, :], ALU.add)\
                            .then_inc(*es.step("sum", TOPK * t + k))
                        dve.wait_ge(*es.at("sum", TOPK * t + k))
                ln(es, end_act[l], macc, 2 + 2 * l)

            moe(0)

            dve.wait_ge(attn_loaded, 16 * 6)
            V.tensor_scalar(bq8, bqkv[:, 0:8], 0.125, None, ALU.mult).then_inc(*av.step("sink"))
            for k in range(KC):
                V.tensor_copy(ahT[:, k, :], got("hT", k, ap)[:, 0:T]).then_inc(*av.step("hT", k))
            for t, (r0, n) in enumerate(TILES):
                V.tensor_copy(vtok[0:n, t, :], got("vt", t, ap)[0:n, 0:256]).then_inc(*av.step("vt", t))
            def maxima(k):
                t, g = BATCHES[k]
                n, nk = TILES[t][1], NK[t]
                nm, ng, es_ = f"mx{t}_{g}", negm[k % 2], esin[k % 2]
                if k >= 2:
                    pt, pg = BATCHES[k - 2]
                    dve.wait_ge(*aa.at(f"ex{pt}_{pg}"))
                for i in range(4):
                    b = got(f"sc{t}_{g}", i, ap)
                    m = V.tensor_reduce(ng[0:n, i:i + 1], b[0:n, 0:nk], AX.X, ALU.max)
                m.then_inc(*av.step(nm, 0))
                dve.wait_ge(*av.at(nm, 0))
                V.tensor_tensor(ng[0:n, :], ng[0:n, :], sinks[0:n, 4 * g:4 * g + 4], ALU.max)\
                    .then_inc(*av.step(nm, 1))
                dve.wait_ge(*av.at(nm, 1))
                V.tensor_tensor(es_[0:n, :], sinks[0:n, 4 * g:4 * g + 4], ng[0:n, :], ALU.subtract)\
                    .then_inc(*av.step(nm, 2))
                dve.wait_ge(*av.at(nm, 2))
                V.tensor_scalar(ng[0:n, :], ng[0:n, :], -1.0, None, ALU.mult).then_inc(*av.step(nm, 3))

            maxima(0)
            for k, (t, g) in enumerate(BATCHES):
                n = TILES[t][1]
                d, d2, ek = dens[k % 2], dens2[k % 2], esink[k % 2]
                if k + 1 < len(BATCHES):
                    maxima(k + 1)
                dn = f"den{t}_{g}"
                dve.wait_ge(*aa.at(f"ex{t}_{g}", 4))
                V.tensor_tensor(d2[0:n, :], d[0:n, :], ek[0:n, :], ALU.add).then_inc(*av.step(dn, 0))
                dve.wait_ge(*av.at(dn, 0))
                V.reciprocal(d2[0:n, :], d2[0:n, :]).then_inc(*av.step(dn, 1))
                if k:
                    pt, pg = BATCHES[k - 1]
                    dve.wait_ge(*ap.at(f"pv{pt}_{pg}"))
                for j in range(t + 1):
                    kj = TILES[j][1]
                    b = got(f"pt{t}_{g}", j, ap)
                    V.tensor_copy(probT[0:kj, j, :, 0:n], b[0:kj, 0:4 * n].rearrange("p (i m) -> p i m", i=4))\
                        .then_inc(*av.step(f"pt{t}_{g}", j))
                b = got(f"pv{t}_{g}", 0, ap)
                dve.wait_ge(*av.at(dn, 1))
                for i in range(4):
                    V.tensor_scalar(otok[0:n, t, HD * (4 * g + i):HD * (4 * g + i) + HD],
                                    b[0:n, HD * i:HD * i + HD], d2[0:n, i:i + 1], None, ALU.mult)\
                        .then_inc(*av.step(f"pv{t}_{g}", i))
            residual(av, ap, aacc)
            dve.wait_ge(*av.at("res"))
            for t, (r0, n) in enumerate(TILES):
                V.tensor_tensor(aacc[0:n, t, :], aacc[0:n, t, :], borow[0:n, :], ALU.add).then_inc(*av.step("bo", t))
            dve.wait_ge(*av.at("bo"))
            ln(av, aa, aacc, 3)
            moe(1)


_INS = ['x', 'meta', 'rel_bias', 'rwkv_mu', 'rwkv_w0', 'rwkv_w1', 'rwkv_w2', 'rwkv_a0', 'rwkv_a1', 'rwkv_a2',
        'rwkv_g1', 'rwkv_g2', 'rwkv_k_k', 'rwkv_k_a', 'rwkv_r_k', 'rwkv_w_r', 'rwkv_w_k', 'rwkv_w_v', 'rwkv_w_o',
        'rwkv_lnx_g', 'rwkv_lnx_b', 'attn_w_qkv', 'attn_b_qkv', 'attn_sinks', 'attn_w_o', 'attn_b_o', 'ln_mix_g',
        'ln_mix_b', 'ln_ffn_g', 'ln_ffn_b', 'moe_router', 'moe_bias', 'moe_w_gate', 'moe_w_up', 'moe_w_down',
        'shared_w_gate', 'shared_w_up', 'shared_w_down']


def kernel(**inputs):
    import numpy as _np
    import concourse.bacc as _bacc
    from concourse import mybir as _mybir
    from concourse.bass_utils import run_bass_kernel_spmd as _run

    nc = _bacc.Bacc("TRN2", target_bir_lowering=False, num_devices=1)
    arrays, aps = {}, {}
    for name in _INS:
        arrays[f"in_{name}"] = _np.ascontiguousarray(inputs[name])
    arrays["in_t5"] = t5_one_hot()
    for name, a in arrays.items():
        aps[name[3:]] = nc.dram_tensor(name, a.shape, _mybir.dt.from_np(a.dtype), kind="ExternalInput").ap()
    out = nc.dram_tensor("out_0", (1, SEQ, D), _mybir.dt.float32, kind="ExternalOutput").ap()
    hybrid_trunk(nc, aps, out)
    r = _run(nc, [arrays], core_ids=[0])
    return r.results[0]["out_0"]
```
